# Optimizing a Trainium2 kernel written in Bass

```python
import math
import jax, jax.numpy as jnp
from jax import lax
import numpy as np

D_MODEL = 1024
BATCH = 1
SEQ = 512
DEPTH = 2
DEC_BATCH = 8
DEC_SEQ = 1
PAST_LEN = 2048
PAGE_SIZE = 128

N_EVEN = (DEPTH + 1) // 2
N_ODD = DEPTH // 2
HG_HEADS = 4
HG_DK = 128
HG_DV = 128
HG_CHUNK = 64
MLA_HEADS = 4
Q_LORA = 384
KV_LORA = 256
NOPE_DIM = 128
ROPE_DIM = 64
V_DIM = 128
ROPE_THETA = 10000.0
MLA_SCALE = (NOPE_DIM + ROPE_DIM) ** -0.5
Q_BLOCK = 128
CONV_DIM = D_MODEL
CONV_WIDTH = 31
PEER_HEADS = 8
N_KEYS = 128
N_EXPERTS = N_KEYS * N_KEYS
PEER_DK = 256
PEER_HALF = PEER_DK // 2
PEER_TOPK = 16
PEER_BLOCK = 256
DN_ALPHA = (2 * DEPTH) ** 0.25
DN_BETA = (8 * DEPTH) ** -0.25
LN_EPS = 1e-5
RMS_EPS = 1e-6
HG_QK_W = HG_HEADS * HG_DK
HG_V_W = HG_HEADS * HG_DV
MIX_IN_SIZES = (HG_QK_W, HG_QK_W, HG_V_W, HG_V_W, Q_LORA, KV_LORA, ROPE_DIM)
MIX_IN = sum(MIX_IN_SIZES)
SPLIT_POINTS = [int(v) for v in np.cumsum(MIX_IN_SIZES)[:-1]]
MIX_OUT = HG_V_W + MLA_HEADS * V_DIM

kernel_name = 'hybrid_hgrn2_mla_conformer_peer_step'

def layer_norm(x, g, b):
    xf = x.astype(jnp.float32)
    mu = jnp.mean(xf, axis=-1, keepdims=True)
    var = jnp.mean(jnp.square(xf - mu), axis=-1, keepdims=True)
    y = (xf - mu) * lax.rsqrt(var + LN_EPS) * g.astype(jnp.float32) + b.astype(jnp.float32)
    return y.astype(x.dtype)

def rms_norm(x, g):
    xf = x.astype(jnp.float32)
    y = xf * lax.rsqrt(jnp.mean(xf * xf, axis=-1, keepdims=True) + RMS_EPS) * g.astype(jnp.float32)
    return y.astype(x.dtype)

def rope(x, pos):
    half = ROPE_DIM // 2
    inv_freq = ROPE_THETA ** (-jnp.arange(half, dtype=jnp.float32) / half)
    ang = pos.astype(jnp.float32)[:, None] * inv_freq[None, :]
    cos = jnp.cos(ang)[:, None, :]
    sin = jnp.sin(ang)[:, None, :]
    xf = x.astype(jnp.float32)
    x1, x2 = xf[..., :half], xf[..., half:]
    return jnp.concatenate([x1 * cos - x2 * sin, x1 * sin + x2 * cos], axis=-1).astype(x.dtype)

def hgrn2_recurrence(q, k, v, log_f, s0):
    B, L, H, _ = q.shape
    DV = v.shape[-1]
    C = min(HG_CHUNK, L)
    n = -(-L // C)
    pad = n * C - L

    def blocks(t):
        t = jnp.pad(t, ((0, 0), (0, pad), (0, 0), (0, 0)))
        return t.reshape(B, n, C, H, t.shape[-1]).transpose(1, 0, 3, 2, 4)

    tri = jnp.tril(jnp.ones((C, C), dtype=bool))

    def step(S, inp):
        qc, kc, vc, gc = inp
        b = jnp.cumsum(gc, axis=2)
        o_inter = jnp.einsum('bhtk,bhkv->bhtv', qc * jnp.exp(b), S)
        diff = b[:, :, :, None, :] - b[:, :, None, :, :]
        decay = jnp.exp(jnp.where(tri[:, :, None], diff, -jnp.inf))
        attn = jnp.einsum('bhtk,bhtsk,bhsk->bhts', qc, decay, kc)
        o_intra = jnp.einsum('bhts,bhsv->bhtv', attn, vc)
        b_last = b[:, :, -1:, :]
        S_new = jnp.exp(b_last[:, :, 0, :, None]) * S + jnp.einsum('bhsk,bhsv->bhkv', kc * jnp.exp(b_last - b), vc)
        return S_new, o_inter + o_intra

    S_fin, o = lax.scan(step, s0, (blocks(q), blocks(k), blocks(v), blocks(log_f)))
    o = o.transpose(1, 0, 3, 2, 4).reshape(B, n * C, H, DV)[:, :L]
    return o, S_fin

def latent_scores(q_abs, q_pe, c_kv, k_pe):
    s = jnp.einsum('bqhc,bkc->bhqk', q_abs, c_kv) + jnp.einsum('bqhr,bkr->bhqk', q_pe, k_pe)
    return s.astype(jnp.float32) * MLA_SCALE

def mla_prompt_attention(q_abs, q_pe, c_kv, k_pe):
    B, L, H, _ = q_abs.shape
    blk = Q_BLOCK if L % Q_BLOCK == 0 else L
    nb = L // blk
    k_idx = jnp.arange(L)

    def split(t):
        return t.reshape(B, nb, blk, H, t.shape[-1]).transpose(1, 0, 2, 3, 4)

    def block(args):
        qa, qp, q0 = args
        s = latent_scores(qa, qp, c_kv, k_pe)
        q_idx = q0 + jnp.arange(blk)
        s = jnp.where(k_idx[None, :] <= q_idx[:, None], s, -jnp.inf)
        p = jax.nn.softmax(s, axis=-1).astype(c_kv.dtype)
        return jnp.einsum('bhqk,bkc->bqhc', p, c_kv)

    o = lax.map(block, (split(q_abs), split(q_pe), jnp.arange(nb) * blk))
    return o.transpose(1, 0, 2, 3, 4).reshape(B, L, H, KV_LORA)

def mla_sample_attention(q_abs, q_pe, c_new, kpe_new, c_past, kpe_past):
    Lq = q_abs.shape[1]
    s_past = latent_scores(q_abs, q_pe, c_past, kpe_past)
    s_new = latent_scores(q_abs, q_pe, c_new, kpe_new)
    tri = jnp.tril(jnp.ones((Lq, Lq), dtype=bool))
    s_new = jnp.where(tri, s_new, -jnp.inf)
    P = s_past.shape[-1]
    p = jax.nn.softmax(jnp.concatenate([s_past, s_new], axis=-1), axis=-1)
    o = jnp.einsum('bhqk,bkc->bqhc', p[..., :P].astype(c_past.dtype), c_past)
    o = o + jnp.einsum('bhqk,bkc->bqhc', p[..., P:].astype(c_new.dtype), c_new)
    return o.astype(q_abs.dtype)

def hybrid_mixer(x, pos, lb, w_in, q_norm, w_uq, kv_norm, w_ukv, out_norm, w_out, s0, c_past, kpe_past):
    B, L, _ = x.shape
    proj = x @ w_in
    q_hg, f_hg, i_hg, g_hg, cq, ckv, kr = jnp.split(proj, SPLIT_POINTS, axis=-1)
    z = f_hg.astype(jnp.float32).reshape(B, L, HG_HEADS, HG_DK)
    log_f = jnp.log(lb + (1.0 - lb) * jax.nn.sigmoid(z))
    k_in = (1.0 - lb) * jax.nn.sigmoid(-z)
    o_hg, s_new = hgrn2_recurrence(q_hg.astype(jnp.float32).reshape(B, L, HG_HEADS, HG_DK), k_in,
                                   i_hg.astype(jnp.float32).reshape(B, L, HG_HEADS, HG_DV), log_f,
                                   s0.astype(jnp.float32))
    o_hg = rms_norm(o_hg, out_norm) * jax.nn.silu(g_hg.astype(jnp.float32).reshape(B, L, HG_HEADS, HG_DV))
    o_hg = o_hg.reshape(B, L, HG_V_W).astype(x.dtype)
    qh = (rms_norm(cq, q_norm) @ w_uq).reshape(B, L, MLA_HEADS, NOPE_DIM + ROPE_DIM)
    q_nope = qh[..., :NOPE_DIM]
    q_pe = rope(qh[..., NOPE_DIM:], pos)
    c_kv = rms_norm(ckv, kv_norm)
    k_pe = rope(kr[:, :, None, :], pos)[:, :, 0, :]
    q_abs = jnp.einsum('blhn,chn->blhc', q_nope, w_ukv[..., :NOPE_DIM])
    if c_past is None:
        o_lat = mla_prompt_attention(q_abs, q_pe, c_kv, k_pe)
    else:
        o_lat = mla_sample_attention(q_abs, q_pe, c_kv, k_pe, c_past, kpe_past)
    o_mla = jnp.einsum('blhc,chv->blhv', o_lat, w_ukv[..., NOPE_DIM:]).reshape(B, L, MLA_HEADS * V_DIM)
    out = jnp.concatenate([o_hg, o_mla.astype(x.dtype)], axis=-1) @ w_out
    return out, c_kv, k_pe, s_new

def conv_module(x, buf, w_pw1, b_pw1, w_dw, b_dw, ln_g, ln_b, w_pw2, b_pw2):
    B = x.shape[0]
    h = x @ w_pw1 + b_pw1
    u = h[..., :CONV_DIM] * jax.nn.sigmoid(h[..., CONV_DIM:])
    if buf is None:
        buf = jnp.zeros((B, CONV_WIDTH - 1, CONV_DIM), u.dtype)
    ext = jnp.concatenate([buf.astype(u.dtype), u], axis=1)
    y = lax.conv_general_dilated(ext, w_dw[:, None, :].astype(u.dtype), (1,), 'VALID',
                                 dimension_numbers=('NWC', 'WIO', 'NWC'),
                                 feature_group_count=CONV_DIM) + b_dw
    y = jax.nn.silu(layer_norm(y, ln_g, ln_b))
    return y @ w_pw2 + b_pw2, ext[:, ext.shape[1] - (CONV_WIDTH - 1):]

def peer_ffn(x, w_q, sub_keys, u_tab, v_tab):
    B, L, D = x.shape
    n = B * L
    blk = min(PEER_BLOCK, n)
    nb = -(-n // blk)
    xp = jnp.pad(x.reshape(n, D), ((0, nb * blk - n), (0, 0))).reshape(nb, blk, D)

    def block(xb):
        q = (xb @ w_q).reshape(blk, PEER_HEADS, 2, PEER_HALF)
        s = jnp.einsum('thpd,phkd->thpk', q, sub_keys).astype(jnp.float32)
        sv, si = lax.top_k(s, PEER_TOPK)
        cand = sv[:, :, 0, :, None] + sv[:, :, 1, None, :]
        cand_idx = si[:, :, 0, :, None] * N_KEYS + si[:, :, 1, None, :]
        top_s, top_pos = lax.top_k(cand.reshape(blk, PEER_HEADS, PEER_TOPK * PEER_TOPK), PEER_TOPK)
        idx = jnp.take_along_axis(cand_idx.reshape(blk, PEER_HEADS, PEER_TOPK * PEER_TOPK), top_pos, axis=-1)
        g = jax.nn.softmax(top_s, axis=-1)
        u = u_tab[idx]
        v = v_tab[idx]
        act = jax.nn.gelu(jnp.einsum('thkd,td->thk', u, xb).astype(jnp.float32), approximate=False)
        return jnp.einsum('thk,thkd->td', (g * act).astype(xb.dtype), v)

    y = lax.map(block, xp).reshape(nb * blk, D)[:n]
    return y.reshape(B, L, D)

def setup_inputs(seed: int = 0) -> dict:
    key = jax.random.key(seed)
    keys = jax.random.split(key, 40)
    counter = [0]

    def nxt():
        k = keys[counter[0]]
        counter[0] += 1
        return k

    def nrm(shape, scale):
        return jax.random.normal(nxt(), shape, jnp.float32) * scale

    n_pages = PAST_LEN // PAGE_SIZE
    n_used = DEC_BATCH * n_pages
    n_pool = (5 * n_used + 3) // 4
    inp = {}
    inp['x_prompt'] = nrm((BATCH, SEQ, D_MODEL), 1.0)
    inp['x_sample'] = nrm((DEC_BATCH, DEC_SEQ, D_MODEL), 1.0)
    inp['cache_mla_latent'] = nrm((N_EVEN, n_pool, PAGE_SIZE, KV_LORA), 1.0)
    inp['cache_mla_krope'] = nrm((N_EVEN, n_pool, PAGE_SIZE, ROPE_DIM), 1.0)
    inp['state_hgrn'] = nrm((N_EVEN, DEC_BATCH, HG_HEADS, HG_DK, HG_DV), 0.5)
    inp['state_conv'] = nrm((N_ODD, DEC_BATCH, CONV_WIDTH - 1, CONV_DIM), 1.0)
    perm = jax.random.permutation(nxt(), n_pool)
    inp['page_table'] = perm[:n_used].reshape(DEC_BATCH, n_pages).astype(jnp.int32)
    inp['hg_lb_logits'] = nrm((DEPTH + 1, HG_QK_W), 0.1)
    inp['mix_w_in'] = nrm((N_EVEN, D_MODEL, MIX_IN), D_MODEL ** -0.5)
    inp['mla_q_norm'] = 1.0 + nrm((N_EVEN, Q_LORA), 0.02)
    inp['mla_w_uq'] = nrm((N_EVEN, Q_LORA, MLA_HEADS * (NOPE_DIM + ROPE_DIM)), Q_LORA ** -0.5)
    inp['mla_kv_norm'] = 1.0 + nrm((N_EVEN, KV_LORA), 0.02)
    inp['mla_w_ukv'] = nrm((N_EVEN, KV_LORA, MLA_HEADS, NOPE_DIM + V_DIM), KV_LORA ** -0.5)
    inp['hg_out_norm'] = 1.0 + nrm((N_EVEN, HG_DV), 0.02)
    inp['mix_w_out'] = nrm((N_EVEN, MIX_OUT, D_MODEL), DN_BETA * MIX_OUT ** -0.5)
    inp['conv_w_pw1'] = nrm((N_ODD, D_MODEL, 2 * CONV_DIM), D_MODEL ** -0.5)
    inp['conv_b_pw1'] = nrm((N_ODD, 2 * CONV_DIM), 0.02)
    inp['conv_w_dw'] = nrm((N_ODD, CONV_WIDTH, CONV_DIM), CONV_WIDTH ** -0.5)
    inp['conv_b_dw'] = nrm((N_ODD, CONV_DIM), 0.02)
    inp['conv_ln_g'] = 1.0 + nrm((N_ODD, CONV_DIM), 0.02)
    inp['conv_ln_b'] = nrm((N_ODD, CONV_DIM), 0.02)
    inp['conv_w_pw2'] = nrm((N_ODD, CONV_DIM, D_MODEL), DN_BETA * CONV_DIM ** -0.5)
    inp['conv_b_pw2'] = nrm((N_ODD, D_MODEL), 0.02)
    inp['peer_w_q'] = nrm((DEPTH, D_MODEL, PEER_HEADS * PEER_DK), D_MODEL ** -0.5)
    inp['peer_sub_keys'] = nrm((DEPTH, 2, PEER_HEADS, N_KEYS, PEER_HALF), PEER_HALF ** -0.5)
    inp['peer_u'] = nrm((DEPTH, N_EXPERTS, D_MODEL), D_MODEL ** -0.5)
    inp['peer_v'] = nrm((DEPTH, N_EXPERTS, D_MODEL), DN_BETA * PEER_HEADS ** -0.5)
    inp['ln_g'] = 1.0 + nrm((DEPTH, 2, D_MODEL), 0.02)
    inp['ln_b'] = nrm((DEPTH, 2, D_MODEL), 0.02)
    return inp

def reference(x_prompt, x_sample, cache_mla_latent, cache_mla_krope, state_hgrn, state_conv, page_table,
              hg_lb_logits, mix_w_in, mla_q_norm, mla_w_uq, mla_kv_norm, mla_w_ukv, hg_out_norm, mix_w_out,
              conv_w_pw1, conv_b_pw1, conv_w_dw, conv_b_dw, conv_ln_g, conv_ln_b, conv_w_pw2, conv_b_pw2,
              peer_w_q, peer_sub_keys, peer_u, peer_v, ln_g, ln_b):
    bp, lp, _ = x_prompt.shape
    bs, ls, _ = x_sample.shape
    n_pages = page_table.shape[1]
    past_len = n_pages * PAGE_SIZE
    pos_p = jnp.arange(lp)
    pos_s = past_len + jnp.arange(ls)
    lb_all = jnp.cumsum(jax.nn.softmax(hg_lb_logits.astype(jnp.float32), axis=0), axis=0)
    hp, hs = x_prompt, x_sample
    lat_p, kpe_p, hg_p, conv_p = [], [], [], []
    lat_s, kpe_s, hg_s, conv_s = [], [], [], []
    for layer in range(DEPTH):
        if layer % 2 == 0:
            e = layer // 2
            lb = lb_all[layer].reshape(HG_HEADS, HG_DK)
            w = (mix_w_in[e], mla_q_norm[e], mla_w_uq[e], mla_kv_norm[e], mla_w_ukv[e], hg_out_norm[e], mix_w_out[e])
            s0 = jnp.zeros((bp, HG_HEADS, HG_DK, HG_DV), jnp.float32)
            mp, c_new_p, k_new_p, s_new_p = hybrid_mixer(hp, pos_p, lb, *w, s0, None, None)
            c_past = cache_mla_latent[e][page_table].reshape(bs, past_len, KV_LORA)
            k_past = cache_mla_krope[e][page_table].reshape(bs, past_len, ROPE_DIM)
            ms, c_new_s, k_new_s, s_new_s = hybrid_mixer(hs, pos_s, lb, *w, state_hgrn[e], c_past, k_past)
            lat_p.append(c_new_p)
            kpe_p.append(k_new_p)
            hg_p.append(s_new_p)
            lat_s.append(c_new_s)
            kpe_s.append(k_new_s)
            hg_s.append(s_new_s)
        else:
            o = layer // 2
            w = (conv_w_pw1[o], conv_b_pw1[o], conv_w_dw[o], conv_b_dw[o], conv_ln_g[o], conv_ln_b[o],
                 conv_w_pw2[o], conv_b_pw2[o])
            mp, buf_p = conv_module(hp, None, *w)
            ms, buf_s = conv_module(hs, state_conv[o], *w)
            conv_p.append(buf_p)
            conv_s.append(buf_s)
        hp = layer_norm(DN_ALPHA * hp + mp, ln_g[layer, 0], ln_b[layer, 0])
        hs = layer_norm(DN_ALPHA * hs + ms, ln_g[layer, 0], ln_b[layer, 0])
        pw = (peer_w_q[layer], peer_sub_keys[layer], peer_u[layer], peer_v[layer])
        hp = layer_norm(DN_ALPHA * hp + peer_ffn(hp, *pw), ln_g[layer, 1], ln_b[layer, 1])
        hs = layer_norm(DN_ALPHA * hs + peer_ffn(hs, *pw), ln_g[layer, 1], ln_b[layer, 1])
    new_lat_p = jnp.stack(lat_p)
    new_kpe_p = jnp.stack(kpe_p)
    new_hgrn_p = jnp.stack(hg_p)
    new_conv_p = jnp.stack(conv_p)
    new_lat_s = jnp.stack(lat_s)
    new_kpe_s = jnp.stack(kpe_s)
    new_hgrn_s = jnp.stack(hg_s)
    new_conv_s = jnp.stack(conv_s)
    return (hp, hs, new_lat_p, new_kpe_p, new_hgrn_p, new_conv_p, new_lat_s, new_kpe_s, new_hgrn_s, new_conv_s)


_drawn_inputs = setup_inputs


def setup_inputs(seed=0):
    import zlib

    import numpy as np

    out = dict(_drawn_inputs(seed))
    spreads = {}
    factors = {'cache_mla_latent': 4.677,
     'cache_mla_krope': 7.251,
     'mla_q_norm': 24.428,
     'mla_kv_norm': 7.963,
     'hg_out_norm': 23.646,
     'conv_b_pw1': 2.681,
     'conv_b_dw': 5.514,
     'conv_ln_g': 21.895,
     'conv_ln_b': 23.159,
     'conv_b_pw2': 16.97}
    for name, (base, spread) in spreads.items():
        noise = np.random.default_rng([zlib.crc32(name.encode()), seed]).standard_normal(out[name].shape)
        drawn = base * np.exp(spread * noise) if base else spread * noise
        out[name] = __import__('jax').numpy.asarray(drawn.astype(out[name].dtype))
    for name, factor in factors.items():
        out[name] = (out[name] * factor).astype(out[name].dtype)
    return out
```

```python
from contextlib import ExitStack

import concourse.bass as bass
import numpy as np
from concourse import mybir

F32 = mybir.dt.float32
F32R = mybir.dt.float32r
U32 = mybir.dt.uint32
I32 = mybir.dt.int32
ALU = mybir.AluOpType
ACT = mybir.ActivationFunctionType
AX = mybir.AxisListType

P = 128
D = 1024
KC = D // P
TP, TS = 512, 8
T = TP + TS
TH = T // 2
TT, NT = 104, 5
H = 4
CL, NCH = 128, 4
QL, KVL, ROPE = 384, 256, 64
QC, CC = QL // P, KVL // P
PAST, PAGE = 2048, 128
NPG = PAST // PAGE
POOL_PAGES = 160
CW = 31
PH = 8
NK = 128
HP = 2 * PH
TOPK = 16
CANDA, CANDB = 4, 12
NCAND = CANDA * 16 + CANDB * 4
NEG = -3.0e38
ALPHA = 4.0 ** 0.25
SCALE = float(128 + ROPE) ** -0.5
LN_EPS, RMS_EPS = 1e-5, 1e-6
LEVELS = 8
GB = 4
NG = NK // GB

VEC = {}
_at = 0
for _name, _n in (("ln_g00", KC), ("ln_g01", KC), ("ln_g10", KC), ("ln_g11", KC),
                  ("ln_b00", KC), ("ln_b01", KC), ("ln_b10", KC), ("ln_b11", KC),
                  ("b_pw1", 2 * KC), ("b_dw", KC), ("cln_g", KC), ("cln_b", KC), ("b_pw2", KC),
                  ("q_norm", QC), ("kv_norm", CC), ("out_norm", 1), ("lb", 3 * H), ("w_dw", CW * KC)):
    VEC[_name] = _at
    _at += _n
NVEC = _at


def bc(ap, axis, n):
    a = ap.unsqueeze(axis)
    shape = list(a.shape)
    shape[axis] = n
    return a.broadcast_to(shape)


def halves(ap):
    return ap.rearrange("p (a t) -> p a t", a=2)


def wait(eng, sem, value):
    eng.wait_ge(sem, value)
    if not isinstance(value, int):
        eng.nop(nofuse=True)


class Chain:

    def __init__(self, eng, sem):
        self.eng, self.sem, self.n = eng, sem, 0

    def __call__(self, ins, base=0):
        self.n += 1
        ins.then_inc(self.sem, 1)
        wait(self.eng, self.sem, base + self.n)


class Stage:

    def __init__(self, nc, name):
        self.nc, self.name, self.ctx, self.sems = nc, name, ExitStack(), []

    def __enter__(self):
        self.ctx.__enter__()
        return self

    def __exit__(self, *a):
        if self.sems and a[0] is None:
            self.nc.clear_and_free_semaphores(self.sems)
            self.nc.all_engine_barrier()
        return self.ctx.__exit__(*a)

    def sb(self, name, shape, dt=F32):
        return self.ctx.enter_context(self.nc.sbuf_tensor(f"{self.name}_{name}", shape, dt))

    def sem(self, name):
        self.sems.append(self.nc.alloc_semaphore(name=f"{self.name}_{name}"))
        return self.sems[-1]

    def block(self):
        return self.nc.Block()


def load_constants(nc, a, k):
    with Stage(nc, "load") as s:
        landed = s.sem("landed")
        zeroed = s.sem("zeroed")
        filled = s.sem("filled")
        with s.block() as block:
            @block.sync
            def _(sp):
                sp.dma_start(k.x[:], a["x_t"]).then_inc(landed, 16)
                sp.dma_start(k.vec[:], a["vecs"]).then_inc(landed, 16)
                sp.wait_ge(landed, 32)

            @block.vector
            def _(v):
                v.memset(k.mean_d[:], 1.0 / D)
                v.memset(k.ones[:], 1.0)
                v.memset(k.mean_p[:], 1.0 / P)
                v.memset(k.mean_q[:], 1.0 / QL)
                v.memset(k.mean_kv[:], 1.0 / KVL)

            @block.gpsimd
            def _(g):
                g.memset(k.ident[:], 0.0).then_inc(zeroed, 1)
                g.wait_ge(zeroed, 1)
                g.affine_select(out=k.ident[:], in_=k.ident[:], compare_op=ALU.not_equal, fill=1.0, base=0,
                                pattern=[[-1, P]], channel_multiplier=1).then_inc(filled, 1)
                g.iota(k.iota[:], pattern=[[1, P]], base=0, channel_multiplier=0,
                       allow_small_or_imprecise_dtypes=True).then_inc(filled, 1)
                g.wait_ge(filled, 2)


def linear(nc, k, name, w, rhs, out, m, kc):
    with Stage(nc, name) as s:
        slab = s.sb("slab", [P, 2, kc, P])
        landed = [s.sem(f"landed{b}") for b in range(2)]
        slab_free = s.sem("slab_free")
        psum_free = s.sem("psum_free")
        ready = s.sem("ready")
        with s.block() as block:
            @block.sync
            def _(sp):
                for b in range(2):
                    sp.dma_start(slab[:, b], w[b]).then_inc(landed[b], 16)
                with sp.Fori(0, m // 2 - 1) as i:
                    for b in range(2):
                        wait(sp, slab_free, 2 * i + b + 1)
                        sp.dma_start(slab[:, b], w[bass.ds(2 * i + 2 + b, 1)].rearrange("o p k m -> (o p) k m")
                                     ).then_inc(landed[b], 16)

            @block.tensor
            def _(pe):
                with pe.Fori(0, m // 2) as i:
                    for b in range(2):
                        pe.wait_ge(landed[b], 16 * i + 16)
                        pe.wait_ge(psum_free, 2 * i + b + 1)
                        for h in range(2):
                            for c in range(kc):
                                mm = pe.matmul(k.ps[:, 2 * b + h, 0:TH], slab[:, b, c], rhs[:, c, h * TH:(h + 1) * TH],
                                               start=(c == 0), stop=(c == kc - 1))
                            if h == 0:
                                mm.then_inc(ready, 1)
                        mm.then_inc(slab_free, 1)

            @block.vector
            def _(v):
                v.sem_inc(psum_free, 2)
                with v.Fori(0, m // 2) as i:
                    for b in range(2):
                        v.wait_ge(slab_free, 2 * i + b + 1)
                        v.tensor_copy(halves(out[:, bass.ds(2 * i + b, 1), :].rearrange("p o t -> p (o t)")),
                                      k.ps[:, 2 * b:2 * b + 2, 0:TH]).then_inc(psum_free, 1)


def inverse_root(chain, var, root, tmp):
    v = chain.eng
    chain(v.reciprocal(root, root))
    chain(v.tensor_tensor(tmp, root, root, ALU.mult))
    chain(v.tensor_tensor(tmp, tmp, var, ALU.mult))
    chain(v.tensor_scalar(tmp, tmp, -0.5, 1.5, ALU.mult, ALU.add))
    chain(v.tensor_tensor(root, root, tmp, ALU.mult))


def layer_norm(nc, k, name, r, g, b, out, func):
    with Stage(nc, name) as s:
        sq = s.sb("sq", [P, KC, T])
        var = s.sb("var", [P, T])
        rstd = s.sb("rstd", [P, T])
        newton = s.sb("newton", [P, T])
        mean_ready = s.sem("mean_ready")
        centred = s.sem("centred")
        squared = s.sem("squared")
        var_ready = s.sem("var_ready")
        var_copied = s.sem("var_copied")
        rooted = s.sem("rooted")
        link = s.sem("link")
        normed = s.sem("normed")
        with s.block() as block:
            @block.tensor
            def _(pe):
                for h in range(2):
                    for c in range(KC):
                        mm = pe.matmul(k.ps[:, h, 0:TH], k.mean_d[:], r[:, c, h * TH:(h + 1) * TH],
                                       start=(c == 0), stop=(c == KC - 1))
                    mm.then_inc(mean_ready, 1)
                for h in range(2):
                    pe.wait_ge(squared, h + 1)
                    for c in range(KC):
                        mm = pe.matmul(k.ps[:, 2 + h, 0:TH], k.mean_d[:], sq[:, c, h * TH:(h + 1) * TH],
                                       start=(c == 0), stop=(c == KC - 1))
                    mm.then_inc(var_ready, 1)

            @block.vector
            def _(v):
                for h in range(2):
                    rh = r[:, :, h * TH:(h + 1) * TH]
                    v.wait_ge(mean_ready, h + 1)
                    v.tensor_tensor(rh, rh, bc(k.ps[:, h, 0:TH], 1, KC), ALU.subtract).then_inc(centred, 1)
                for h in range(2):
                    v.wait_ge(var_ready, h + 1)
                    v.tensor_scalar(var[:, h * TH:(h + 1) * TH], k.ps[:, 2 + h, 0:TH], LN_EPS, None, ALU.add
                                    ).then_inc(var_copied, 1)
                v.wait_ge(rooted, 1)
                inverse_root(Chain(v, link), var[:], rstd[:], newton[:])
                for h in range(2):
                    rh = r[:, :, h * TH:(h + 1) * TH]
                    v.tensor_tensor(rh, rh, bc(rstd[:, h * TH:(h + 1) * TH], 1, KC), ALU.mult).then_inc(normed, 1)

            @block.scalar
            def _(act):
                for h in range(2):
                    act.wait_ge(centred, h + 1)
                    act.activation(sq[:, :, h * TH:(h + 1) * TH], r[:, :, h * TH:(h + 1) * TH], ACT.Square
                                   ).then_inc(squared, 1)
                act.wait_ge(var_copied, 2)
                act.activation(rstd[:], var[:], ACT.Sqrt).then_inc(rooted, 1)
                for h in range(2):
                    act.wait_ge(normed, h + 1)
                    for c in range(KC):
                        act.activation(out[:, c, h * TH:(h + 1) * TH], r[:, c, h * TH:(h + 1) * TH], func,
                                       bias=k.col(b, c), scale=k.col(g, c))


def residual(nc, k, name, r):
    with Stage(nc, name) as s, s.block() as block:
        @block.vector
        def _(v):
            v.scalar_tensor_tensor(r[:], k.x[:], ALPHA, r[:], ALU.mult, ALU.add)


class Kept:

    def __init__(self, nc, ctx):
        def sb(name, shape, dt=F32):
            return ctx.enter_context(nc.sbuf_tensor(name, shape, dt))

        self.x = sb("x", [P, KC, T])
        self.vec = sb("vec", [P, NVEC])
        self.mean_d = sb("mean_d", [P, P])
        self.ones = sb("ones", [P, P])
        self.mean_p = sb("mean_p", [P, P])
        self.mean_q = sb("mean_q", [P, P])
        self.mean_kv = sb("mean_kv", [P, P])
        self.ident = sb("ident", [P, P])
        self.iota = sb("iota", [P, P])
        self.ps = ctx.enter_context(nc.psum_tensor("ps", [P, 8, 512], F32))

    def col(self, name, j=0):
        at = VEC[name] + j
        return self.vec[:, at:at + 1]


def mix_values(nc, k, a, vt, vs):
    with Stage(nc, "values") as s:
        w = s.sb("w", [P, KC, H * P])
        landed = s.sem("landed")
        ready = s.sem("ready")
        with s.block() as block:
            @block.sync
            def _(sp):
                sp.dma_start(w[:], a["w_val"]).then_inc(landed, 16)

            @block.tensor
            def _(pe):
                pe.wait_ge(landed, 16)
                for t in range(NCH + 1):
                    n = CL if t < NCH else TS
                    for c in range(KC):
                        mm = pe.matmul(k.ps[0:n, t, :], k.x[:, c, t * CL:t * CL + n], w[:, c, :],
                                       start=(c == 0), stop=(c == KC - 1))
                    mm.then_inc(ready, 1)

            @block.vector
            def _(v):
                for t in range(NCH):
                    v.wait_ge(ready, t + 1)
                    v.tensor_copy(vt[:, t, :], k.ps[:, t, :])
                v.wait_ge(ready, NCH + 1)
                v.tensor_copy(vs[:], k.ps[0:TS, NCH, :])


def recurrence(nc, k, a, proj, vt, vs, cat):
    with Stage(nc, "rec") as s:
        f = s.sb("f", [P, H, T])
        kk = s.sb("k", [P, H, T])
        pre = s.sb("pre", [P, H, TP])
        suf = s.sb("suf", [P, H, TP])
        kd = s.sb("kd", [P, 2, H, TP])
        qd = s.sb("qd", [P, 2, H, TP])
        attn = s.sb("attn", [P, H, NCH, CL])
        masks = s.sb("masks", [P, LEVELS, CL], U32)
        lb = s.sb("lb", [P, 6, H])
        kt = s.sb("kt", [P, H, NCH, P])
        state = s.sb("state", [P, H, P])
        q = proj[:, 0:H]
        gate = proj[:, 2 * H:3 * H]
        landed = s.sem("landed")
        link = s.sem("link")
        lb_e = s.sem("lb_e")
        lb_m = s.sem("lb_m")
        sig = s.sem("sig")
        decayed = s.sem("decayed")
        level_ready = s.sem("level_ready")
        level_read = s.sem("level_read")
        turned = s.sem("turned")
        kt_ready = s.sem("kt_ready")
        chunk_ready = s.sem("chunk_ready")
        chunk_read = s.sem("chunk_read")
        stored = s.sem("stored")
        with s.block() as block:
            @block.sync
            def _(sp):
                sp.dma_start(masks[:], a["masks"]).then_inc(landed, 16)
                sp.wait_ge(chunk_read, NCH)
                sp.dma_start(a["new_hgrn_p"], state[:]).then_inc(stored, 16)
                sp.wait_ge(stored, 16)

            @block.scalar
            def _(act):
                act.activation(f[:], proj[:, H:2 * H], ACT.Sigmoid).then_inc(sig, 1)
                act.activation(kk[:], proj[:, H:2 * H], ACT.Sigmoid, scale=-1.0).then_inc(sig, 1)
                act.activation(gate, gate, ACT.Silu)
                act.wait_ge(lb_m, 1)
                act.activation(lb[:, 0:3], lb[:, 0:3], ACT.Exp).then_inc(lb_e, 1)

            @block.vector
            def _(v):
                chain = Chain(v, link)
                logit = k.vec[:, VEC["lb"]:VEC["lb"] + 3 * H].rearrange("p (l h) -> p l h", l=3)
                chain(v.tensor_tensor(lb[:, 3], logit[:, 0], logit[:, 1], ALU.max))
                chain(v.tensor_tensor(lb[:, 3], lb[:, 3], logit[:, 2], ALU.max))
                v.tensor_tensor(lb[:, 0:3], logit, bc(lb[:, 3], 1, 3), ALU.subtract).then_inc(lb_m, 1)
                v.wait_ge(lb_e, 1)
                chain(v.tensor_tensor(lb[:, 3], lb[:, 0], lb[:, 1], ALU.add))
                chain(v.tensor_tensor(lb[:, 3], lb[:, 3], lb[:, 2], ALU.add))
                chain(v.reciprocal(lb[:, 3], lb[:, 3]))
                chain(v.tensor_tensor(lb[:, 4], lb[:, 0], lb[:, 3], ALU.mult))
                chain(v.tensor_scalar(lb[:, 5], lb[:, 4], -1.0, 1.0, ALU.mult, ALU.add))
                v.wait_ge(sig, 2)
                for h in range(H):
                    v.tensor_scalar(f[:, h], f[:, h], lb[:, 5, h:h + 1], lb[:, 4, h:h + 1], ALU.mult, ALU.add)
                    ins = v.tensor_scalar(kk[:, h], kk[:, h], lb[:, 5, h:h + 1], None, ALU.mult)
                chain(ins)
                v.tensor_copy(pre[:], f[:, :, 0:TP])
                v.memset(suf[:], 1.0)
                v.memset(attn[:], 0.0)
                chain(v.tensor_copy(kd[:, 0], kk[:, :, 0:TP]))
                v.tensor_copy(qd[:, 0], q[:, :, 0:TP]).then_inc(decayed, 1)
                v.wait_ge(landed, 16)

                def take(level):
                    v.wait_ge(level_ready, level + 1)
                    v.copy_predicated(attn[:].rearrange("s h c t -> s (h c) t"), bc(masks[:, level], 1, H * NCH),
                                      k.ps[:, 4 * (level % 2):4 * (level % 2) + 4, :]
                                      .rearrange("s h (c t) -> s (h c) t", t=CL)).then_inc(level_read, 1)

                for level in range(1, LEVELS + 1):
                    m = 1 << (level - 1)
                    if level > 1:
                        hf = m // 2
                        v.wait_ge(decayed, level)
                        p2 = pre[:].rearrange("p h (n m) -> p (h n) m", m=m)
                        s2 = suf[:].rearrange("p h (n m) -> p (h n) m", m=m)
                        chain(v.tensor_tensor(s2[:, :, 0:hf], s2[:, :, 0:hf], bc(p2[:, :, m - 1], 2, hf), ALU.mult))
                        chain(v.tensor_tensor(p2[:, :, hf:m], p2[:, :, hf:m], bc(p2[:, :, hf - 1], 2, hf), ALU.mult))
                    if level >= 2:
                        v.wait_ge(level_ready, level - 1)
                    v.tensor_tensor(kd[:, level % 2], kk[:, :, 0:TP], suf[:], ALU.mult)
                    v.tensor_tensor(qd[:, level % 2], q[:, :, 0:TP], pre[:], ALU.mult).then_inc(decayed, 1)
                    take(level - 1)
                v.wait_ge(turned, 1)
                v.tensor_copy(kt[:].rearrange("s h c d -> s (h c d)"), k.ps[:, 0:4, :].rearrange("s b d -> s (b d)")
                              ).then_inc(kt_ready, 1)
                for c in range(NCH):
                    v.wait_ge(chunk_ready, c + 1)
                    bank = 4 + 2 * (c % 2)
                    v.tensor_copy(cat[:, 0:H, c * CL:(c + 1) * CL], k.ps[:, bank, :].rearrange("p (h t) -> p h t", h=H))
                    new = k.ps[:, bank + 1, :].rearrange("p (h d) -> p h d", h=H)
                    if c == 0:
                        v.tensor_copy(state[:], new).then_inc(chunk_read, 1)
                    else:
                        last = pre[:].rearrange("p h (c t) -> p h c t", t=CL)[:, :, c, CL - 1]
                        chain(v.tensor_tensor(state[:], state[:], bc(last, 2, P), ALU.mult))
                        v.tensor_tensor(state[:], state[:], new, ALU.add).then_inc(chunk_read, 1)
                    v.wait_ge(chunk_read, c + 1)

            @block.tensor
            def _(pe):
                for level in range(LEVELS):
                    pe.wait_ge(decayed, level + 1)
                    if level >= 2:
                        pe.wait_ge(level_read, level - 1)
                    for h in range(H):
                        for c in range(NCH):
                            t = slice(c * CL, (c + 1) * CL)
                            mm = pe.matmul(k.ps[:, 4 * (level % 2) + h, t], kd[:, level % 2, h, t], qd[:, level % 2, h, t],
                                           start=True, stop=True)
                    mm.then_inc(level_ready, 1)
                pe.wait_ge(decayed, LEVELS + 1)
                pe.wait_ge(level_read, LEVELS)
                for h in range(H):
                    for c in range(NCH):
                        t = slice(c * CL, (c + 1) * CL)
                        mm = pe.transpose(k.ps[:, h, t], kd[:, 0, h, t], k.ident[:])
                mm.then_inc(turned, 1)
                pe.wait_ge(kt_ready, 1)
                for c in range(NCH):
                    bank = 4 + 2 * (c % 2)
                    if c:
                        pe.wait_ge(chunk_read, c)
                    for h in range(H):
                        o = k.ps[:, bank, h * CL:(h + 1) * CL]
                        pe.matmul(o, vt[:, c, h * P:(h + 1) * P], attn[:, h, c], start=True, stop=(c == 0))
                        if c:
                            pe.matmul(o, state[:, h], qd[:, 0, h, c * CL:(c + 1) * CL], start=False, stop=True)
                        mm = pe.matmul(k.ps[:, bank + 1, h * P:(h + 1) * P], kt[:, h, c], vt[:, c, h * P:(h + 1) * P],
                                       start=True, stop=True)
                    mm.then_inc(chunk_ready, 1)

        old = s.sb("old", [P, 2, H, P])
        new = s.sb("new", [P, 2, H, P])
        kv = s.sb("kv", [P, H, P])
        old_landed = [s.sem(f"old_landed{b}") for b in range(2)]
        new_stored = [s.sem(f"new_stored{b}") for b in range(2)]
        v_spread = s.sem("v_spread")
        step = s.sem("step")
        new_ready = s.sem("new_ready")
        read_out = s.sem("read_out")
        with s.block() as block:
            @block.sync
            def _(sp):
                for b in range(2):
                    sp.dma_start(old[:, b], a["state_hgrn"][b]).then_inc(old_landed[b], 16)
                for n in range(TS):
                    sp.wait_ge(new_ready, n + 1)
                    sp.dma_start(a["new_hgrn_s"][n], new[:, n % 2]).then_inc(new_stored[n % 2], 16)
                    if n + 2 < TS:
                        sp.dma_start(old[:, n % 2], a["state_hgrn"][n + 2]).then_inc(old_landed[n % 2], 16)
                for b in range(2):
                    sp.wait_ge(new_stored[b], 16 * TS // 2)

            @block.tensor
            def _(pe):
                for n in range(TS):
                    if n >= 2:
                        pe.wait_ge(new_ready, n - 1)
                    pe.matmul(k.ps[:, n % 2, :], k.ident[0:TS, n:n + 1].broadcast_to([TS, P]), vs[:],
                              start=True, stop=True).then_inc(v_spread, 1)
                    pe.wait_ge(new_ready, n + 1)
                    for h in range(H):
                        mm = pe.matmul(k.ps[:, 2, n * H + h:n * H + h + 1], new[:, n % 2, h],
                                       q[:, h, TP + n:TP + n + 1], start=True, stop=True)
                    mm.then_inc(read_out, 1)

            @block.vector
            def _(v):
                chain = Chain(v, step)
                for n in range(TS):
                    v.wait_ge(v_spread, n + 1)
                    v.wait_ge(old_landed[n % 2], n // 2 * 16 + 16)
                    if n >= 2:
                        v.wait_ge(new_stored[n % 2], (n // 2) * 16)
                        v.wait_ge(read_out, n - 1)
                    chain(v.tensor_tensor(kv[:], k.ps[:, n % 2, :].rearrange("p (h d) -> p h d", h=H),
                                          bc(kk[:, :, TP + n], 2, P), ALU.mult))
                    chain(v.tensor_tensor(new[:, n % 2], old[:, n % 2], bc(f[:, :, TP + n], 2, P), ALU.mult))
                    v.tensor_tensor(new[:, n % 2], new[:, n % 2], kv[:], ALU.add).then_inc(new_ready, 1)
                    v.wait_ge(new_ready, n + 1)
                v.wait_ge(read_out, TS)
                v.tensor_copy(cat[:, 0:H, TP:T], k.ps[:, 2, 0:TS * H].rearrange("p (n h) -> p h n", h=H))

        sq = kd[:].rearrange("p a h t -> p (a h t)")[:, 0:H * T].rearrange("p (h t) -> p h t", h=H)
        var, rstd, tmp = (z[:].rearrange("p h t -> p (h t)")[:, 0:2 * T] for z in (pre, suf, kk))
        squared = s.sem("squared")
        rms_ready = s.sem("rms_ready")
        copied = s.sem("copied")
        rooted = s.sem("rooted")
        rlink = s.sem("rlink")
        with s.block() as block:
            @block.scalar
            def _(act):
                act.activation(sq, cat[:, 0:H], ACT.Square).then_inc(squared, 1)
                for g in range(2):
                    act.wait_ge(copied, g + 1)
                    act.activation(rstd, var, ACT.Sqrt).then_inc(rooted, 1)

            @block.tensor
            def _(pe):
                pe.wait_ge(squared, 1)
                for h in range(H):
                    for b in range(2):
                        mm = pe.matmul(k.ps[:, 2 * h + b, 0:TH], k.mean_p[:], sq[:, h, b * TH:(b + 1) * TH],
                                       start=True, stop=True)
                mm.then_inc(rms_ready, 1)

            @block.vector
            def _(v):
                chain = Chain(v, rlink)
                v.wait_ge(rms_ready, 1)
                for g in range(2):
                    v.tensor_scalar(var.rearrange("p (b t) -> p b t", b=4), k.ps[:, 4 * g:4 * g + 4, 0:TH], RMS_EPS,
                                    None, ALU.add).then_inc(copied, 1)
                    v.wait_ge(rooted, g + 1)
                    inverse_root(chain, var, rstd, tmp)
                    for h in range(2):
                        o = cat[:, 2 * g + h]
                        chain(v.scalar_tensor_tensor(o, o, k.col("out_norm"), rstd[:, h * T:(h + 1) * T], ALU.mult, ALU.mult))
                        chain(v.tensor_tensor(o, o, gate[:, 2 * g + h], ALU.mult))


def rms(nc, k, name, x, n, mean, g, out):
    with Stage(nc, name) as s:
        sq = s.sb("sq", [P, n, T])
        var = s.sb("var", [P, T])
        rstd = s.sb("rstd", [P, T])
        tmp = s.sb("tmp", [P, T])
        squared = s.sem("squared")
        ready = s.sem("ready")
        copied = s.sem("copied")
        rooted = s.sem("rooted")
        link = s.sem("link")
        with s.block() as block:
            @block.scalar
            def _(act):
                act.activation(sq[:], x, ACT.Square).then_inc(squared, 1)
                act.wait_ge(copied, 1)
                act.activation(rstd[:], var[:], ACT.Sqrt).then_inc(rooted, 1)

            @block.tensor
            def _(pe):
                pe.wait_ge(squared, 1)
                for h in range(2):
                    for c in range(n):
                        mm = pe.matmul(k.ps[:, h, 0:TH], mean[:], sq[:, c, h * TH:(h + 1) * TH],
                                       start=(c == 0), stop=(c == n - 1))
                mm.then_inc(ready, 1)

            @block.vector
            def _(v):
                chain = Chain(v, link)
                v.wait_ge(ready, 1)
                v.tensor_scalar(halves(var[:]), k.ps[:, 0:2, 0:TH], RMS_EPS, None, ALU.add).then_inc(copied, 1)
                v.wait_ge(rooted, 1)
                inverse_root(chain, var[:], rstd[:], tmp[:])
                for c in range(n):
                    v.scalar_tensor_tensor(out[:, c], x[:, c], k.col(g, c), rstd[:], ALU.mult, ALU.mult)


def latent_queries(nc, k, a, proj, qabs, qpe, kpe, ckv):
    with Stage(nc, "lq") as s:
        cq = s.sb("cq", [P, QC, T])
        rms(nc, k, "rms_q", proj[:, 3 * H:3 * H + QC], QC, k.mean_q, "q_norm", cq)
        rms(nc, k, "rms_kv", proj[:, 3 * H + QC:3 * H + QC + CC], CC, k.mean_kv, "kv_norm", ckv)
        wuq = s.sb("wuq", [P, QC, 2 * H * P])
        wuk = s.sb("wuk", [P, H, KVL])
        qn = s.sb("qn", [P, H, T])
        cos = s.sb("cos", [ROPE, T])
        sin = s.sb("sin", [ROPE, T])
        swapped = s.sb("swapped", [ROPE, T])
        rot = s.sb("rot", [ROPE, T])
        landed = s.sem("landed")
        tables = s.sem("tables")
        ready = s.sem("ready")
        free = s.sem("free")
        link = s.sem("link")
        abs_ready = s.sem("abs_ready")
        abs_free = s.sem("abs_free")
        k_ready = s.sem("k_ready")
        stored = s.sem("stored")
        with s.block() as block:
            @block.sync
            def _(sp):
                sp.dma_start(wuq[:], a["w_uq"]).then_inc(landed, 16)
                sp.dma_start(wuk[:], a["w_uk"]).then_inc(landed, 16)
                sp.dma_start(cos[:], a["cos"]).then_inc(tables, 16)
                sp.dma_start(sin[:], a["sin"]).then_inc(tables, 16)
                sp.dma_start(swapped[:], proj[ROPE:P, 3 * H + QC + CC, :]).then_inc(tables, 16)
                sp.dma_start(a["new_lat"], ckv[:]).then_inc(stored, 16)
                sp.wait_ge(k_ready, 1)
                sp.dma_start(a["new_kpe"], kpe[:]).then_inc(stored, 16)
                sp.wait_ge(stored, 32)

            @block.tensor
            def _(pe):
                pe.wait_ge(landed, 32)
                n = 0
                for h in range(H):
                    if n >= 2:
                        pe.wait_ge(free, n - 1)
                    for b in range(2):
                        for c in range(QC):
                            mm = pe.matmul(k.ps[:, 2 * (n % 2) + b, 0:TH], wuq[:, c, h * P:(h + 1) * P],
                                           cq[:, c, b * TH:(b + 1) * TH], start=(c == 0), stop=(c == QC - 1))
                    mm.then_inc(ready, 1)
                    n += 1
                for h in range(H):
                    for sw in range(2):
                        pe.wait_ge(free, n - 1)
                        at = H * P + sw * H * ROPE + h * ROPE
                        for b in range(2):
                            for c in range(QC):
                                mm = pe.matmul(k.ps[0:ROPE, 2 * (n % 2) + b, 0:TH], wuq[:, c, at:at + ROPE],
                                               cq[:, c, b * TH:(b + 1) * TH], start=(c == 0), stop=(c == QC - 1))
                        mm.then_inc(ready, 1)
                        n += 1
                pe.wait_ge(free, H)
                for h in range(H):
                    for c in range(CC):
                        m = CC * h + c
                        if m >= 2:
                            pe.wait_ge(abs_free, m - 1)
                        for b in range(2):
                            mm = pe.matmul(k.ps[:, 4 + 2 * (m % 2) + b, 0:TH], wuk[:, h, c * P:(c + 1) * P],
                                           qn[:, h, b * TH:(b + 1) * TH], start=True, stop=True)
                        mm.then_inc(abs_ready, 1)

            @block.scalar
            def _(act):
                for m in range(H * CC):
                    act.wait_ge(abs_ready, m + 1)
                    act.copy(halves(qabs[:, m // CC, m % CC]), k.ps[:, 4 + 2 * (m % 2):6 + 2 * (m % 2), 0:TH]
                             ).then_inc(abs_free, 1)

            @block.vector
            def _(v):
                chain = Chain(v, link)
                v.wait_ge(tables, 48)
                kr = proj[0:ROPE, 3 * H + QC + CC]
                v.tensor_tensor(kpe[:], kr, cos[:], ALU.mult)
                chain(v.tensor_tensor(rot[:], swapped[:], sin[:], ALU.mult))
                v.tensor_tensor(kpe[:], kpe[:], rot[:], ALU.add).then_inc(k_ready, 1)
                for h in range(H):
                    v.wait_ge(ready, h + 1)
                    v.tensor_copy(halves(qn[:, h]), k.ps[:, 2 * (h % 2):2 * (h % 2) + 2, 0:TH]).then_inc(free, 1)
                for h in range(H):
                    v.wait_ge(ready, H + 2 * h + 1)
                    v.tensor_tensor(halves(qpe[:, h]), k.ps[0:ROPE, 0:2, 0:TH], halves(cos[:]), ALU.mult).then_inc(free, 1)
                    v.wait_ge(ready, H + 2 * h + 2)
                    v.tensor_tensor(halves(rot[:]), k.ps[0:ROPE, 2:4, 0:TH], halves(sin[:]), ALU.mult).then_inc(free, 1)
                    v.wait_ge(free, H + 2 * h + 2)
                    chain(v.tensor_tensor(qpe[:, h], qpe[:, h], rot[:], ALU.add))


def attention(nc, k, a, qabs, qpe, kpe, ckv, olat):
    NS = TS * H
    with Stage(nc, "pa") as s:
        ctok = s.sb("ctok", [P, NCH, KVL])
        mask = s.sb("mask", [P, 512])
        sc = s.sb("sc", [P, H, 512])
        prob = s.sb("prob", [P, H, 512])
        pt = s.sb("pt", [P, H, 512])
        mx = s.sb("mx", [P, H])
        total = s.sb("total", [P, H])
        pages = s.sb("pages", [1, TS * NPG], I32)
        ct = s.sb("ct", [P, 2, NPG, KVL + PAGE])
        qa = s.sb("qa", [P, CC, TS, H])
        qp = s.sb("qp", [ROPE, TS, H])
        prod = s.sb("prod", [P, CC + 1, TS, H])
        smx = s.sb("smx", [P, NS])
        mrow = s.sb("mrow", [NS, 1])
        mdiag = s.sb("mdiag", [NS, NS])
        sprob = s.sb("sprob", [P, TS, NPG, H])
        pnew = s.sb("pnew", [P, TS, H])
        part = s.sb("part", [P, TS, H])
        rec = s.sb("rec", [P, TS, H])
        add = s.sb("add", [P, CC, TS, H])
        zeroed = s.sem("zeroed")
        masked = s.sem("masked")
        c_turned = s.sem("c_turned")
        c_ready = s.sem("c_ready")
        s_ready = s.sem("s_ready")
        s_read = s.sem("s_read")
        mx_ready = s.sem("mx_ready")
        exped = s.sem("exped")
        p_ready = s.sem("p_ready")
        p_turned = s.sem("p_turned")
        pt_ready = s.sem("pt_ready")
        o_ready = s.sem("o_ready")
        o_read = s.sem("o_read")
        link = s.sem("link")
        page_list = s.sem("page_list")
        pages_landed = [s.sem(f"pages_landed{b}") for b in range(2)]
        scored = s.sem("scored")
        q_ready = s.sem("q_ready")
        prod_ready = s.sem("prod_ready")
        new_ready = s.sem("new_ready")
        smx_ready = s.sem("smx_ready")
        mx_turned = s.sem("mx_turned")
        diag_ready = s.sem("diag_ready")
        spread = s.sem("spread")
        shifted = s.sem("shifted")
        sexped = s.sem("sexped")
        part_ready = s.sem("part_ready")
        sum_ready = s.sem("sum_ready")
        weighed = s.sem("weighed")
        sscore = s.sb("sscore", [P, TS, NPG, H])
        score_read = s.sem("score_read")
        UNR = 4

        def fetch(eng, n, second):
            b = n % 2
            if second:
                if n >= 2:
                    eng.wait_ge(weighed, n - 1)
                else:
                    eng.wait_ge(scored, TS - 1 + n)
            elif n >= 2:
                eng.wait_ge(scored, n - 1)
            src, w = (a["cache_lat"], KVL) if second else (a["cache_t"], KVL + PAGE)
            with eng.Fori(0, NPG // UNR) as p:
                page = [eng.value_load(pages[0:1, bass.ds(UNR * p + (NPG * n + j), 1)], min_val=0, max_val=POOL_PAGES - 1)
                        for j in range(UNR)]
                for j in range(UNR):
                    eng.dma_start(ct[:, b, bass.ds(UNR * p + j, 1), 0:w].rearrange("k o f -> k (o f)"),
                                  src[bass.ds(page[j], 1)].rearrange("o k f -> (o k) f")).then_inc(pages_landed[b], 16)

        with s.block() as block:
            @block.gpsimd
            def _(pool):
                pool.memset(mask[:], 0.0).then_inc(zeroed, 1)
                pool.wait_ge(zeroed, 1)
                pool.affine_select(out=mask[:, 384:512], in_=mask[:, 384:512], compare_op=ALU.is_ge, fill=NEG, base=0,
                                   pattern=[[-1, P]], channel_multiplier=1).then_inc(masked, 1)

            @block.sync
            def _(sp):
                sp.dma_start(pages[:], a["page_table"]).then_inc(page_list, 16)
                sp.wait_ge(page_list, 16)
                for second in (False, True):
                    for n in range(0, TS, 2):
                        fetch(sp, n, second)

            @block.tensor
            def _(pe):
                def score_sequence(n):
                    b = n % 2
                    pe.wait_ge(pages_landed[b], 16 * NPG * (n // 2 + 1))
                    if n:
                        pe.wait_ge(score_read, n)
                    pe.wait_ge(pt_ready, n // 2 + 1)
                    for p in range(NPG):
                        o = k.ps[:, 4, p * H:(p + 1) * H]
                        for c in range(CC):
                            pe.matmul(o, ct[:, b, p, c * PAGE:(c + 1) * PAGE], qa[:, c, n, :], start=(c == 0), stop=False)
                        mm = pe.matmul(o, ct[0:ROPE, b, p, KVL:KVL + PAGE], qp[:, n, :], start=False, stop=True)
                    mm.then_inc(scored, 1)

                for c in range(CC):
                    for t in range(NCH):
                        mm = pe.transpose(k.ps[:, 4 + c, t * P:(t + 1) * P], ckv[:, c, t * P:(t + 1) * P], k.ident[:])
                mm.then_inc(c_turned, 1)
                for qb in range(NCH):
                    w = (qb + 1) * P
                    qs = slice(qb * P, w)
                    if qb:
                        pe.wait_ge(o_read, qb)
                    for h in range(H):
                        o = k.ps[:, h, 0:w]
                        for c in range(CC):
                            pe.matmul(o, qabs[:, h, c, qs], ckv[:, c, 0:w], start=(c == 0), stop=False)
                        mm = pe.matmul(o, qpe[:, h, qs], kpe[:, 0:w], start=False, stop=True)
                    mm.then_inc(s_ready, 1)
                    pe.wait_ge(p_ready, qb + 1)
                    pe.wait_ge(c_ready, 1)
                    if qb:
                        pe.wait_ge(pt_ready, qb)
                        pe.wait_ge(score_read, 2 * qb)
                    for h in range(H):
                        for kb in range(qb + 1):
                            mm = pe.transpose(k.ps[:, 4 + h, kb * P:(kb + 1) * P], prob[:, h, kb * P:(kb + 1) * P], k.ident[:])
                    mm.then_inc(p_turned, 1)
                    pe.wait_ge(pt_ready, qb + 1)
                    for h in range(H):
                        for c in range(CC):
                            for kb in range(qb + 1):
                                mm = pe.matmul(k.ps[:, h, c * P:(c + 1) * P], ctok[:, kb, c * P:(c + 1) * P],
                                               pt[:, h, kb * P:(kb + 1) * P], start=(kb == 0), stop=(kb == qb))
                    mm.then_inc(o_ready, 1)
                    if qb == 0:
                        pe.wait_ge(q_ready, 1)
                    score_sequence(2 * qb)
                    score_sequence(2 * qb + 1)
                pe.wait_ge(o_read, NCH)
                pe.wait_ge(prod_ready, 1)
                for c in range(CC):
                    pe.matmul(k.ps[:, 0, 0:NS], k.ones[:], prod[:, c].rearrange("p n h -> p (n h)"),
                              start=(c == 0), stop=False)
                pe.matmul(k.ps[:, 0, 0:NS], k.ones[0:ROPE, :], prod[0:ROPE, CC].rearrange("p n h -> p (n h)"),
                          start=False, stop=True).then_inc(new_ready, 1)
                pe.wait_ge(smx_ready, 1)
                pe.transpose(k.ps[0:NS, 1, 0:P], smx[:], k.ident[:]).then_inc(mx_turned, 1)
                pe.wait_ge(diag_ready, 1)
                pe.matmul(k.ps[:, 2, 0:NS], k.ones[0:NS, :], mdiag[:], start=True, stop=True).then_inc(spread, 1)
                pe.wait_ge(part_ready, 1)
                pe.matmul(k.ps[:, 3, 0:NS], k.ones[:], part[:].rearrange("p n h -> p (n h)"), start=True, stop=True
                          ).then_inc(sum_ready, 1)
                pe.wait_ge(score_read, TS)
                for n in range(TS):
                    b = n % 2
                    pe.wait_ge(pages_landed[b], 16 * NPG * (TS // 2 + n // 2 + 1))
                    for c in range(CC):
                        at = (n * CC + c) * H
                        for p in range(NPG):
                            mm = pe.matmul(k.ps[:, 5, at:at + H], ct[:, b, p, c * P:(c + 1) * P], sprob[:, n, p, :],
                                           start=(p == 0), stop=(p == NPG - 1))
                    mm.then_inc(weighed, 1)

            @block.vector
            def _(v):
                chain = Chain(v, link)

                def take_scores(n):
                    v.wait_ge(scored, n + 1)
                    v.tensor_copy(sscore[:, n].rearrange("p g h -> p (g h)"), k.ps[:, 4, 0:NPG * H]).then_inc(score_read, 1)

                v.wait_ge(c_turned, 1)
                v.tensor_copy(ctok[:].rearrange("t n (c f) -> t c n f", c=CC),
                              k.ps[:, 4:6, :].rearrange("t c (n f) -> t c n f", n=NCH)).then_inc(c_ready, 1)
                v.tensor_copy(qa[:].rearrange("p c n h -> p c h n"),
                              qabs[:].rearrange("p h c t -> p c h t")[:, :, :, TP:T])
                v.tensor_copy(qp[:].rearrange("p n h -> p h n"), qpe[:, :, TP:T]).then_inc(q_ready, 1)
                v.wait_ge(q_ready, 1)
                for c in range(CC):
                    v.tensor_tensor(prod[:, c], qa[:, c], bc(ckv[:, c, TP:T], 2, H), ALU.mult)
                v.tensor_tensor(prod[0:ROPE, CC], qp[:], bc(kpe[:, TP:T], 2, H), ALU.mult).then_inc(prod_ready, 1)
                v.wait_ge(masked, 1)
                for qb in range(NCH):
                    w = (qb + 1) * P
                    v.wait_ge(s_ready, qb + 1)
                    v.wait_ge(c_ready, 1)
                    v.tensor_tensor(sc[:, :, 0:w], k.ps[:, 0:H, 0:w], bc(mask[:, 512 - w:512], 1, H), ALU.add
                                    ).then_inc(s_read, 1)
                    v.wait_ge(s_read, qb + 1)
                    chain(v.tensor_reduce(mx[:], sc[:, :, 0:w], AX.X, ALU.max))
                    v.tensor_scalar(mx[:], mx[:], -SCALE, None, ALU.mult).then_inc(mx_ready, 1)
                    v.wait_ge(exped, qb + 1)
                    chain(v.reciprocal(total[:], total[:]))
                    v.tensor_tensor(prob[:, :, 0:w], prob[:, :, 0:w], bc(total[:], 2, w), ALU.mult).then_inc(p_ready, 1)
                    v.wait_ge(p_turned, qb + 1)
                    v.tensor_copy(pt[:, :, 0:w], k.ps[:, 4:4 + H, 0:w]).then_inc(pt_ready, 1)
                    v.wait_ge(o_ready, qb + 1)
                    v.tensor_copy(olat[:, :, :, qb * P:(qb + 1) * P],
                                  k.ps[:, 0:H, 0:CC * P].rearrange("p h (c q) -> p h c q", c=CC)).then_inc(o_read, 1)
                    take_scores(2 * qb)
                    take_scores(2 * qb + 1)
                v.wait_ge(score_read, TS)
                v.tensor_reduce(smx[:].rearrange("p (n h) -> p n h", n=TS), sscore[:].rearrange("p n g h -> p n h g"),
                                AX.X, ALU.max).then_inc(smx_ready, 1)
                v.wait_ge(mx_turned, 1)
                chain(v.tensor_reduce(mrow[:], k.ps[0:NS, 1, 0:P], AX.X, ALU.max))
                v.tensor_scalar(mdiag[:], k.ident[0:NS, 0:NS], mrow[:], None, ALU.mult).then_inc(diag_ready, 1)
                v.wait_ge(spread, 1)
                v.wait_ge(new_ready, 1)
                chain(v.tensor_copy(part[:].rearrange("p n h -> p (n h)"), k.ps[:, 0, 0:NS]))
                chain(v.tensor_tensor(smx[:], part[:].rearrange("p n h -> p (n h)"), k.ps[:, 2, 0:NS], ALU.max))
                m = smx[:].rearrange("p (n h) -> p n h", n=TS)
                v.tensor_tensor(pnew[:], part[:], m, ALU.subtract)
                v.tensor_tensor(sprob[:], sscore[:], bc(m, 2, NPG), ALU.subtract).then_inc(shifted, 1)
                v.wait_ge(sexped, 2)
                v.tensor_reduce(part[:], sprob[:].rearrange("p n g h -> p n h g"), AX.X, ALU.add).then_inc(part_ready, 1)
                v.wait_ge(sum_ready, 1)
                chain(v.tensor_tensor(rec[:], pnew[:], k.ps[:, 3, 0:NS].rearrange("p (n h) -> p n h", n=TS), ALU.add))
                chain(v.reciprocal(rec[:], rec[:]))
                for c in range(CC):
                    ins = v.tensor_tensor(add[:, c], pnew[:], bc(ckv[:, c, TP:T], 2, H), ALU.mult)
                chain(ins)
                v.wait_ge(weighed, TS)
                chain(v.tensor_tensor(add[:], add[:], k.ps[:, 5, 0:NS * CC].rearrange("p (n c h) -> p c n h", c=CC, h=H), ALU.add))
                v.tensor_tensor(olat[:].rearrange("p h c t -> p c t h")[:, :, TP:T, :], add[:], bc(rec[:], 1, CC), ALU.mult)

            @block.scalar
            def _(act):
                act.wait_ge(page_list, 16)
                fetch(act, 1, False)
                for qb in range(NCH):
                    w = (qb + 1) * P
                    act.wait_ge(mx_ready, qb + 1)
                    if qb:
                        act.wait_ge(p_turned, qb)
                    for h in range(H):
                        ins = act.activation(prob[:, h, 0:w], sc[:, h, 0:w], ACT.Exp, bias=mx[:, h:h + 1], scale=SCALE,
                                             accum_out=total[:, h:h + 1])
                    ins.then_inc(exped, 1)
                    if qb < NCH - 1:
                        fetch(act, 2 * qb + 3, False)
                fetch(act, 1, True)
                act.wait_ge(shifted, 1)
                act.activation(sprob[:], sprob[:], ACT.Exp, scale=SCALE).then_inc(sexped, 1)
                act.activation(pnew[:], pnew[:], ACT.Exp, scale=SCALE).then_inc(sexped, 1)
                for n in range(3, TS, 2):
                    fetch(act, n, True)


def latent_values(nc, k, a, olat, cat):
    with Stage(nc, "lv") as s:
        w = s.sb("w", [P, H, CC, P])
        landed = s.sem("landed")
        ready = s.sem("ready")
        with s.block() as block:
            @block.sync
            def _(sp):
                sp.dma_start(w[:], a["w_uv"]).then_inc(landed, 16)

            @block.tensor
            def _(pe):
                pe.wait_ge(landed, 16)
                for h in range(H):
                    for b in range(2):
                        for c in range(CC):
                            mm = pe.matmul(k.ps[:, 2 * h + b, 0:TH], w[:, h, c], olat[:, h, c, b * TH:(b + 1) * TH],
                                           start=(c == 0), stop=(c == CC - 1))
                    mm.then_inc(ready, 1)

            @block.vector
            def _(v):
                for h in range(H):
                    v.wait_ge(ready, h + 1)
                    v.tensor_copy(halves(cat[:, H + h]), k.ps[:, 2 * h:2 * h + 2, 0:TH])


def mixer(nc, k, a, r):
    with Stage(nc, "mixer") as s:
        cat = s.sb("cat", [P, 2 * H, T])
        proj = s.sb("proj", [P, 18, T])
        linear(nc, k, "mix_in", a["w_mix"], k.x, proj, 18, KC)
        with Stage(nc, "hg") as t:
            vt = t.sb("vt", [P, NCH, H * P])
            vs = t.sb("vs", [TS, H * P])
            mix_values(nc, k, a, vt, vs)
            recurrence(nc, k, a, proj, vt, vs, cat)
        with Stage(nc, "mla") as t:
            ckv = t.sb("ckv", [P, CC, T])
            kpe = t.sb("kpe", [ROPE, T])
            qabs = t.sb("qabs", [P, H, CC, T])
            qpe = t.sb("qpe", [ROPE, H, T])
            latent_queries(nc, k, a, proj, qabs, qpe, kpe, ckv)
            olat = proj[:, 0:H * CC].rearrange("p (h c) t -> p h c t", h=H)
            attention(nc, k, a, qabs, qpe, kpe, ckv, olat)
            latent_values(nc, k, a, olat, cat)
        linear(nc, k, "mix_out", a["w_mix_out"], cat, r, KC, KC)


def peer_retrieve(nc, k, a, layer, values, ranks):
    with Stage(nc, f"retrieve{layer}") as s:
        w = a["peer_wq"][layer]
        slab = s.sb("slab", [P, 2, KC, P])
        q = s.sb("q", [P, 2, T])
        keys = s.sb("keys", [P, HP, NK])
        rest = s.sb("rest", [TT, NT, NK])
        top = s.sb("top", [TT, NT, TOPK])
        topi = s.sb("topi", [TT, NT, TOPK], U32)
        landed = [s.sem(f"landed{b}") for b in range(2)]
        keys_landed = s.sem("keys_landed")
        slab_free = s.sem("slab_free")
        q_copied = s.sem("q_copied")
        score_free = s.sem("score_free")
        score_ready = s.sem("score_ready")
        link = s.sem("link")
        score = [k.ps[0:TT, 4 + 2 * b:6 + 2 * b, :].rearrange("t a n -> t (a n)")[:, 0:NT * NK]
                 .rearrange("t (n m) -> t n m", m=NK) for b in range(2)]
        with s.block() as block:
            @block.sync
            def _(sp):
                for b in range(2):
                    sp.dma_start(slab[:, b], w[b]).then_inc(landed[b], 16)
                sp.dma_start(keys[:], a["peer_keys"][layer]).then_inc(keys_landed, 16)
                with sp.Fori(0, HP // 2 - 1) as i:
                    for b in range(2):
                        wait(sp, slab_free, 2 * i + b + 1)
                        sp.dma_start(slab[:, b], w[bass.ds(2 * i + 2 + b, 1)].rearrange("o p k m -> (o p) k m")
                                     ).then_inc(landed[b], 16)

            @block.tensor
            def _(pe):
                def project(i, b):
                    pe.wait_ge(landed[b], 16 * i + 16)
                    pe.wait_ge(q_copied, 2 * i + b + 1)
                    for h in range(2):
                        for c in range(KC):
                            mm = pe.matmul(k.ps[:, 2 * b + h, 0:TH], slab[:, b, c], k.x[:, c, h * TH:(h + 1) * TH],
                                           start=(c == 0), stop=(c == KC - 1))
                    mm.then_inc(slab_free, 1)

                def scores(i, b):
                    n = 2 * i + b
                    pe.wait_ge(q_copied, n + 3)
                    pe.wait_ge(score_free, n + 1)
                    for t in range(NT):
                        mm = pe.matmul(score[b][:, t], q[:, b, t * TT:(t + 1) * TT],
                                       keys[:, bass.ds(n, 1) if not isinstance(n, int) else slice(n, n + 1), :]
                                       .rearrange("p o n -> p (o n)"), start=True, stop=True)
                    mm.then_inc(score_ready, 1)

                pe.wait_ge(keys_landed, 16)
                project(0, 0)
                with pe.Fori(0, HP // 2 - 1) as i:
                    project(i, 1)
                    scores(i, 0)
                    project(i + 1, 0)
                    scores(i, 1)
                project(HP // 2 - 1, 1)
                scores(HP // 2 - 1, 0)
                scores(HP // 2 - 1, 1)

            @block.scalar
            def _(act):
                act.sem_inc(q_copied, 2)
                with act.Fori(0, HP // 2) as i:
                    for b in range(2):
                        act.wait_ge(slab_free, 2 * i + b + 1)
                        act.wait_ge(score_ready, 2 * i + b)
                        act.copy(halves(q[:, b]), k.ps[:, 2 * b:2 * b + 2, 0:TH]).then_inc(q_copied, 1)

            @block.vector
            def _(v):
                v.sem_inc(score_free, 2)
                with v.Fori(0, HP // 2) as i:
                    chain = Chain(v, link)
                    base = 8 * i
                    for b in range(2):
                        sc = score[b]
                        wait(v, score_ready, 2 * i + b + 1)
                        for t in range(NT):
                            ins = v.max(top[:, t, 0:8], sc[:, t])
                        chain(ins, base)
                        for t in range(NT):
                            v.max_index(topi[:, t, 0:8], top[:, t, 0:8], sc[:, t])
                            ins = v.match_replace(rest[:, t], top[:, t, 0:8], sc[:, t], NEG)
                            if t == NT - 1:
                                ins.then_inc(score_free, 1)
                        wait(v, score_free, 2 * i + b + 3)
                        for t in range(NT):
                            ins = v.max(top[:, t, 8:16], rest[:, t])
                        chain(ins, base)
                        for t in range(NT):
                            ins = v.max_index(topi[:, t, 8:16], top[:, t, 8:16], rest[:, t])
                        chain(ins, base)
                        n = bass.ds(2 * i + b, 1)
                        v.tensor_copy(values[:, :, n, :].rearrange("t n o r -> t n (o r)"), top[:])
                        chain(v.tensor_copy(ranks[:, :, n, :].rearrange("t n o r -> t n (o r)"), topi[:]), base)
                    assert chain.n == 8


def peer_gates(nc, k, a, layer, values, ranks):
    with Stage(nc, f"gates{layer}") as s:
        cand = s.sb("cand", [TT, PH, NCAND])
        rest = s.sb("rest", [TT, PH, NCAND])
        best = s.sb("best", [TT, PH, TOPK])
        expd = s.sb("expd", [TT, PH, TOPK])
        pos = s.sb("pos", [TT, PH, TOPK], U32)
        part = s.sb("part", [TT, PH, TOPK], U32)
        shift = s.sb("shift", [TT, 2, PH, TOPK], U32)
        is_b = s.sb("is_b", [TT, PH, TOPK])
        ra = s.sb("ra", [TT, PH, TOPK])
        rb = s.sb("rb", [TT, PH, TOPK])
        pick = s.sb("pick", [TT, 2, PH * TOPK, TOPK])
        ijg = s.sb("ijg", [TT, 3, PH * TOPK])
        total = s.sb("total", [TT, PH])
        cols = s.sb("cols", [P, 3, TT])
        onej = s.sb("onej", [P, 2, 4, NK])
        onei = s.sb("onei", [P, 2, 4, NK])
        g = s.sb("g", [P, NK, TT])
        link = s.sem("link")
        centred = s.sem("centred")
        exped = s.sem("exped")
        ijg_ready = s.sem("ijg_ready")
        turned = s.sem("turned")
        one_ready = s.sem("one_ready")
        g_ready = s.sem("g_ready")
        g_free = s.sem("g_free")
        g_stored = s.sem("g_stored")
        turn = k.ps[:, 2, 0:3 * TT].rearrange("p (c t) -> p c t", c=3)
        iota16 = k.iota[0:TT, 0:TOPK]
        groups = TT // 8
        with s.block() as block:
            @block.vector
            def _(v):
                with v.Fori(0, NT) as t:
                    chain = Chain(v, link)
                    base = 15 * t
                    tile = bass.ds(t, 1)
                    val = values[:, tile].rearrange("t o (h p) r -> t (o h) p r", p=2)
                    rank = ranks[:, tile].rearrange("t o (h p) r -> t (o h) p r", p=2)
                    v.tensor_tensor(cand[:, :, 0:CANDA * 16].rearrange("t h (x y) -> t h x y", y=16),
                                    bc(val[:, :, 0, 0:CANDA], 3, 16), bc(val[:, :, 1, :], 2, CANDA), ALU.add)
                    chain(v.tensor_tensor(cand[:, :, CANDA * 16:NCAND].rearrange("t h (x y) -> t h x y", y=4),
                                          bc(val[:, :, 0, CANDA:16], 3, 4), bc(val[:, :, 1, 0:4], 2, CANDB), ALU.add), base)
                    for h in range(PH):
                        ins = v.max(best[:, h, 0:8], cand[:, h])
                    chain(ins, base)
                    for h in range(PH):
                        v.max_index(pos[:, h, 0:8], best[:, h, 0:8], cand[:, h])
                        ins = v.match_replace(rest[:, h], best[:, h, 0:8], cand[:, h], NEG)
                    chain(ins, base)
                    for h in range(PH):
                        ins = v.max(best[:, h, 8:16], rest[:, h])
                    chain(ins, base)
                    for h in range(PH):
                        ins = v.max_index(pos[:, h, 8:16], best[:, h, 8:16], rest[:, h])
                    chain(ins, base)
                    v.tensor_tensor(expd[:], best[:], bc(best[:, :, 0], 2, TOPK), ALU.subtract).then_inc(centred, 1)
                    v.tensor_single_scalar(shift[:, 0], pos[:], 4, ALU.logical_shift_right)
                    v.tensor_single_scalar(shift[:, 1], pos[:], 2, ALU.logical_shift_right)
                    v.tensor_single_scalar(is_b[:], pos[:], float(CANDA * 16), ALU.is_ge)
                    chain(v.tensor_single_scalar(part[:], pos[:], 3, ALU.bitwise_and), base)
                    v.tensor_tensor(ra[:], shift[:, 1], shift[:, 0], ALU.subtract)
                    chain(v.tensor_single_scalar(pos[:], pos[:], 15, ALU.bitwise_and), base)
                    v.tensor_scalar(ra[:], ra[:], -12.0, None, ALU.add)
                    chain(v.tensor_tensor(rb[:], part[:], pos[:], ALU.subtract), base)
                    v.tensor_tensor(ra[:], ra[:], is_b[:], ALU.mult)
                    chain(v.tensor_tensor(rb[:], rb[:], is_b[:], ALU.mult), base)
                    v.tensor_tensor(ra[:], ra[:], shift[:, 0], ALU.add)
                    chain(v.tensor_tensor(rb[:], rb[:], pos[:], ALU.add), base)
                    for p, r in enumerate((ra, rb)):
                        ins = v.tensor_tensor(pick[:, p], bc(r[:].rearrange("t h r -> t (h r)"), 2, TOPK),
                                              bc(iota16, 1, PH * TOPK), ALU.is_equal)
                    chain(ins, base)
                    for p in range(2):
                        ins = v.tensor_tensor(pick[:, p].rearrange("t (h r) x -> t h r x", h=PH),
                                              pick[:, p].rearrange("t (h r) x -> t h r x", h=PH),
                                              bc(rank[:, :, p, :], 2, TOPK), ALU.mult)
                    chain(ins, base)
                    for p in range(2):
                        v.tensor_reduce(ijg[:, p], pick[:, p], AX.X, ALU.add)
                    v.wait_ge(exped, t + 1)
                    chain(v.tensor_reduce(total[:], expd[:], AX.X, ALU.add), base)
                    chain(v.reciprocal(total[:], total[:]), base)
                    v.tensor_tensor(ijg[:, 2].rearrange("t (h r) -> t h r", h=PH), expd[:], bc(total[:], 2, TOPK),
                                    ALU.mult).then_inc(ijg_ready, 1)
                    v.wait_ge(turned, t + 1)
                    v.wait_ge(g_ready, 2 * groups * t + 2)
                    chain(v.tensor_copy(cols[:], turn), base)
                    with v.Fori(0, groups) as u:
                        for b in range(2):
                            v.wait_ge(g_ready, 2 * groups * t + 2 * u + b + 1)
                            for n in range(4):
                                tok = bass.ds(8 * u + 4 * b + n, 1)
                                v.tensor_scalar(onej[:, b, n], k.iota[:], cols[:, 1, tok], None, ALU.is_equal)
                                ins = v.tensor_scalar(onei[:, b, n], k.iota[:], cols[:, 0, tok], cols[:, 2, tok],
                                                      ALU.is_equal, ALU.mult)
                            ins.then_inc(one_ready, 1)
                    assert chain.n == 15

            @block.tensor
            def _(pe):
                pe.sem_inc(g_ready, 2)
                with pe.Fori(0, NT) as t:
                    pe.wait_ge(ijg_ready, t + 1)
                    for c in range(3):
                        mm = pe.transpose(turn[:, c], ijg[:, c], k.ident[0:TT, 0:TT])
                    mm.then_inc(turned, 1)
                    with pe.Fori(0, groups) as u:
                        for b in range(2):
                            n = 2 * groups * t + 2 * u + b
                            pe.wait_ge(one_ready, n + 1)
                            pe.wait_ge(g_free, n + 1)
                            for m in range(4):
                                mm = pe.matmul(k.ps[:, b, m * NK:(m + 1) * NK], onej[:, b, m], onei[:, b, m],
                                               start=True, stop=True)
                            mm.then_inc(g_ready, 1)

            @block.scalar
            def _(act):
                act.sem_inc(g_free, 2)
                with act.Fori(0, NT) as t:
                    act.wait_ge(centred, t + 1)
                    act.activation(expd[:], expd[:], ACT.Exp).then_inc(exped, 1)
                    act.wait_ge(g_stored, 16 * t)
                    with act.Fori(0, groups) as u:
                        for b in range(2):
                            act.wait_ge(g_ready, 2 * groups * t + 2 * u + b + 3)
                            act.activation(g[:, :, bass.ds(8 * u + 4 * b, 4)],
                                           k.ps[:, b].rearrange("j (t i) -> j i t", t=4), ACT.Copy).then_inc(g_free, 1)

            @block.sync
            def _(sp):
                for t in range(NT):
                    sp.wait_ge(g_free, 2 * groups * (t + 1) + 2)
                    sp.dma_start(a["gates"][:, :, t * TT:(t + 1) * TT].rearrange("i j t -> j i t"), g[:]
                                 ).then_inc(g_stored, 16)
                sp.wait_ge(g_stored, 16 * NT)


def peer_experts(nc, k, a, layer, r):
    with Stage(nc, f"experts{layer}") as s:
        xh = s.sb("xh", [P, KC, T], F32R)
        xl = s.sb("xl", [P, KC, T], F32R)
        u = s.sb("u", [P, 2, KC, P])
        uh = s.sb("uh", [P, 2, KC, P], F32R)
        ul = s.sb("ul", [P, 2, KC, P], F32R)
        w = s.sb("v", [P, 2, D])
        wh = s.sb("vh", [P, GB, D], F32R)
        wl = s.sb("vl", [P, GB, D], F32R)
        g = s.sb("g", [P, 2, T])
        act_out = s.sb("act", [P, 2, T])
        gated = s.sb("gated", [P, T])
        gh = s.sb("gh", [P, 2, GB, T], F32R)
        gl = s.sb("gl", [P, 2, GB, T], F32R)
        u_landed = [s.sem(f"u_landed{b}") for b in range(2)]
        g_landed = [s.sem(f"g_landed{b}") for b in range(2)]
        v_landed = [s.sem(f"v_landed{b}") for b in range(2)]
        x_split = s.sem("x_split")
        u_high = s.sem("u_high")
        u_split = s.sem("u_split")
        v_high = s.sem("v_high")
        v_split = s.sem("v_split")
        h_ready = s.sem("h_ready")
        gelu_ready = s.sem("gelu_ready")
        gated_ready = s.sem("gated_ready")
        a_high = s.sem("a_high")
        a_ready = s.sem("a_ready")
        y_ready = s.sem("y_ready")
        y_free = s.sem("y_free")
        with s.block() as block:
            @block.sync
            def _(sp):
                def load_u(n, b):
                    sp.dma_start(u[:, b % 2], a["peer_u"][bass.ds(layer * NK + n, 1)].rearrange("o p k e -> (o p) k e")
                                 ).then_inc(u_landed[b % 2], 16)

                def load_g(n, b):
                    sp.dma_start(g[:, b % 2], a["gates"][bass.ds(n, 1)].rearrange("o j t -> (o j) t")
                                 ).then_inc(g_landed[b % 2], 16)

                def load_v(n, b):
                    sp.dma_start(w[:, b % 2], a["peer_v"][bass.ds(layer * NK + n, 1)].rearrange("o e d -> (o e) d")
                                 ).then_inc(v_landed[b % 2], 16)

                for b in range(2):
                    load_u(b, b)
                    load_g(b, b)
                    load_v(b, b)

                def next_ug(n, b):
                    wait(sp, u_split, n + 1)
                    load_u(n + 2, b)
                    wait(sp, gated_ready, n + 1)
                    load_g(n + 2, b)

                def next_v(n, b):
                    wait(sp, v_split, n - 3)
                    load_v(n - 2, b)

                for n in range(GB):
                    next_ug(n, n % 2)
                with sp.Fori(GB // 2, NK // 2 - 1) as i:
                    for b in range(2):
                        next_ug(2 * i + b, b)
                        next_v(2 * i + b, b)
                for n in range(NK - 2, NK + 2):
                    next_v(n, n % 2)

            @block.tensor
            def _(pe):
                def hidden(grp):
                    for b in range(GB):
                        n = GB * grp + b
                        pe.wait_ge(u_split, n + 1)
                        pe.wait_ge(gelu_ready, n + 1)
                        for h in range(2):
                            o = k.ps[:, 2 * (b % 2) + h, 0:TH]
                            t = slice(h * TH, (h + 1) * TH)
                            for c in range(KC):
                                pe.matmul(o, ul[:, b % 2, c], xh[:, c, t], start=(c == 0), stop=False)
                                pe.matmul(o, uh[:, b % 2, c], xl[:, c, t], start=False, stop=False)
                                mm = pe.matmul(o, uh[:, b % 2, c], xh[:, c, t], start=False, stop=(c == KC - 1))
                        mm.then_inc(h_ready, 1)

                def output(grp, par):
                    pe.wait_ge(v_split, GB * grp + GB)
                    pe.wait_ge(a_ready, GB * grp + GB)
                    for c in range(KC):
                        pe.wait_ge(y_free, KC * grp + c + 1)
                        for h in range(2):
                            o = k.ps[:, 4 + 2 * (c % 2) + h, 0:TH]
                            t = slice(h * TH, (h + 1) * TH)
                            f = slice(c * P, (c + 1) * P)
                            for b in range(GB):
                                pe.matmul(o, wl[:, b, f], gh[:, par, b, t], start=(b == 0), stop=False)
                                pe.matmul(o, wh[:, b, f], gl[:, par, b, t], start=False, stop=False)
                                mm = pe.matmul(o, wh[:, b, f], gh[:, par, b, t], start=False, stop=(b == GB - 1))
                        mm.then_inc(y_ready, 1)

                pe.wait_ge(x_split, 2)
                hidden(0)
                with pe.Fori(0, NG // 2 - 1) as i:
                    hidden(2 * i + 1)
                    output(2 * i, 0)
                    hidden(2 * i + 2)
                    output(2 * i + 1, 1)
                hidden(NG - 1)
                output(NG - 2, 0)
                output(NG - 1, 1)

            @block.scalar
            def _(act):
                def split_u(n, b):
                    act.wait_ge(u_landed[b % 2], (n - b % 2) * 8 + 16)
                    if not isinstance(n, int) or n > 1:
                        act.wait_ge(h_ready, n - 1)
                    act.activation(uh[:, b % 2], u[:, b % 2], ACT.Copy).then_inc(u_high, 1)

                def split_v(n, b):
                    act.wait_ge(v_landed[b % 2], (n - b % 2) * 8 + 16)
                    act.activation(wh[:, b], w[:, b % 2], ACT.Copy).then_inc(v_high, 1)

                def gelu(n, b):
                    act.wait_ge(h_ready, n + 1)
                    if not isinstance(n, int) or n > 1:
                        act.wait_ge(gated_ready, n - 1)
                    act.activation(halves(act_out[:, b % 2]), k.ps[:, 2 * (b % 2):2 * (b % 2) + 2, 0:TH], ACT.Gelu
                                   ).then_inc(gelu_ready, 1)

                def group(grp, last):
                    for b in range(GB):
                        n = GB * grp + b
                        if b == 0:
                            act.wait_ge(y_ready, KC * (grp - 1))
                        if not (last and b == GB - 1):
                            split_u(n + 1, b + 1)
                        split_v(n - GB, b)
                        gelu(n, b)

                act.sem_inc(gelu_ready, 2)
                split_u(0, 0)
                for b in range(GB):
                    split_u(b + 1, b + 1)
                    gelu(b, b)
                with act.Fori(0, NG // 2 - 1) as i:
                    group(2 * i + 1, False)
                    group(2 * i + 2, False)
                group(NG - 1, True)
                act.wait_ge(y_ready, KC * (NG - 1))
                for b in range(GB):
                    split_v(NK - GB + b, b)

            @block.vector
            def _(v):
                def split_u(n, b):
                    v.wait_ge(u_high, n + 1)
                    v.tensor_tensor(ul[:, b % 2], u[:, b % 2], uh[:, b % 2].bitcast(F32), ALU.subtract
                                    ).then_inc(u_split, 1)

                def split_v(n, b):
                    v.wait_ge(v_high, n + 1)
                    v.tensor_tensor(wl[:, b], w[:, b % 2], wh[:, b].bitcast(F32), ALU.subtract).then_inc(v_split, 1)

                def gate(n, b, par):
                    v.wait_ge(gelu_ready, n + 3)
                    if not isinstance(n, int) or n > 0:
                        v.wait_ge(a_ready, n)
                    v.wait_ge(g_landed[b % 2], (n - b % 2) * 8 + 16)
                    v.tensor_tensor(gated[:], act_out[:, b % 2], g[:, b % 2], ALU.mult).then_inc(gated_ready, 1)
                    v.wait_ge(gated_ready, n + 1)
                    v.tensor_copy(gh[:, par, b], gated[:]).then_inc(a_high, 1)
                    v.wait_ge(a_high, n + 1)
                    v.tensor_tensor(gl[:, par, b], gated[:], gh[:, par, b].bitcast(F32), ALU.subtract
                                    ).then_inc(a_ready, 1)

                def collect(grp):
                    for c in range(KC):
                        v.wait_ge(y_ready, KC * grp + c + 1)
                        rc = halves(r[:, c])
                        v.tensor_tensor(rc, rc, k.ps[:, 4 + 2 * (c % 2):6 + 2 * (c % 2), 0:TH], ALU.add
                                        ).then_inc(y_free, 1)

                def group(grp, par, last):
                    for b in range(GB):
                        n = GB * grp + b
                        if not (last and b == GB - 1):
                            split_u(n + 1, b + 1)
                        split_v(n - GB, b)
                        gate(n, b, par)
                    collect(grp - 1)

                v.sem_inc(y_free, 2)
                v.tensor_copy(xh[:], k.x[:]).then_inc(x_split, 1)
                v.tensor_scalar(r[:], k.x[:], ALPHA, None, ALU.mult)
                v.wait_ge(x_split, 1)
                v.tensor_tensor(xl[:], k.x[:], xh[:].bitcast(F32), ALU.subtract).then_inc(x_split, 1)
                split_u(0, 0)
                for b in range(GB):
                    split_u(b + 1, b + 1)
                    gate(b, b, 0)
                with v.Fori(0, NG // 2 - 1) as i:
                    group(2 * i + 1, 1, False)
                    group(2 * i + 2, 0, False)
                group(NG - 1, 1, True)
                for b in range(GB):
                    split_v(NK - GB + b, b)
                collect(NG - 1)


def peer_layer(nc, k, a, layer):
    with Stage(nc, f"peer{layer}") as s:
        values = s.sb("values", [TT, NT, HP, TOPK])
        ranks = s.sb("ranks", [TT, NT, HP, TOPK])
        peer_retrieve(nc, k, a, layer, values, ranks)
        peer_gates(nc, k, a, layer, values, ranks)
    with Stage(nc, f"peer_out{layer}") as s:
        r = s.sb("r", [P, KC, T])
        peer_experts(nc, k, a, layer, r)
        layer_norm(nc, k, f"ln{layer}1", r, f"ln_g{layer}1", f"ln_b{layer}1", k.x, ACT.Identity)


def conv_module(nc, k, a, r):
    LEFT = CW - 1
    with Stage(nc, "conv") as s:
        y = s.sb("y", [P, KC, T])
        with Stage(nc, "convin") as t:
            h = t.sb("h", [P, 2 * KC, T])
            linear(nc, k, "pw1", a["w_pw1"], k.x, h, 2 * KC, KC)
            ext = t.sb("ext", [P, KC, LEFT + TP])
            exts = t.sb("exts", [P, KC, TS, CW])
            old = t.sb("old", [P, KC, TS, LEFT])
            tails = t.sb("tails", [P, KC, TS, LEFT])
            prod = t.sb("prod", [P, 2, TS, CW])
            landed = t.sem("landed")
            sig = t.sem("sig")
            glu = t.sem("glu")
            done = t.sem("done")
            tails_ready = t.sem("tails_ready")
            link = t.sem("link")
            stored = t.sem("stored")
            with t.block() as block:
                @block.sync
                def _(sp):
                    sp.dma_start(old[:], a["state_conv"]).then_inc(landed, 16)
                    sp.wait_ge(tails_ready, 1)
                    sp.dma_start(a["new_conv_s"], tails[:]).then_inc(stored, 16)
                    sp.dma_start(a["new_conv_p"], ext[:, :, TP:TP + LEFT]).then_inc(stored, 16)
                    sp.wait_ge(stored, 32)

                @block.scalar
                def _(act):
                    for c in range(KC):
                        act.activation(h[:, KC + c], h[:, KC + c], ACT.Sigmoid, bias=k.col("b_pw1", KC + c)).then_inc(sig, 1)

                @block.vector
                def _(v):
                    chain = Chain(v, link)
                    v.memset(ext[:, :, 0:LEFT], 0.0)
                    v.wait_ge(landed, 16)
                    v.tensor_copy(exts[:, :, :, 0:LEFT], old[:])
                    for c in range(KC):
                        v.wait_ge(sig, c + 1)
                        b = k.col("b_pw1", c)
                        v.scalar_tensor_tensor(ext[:, c, LEFT:LEFT + TP], h[:, c, 0:TP], b, h[:, KC + c, 0:TP], ALU.add, ALU.mult)
                        ins = v.scalar_tensor_tensor(exts[:, c, :, LEFT], h[:, c, TP:T], b, h[:, KC + c, TP:T], ALU.add, ALU.mult)
                        ins.then_inc(glu, 1)
                    v.wait_ge(glu, KC)
                    v.tensor_copy(tails[:], exts[:, :, :, 1:CW]).then_inc(tails_ready, 1)
                    for c in range(KC):
                        w = k.vec[:, VEC["w_dw"] + c * CW:VEC["w_dw"] + (c + 1) * CW]
                        ins = v.tensor_tensor(prod[:, c % 2], exts[:, c], bc(w, 1, TS), ALU.mult)
                        chain(ins)
                        chain(v.tensor_reduce(y[:, c, TP:T], prod[:, c % 2], AX.X, ALU.add))
                    for c in range(0, KC, 2):
                        for j in range(CW):
                            for d in (c, c + 1):
                                w = k.col("w_dw", d * CW + j)
                                o = y[:, d, 0:TP]
                                x = ext[:, d, j:j + TP]
                                if j == 0:
                                    v.tensor_scalar(o, x, w, k.col("b_dw", d), ALU.mult, ALU.add).then_inc(done, 1)
                                else:
                                    v.wait_ge(done, (c // 2) * 2 * CW + 2 * (j - 1) + d - c + 1)
                                    v.scalar_tensor_tensor(o, x, w, o, ALU.mult, ALU.add).then_inc(done, 1)
                    chain(v.tensor_tensor(y[:, :, TP:T], y[:, :, TP:T],
                                          bc(k.vec[:, VEC["b_dw"]:VEC["b_dw"] + KC], 2, TS), ALU.add))
        act_in = s.sb("act", [P, KC, T])
        layer_norm(nc, k, "cln", y, "cln_g", "cln_b", act_in, ACT.Silu)
        linear(nc, k, "pw2", a["w_pw2"], act_in, r, KC, KC)
    with Stage(nc, "pw2bias") as s, s.block() as block:
        @block.scalar
        def _(act):
            for c in range(KC):
                act.activation(r[:, c], r[:, c], ACT.Identity, bias=k.col("b_pw2", c))


def build(nc, a):
    with ExitStack() as ctx:
        k = Kept(nc, ctx)
        load_constants(nc, a, k)
        for layer, mix in enumerate((mixer, conv_module)):
            with Stage(nc, f"layer{layer}") as s:
                r = s.sb("r", [P, KC, T])
                mix(nc, k, a, r)
                residual(nc, k, f"res{layer}", r)
                layer_norm(nc, k, f"ln{layer}0", r, f"ln_g{layer}0", f"ln_b{layer}0", k.x, ACT.Identity)
            peer_layer(nc, k, a, layer)
        with Stage(nc, "store") as s:
            stored = s.sem("stored")
            with s.block() as block:
                @block.sync
                def _(sp):
                    sp.dma_start(a["y"], k.x[:]).then_inc(stored, 16)
                    sp.wait_ge(stored, 16)


_OUTS = {"y": (P, KC, T), "new_lat": (P, CC, T), "new_kpe": (ROPE, T), "new_hgrn_p": (P, H, P),
         "new_hgrn_s": (TS, P, H, P), "new_conv_p": (P, KC, CW - 1), "new_conv_s": (P, KC, TS, CW - 1)}


def _slabs(w):
    i, o = w.shape
    return w.reshape(i // P, P, o // P, P).transpose(2, 1, 0, 3)


def _rows(w):
    return w.reshape(w.shape[0] // P, P, -1).transpose(1, 0, 2)


def _layout(i):
    swap = np.r_[ROPE // 2:ROPE, 0:ROPE // 2]
    x = np.concatenate([i["x_prompt"].reshape(TP, D), i["x_sample"].reshape(TS, D)])
    w_in = i["mix_w_in"][0]
    kr = w_in[:, 2048 + QL + KVL:]
    w_mix = np.concatenate([w_in[:, 0:1024], w_in[:, 1536:2048], w_in[:, 2048:2048 + QL + KVL], kr, kr[:, swap]], axis=1)
    uq = i["mla_w_uq"][0].reshape(QL, H, P + ROPE)
    w_uq = np.concatenate([uq[:, :, :P].reshape(QL, -1), uq[:, :, P:].reshape(QL, -1), uq[:, :, P:][:, :, swap].reshape(QL, -1)], axis=1)
    ukv = i["mla_w_ukv"][0]
    half = ROPE // 2
    inv = np.float32(10000.0) ** (-np.arange(half, dtype=np.float32) / np.float32(half))
    pos = np.r_[0:TP, [PAST] * TS].astype(np.float32)
    ang = (pos[:, None] * inv[None, :]).astype(np.float32).astype(np.float64)
    cos, sin = np.cos(ang).T.astype(np.float32), np.sin(ang).T.astype(np.float32)
    s_, t_ = np.arange(P)[:, None], np.arange(P)[None, :]
    masks = [s_ == t_] + [(s_ // (2 * m) == t_ // (2 * m)) & (s_ % (2 * m) < m) & (t_ % (2 * m) >= m)
                          for m in (1 << n for n in range(LEVELS - 1))]

    lat_t = i["cache_mla_latent"][0].reshape(POOL_PAGES, PAGE, CC, P).transpose(0, 3, 2, 1).reshape(POOL_PAGES, P, KVL)
    rope_t = np.pad(i["cache_mla_krope"][0].transpose(0, 2, 1), ((0, 0), (0, P - ROPE), (0, 0)))

    def cols(w):
        return w.reshape(-1, P).T

    vec = [cols(i["ln_g"][l, j]) for l in range(2) for j in range(2)] + [cols(i["ln_b"][l, j]) for l in range(2) for j in range(2)]
    vec += [cols(i["conv_b_pw1"][0]), cols(i["conv_b_dw"][0]), cols(i["conv_ln_g"][0]), cols(i["conv_ln_b"][0]),
            cols(i["conv_b_pw2"][0]), cols(i["mla_q_norm"][0]), cols(i["mla_kv_norm"][0]), cols(i["hg_out_norm"][0]),
            cols(i["hg_lb_logits"]), i["conv_w_dw"][0].reshape(CW, KC, P).transpose(2, 1, 0).reshape(P, -1)]
    return {
        "x_t": _rows(x.T),
        "vecs": np.concatenate(vec, axis=1),
        "masks": np.stack(masks, axis=1).astype(np.uint32),
        "cos": np.concatenate([cos, cos]),
        "sin": np.concatenate([-sin, sin]),
        "w_mix": _slabs(w_mix),
        "w_val": _rows(w_in[:, 1024:1536]),
        "w_uq": _rows(w_uq),
        "w_uk": ukv[:, :, :P].transpose(2, 1, 0),
        "w_uv": ukv[:, :, P:].reshape(CC, P, H, P).transpose(1, 2, 0, 3),
        "w_mix_out": _slabs(i["mix_w_out"][0]),
        "page_table": i["page_table"].reshape(1, -1),
        "cache_t": np.concatenate([lat_t, rope_t], axis=2),
        "cache_lat": i["cache_mla_latent"][0],
        "state_hgrn": i["state_hgrn"][0].transpose(0, 2, 1, 3),
        "state_conv": i["state_conv"][0].reshape(TS, CW - 1, KC, P).transpose(3, 2, 0, 1),
        "w_pw1": _slabs(i["conv_w_pw1"][0]),
        "w_pw2": _slabs(i["conv_w_pw2"][0]),
        "peer_wq": np.stack([_slabs(w) for w in i["peer_w_q"]]),
        "peer_keys": i["peer_sub_keys"].transpose(0, 4, 2, 1, 3).reshape(2, P, HP, NK),
        "peer_u": i["peer_u"].reshape(2 * NK, P, KC, P).transpose(0, 3, 2, 1),
        "peer_v": i["peer_v"].reshape(2 * NK, P, D),
    }


def kernel(**inputs):
    import concourse.bacc as bacc
    from concourse.bass_utils import run_bass_kernel_spmd

    nc = bacc.Bacc("TRN2", target_bir_lowering=False, num_devices=1)
    arrays = {n: np.ascontiguousarray(z) for n, z in _layout({n: np.asarray(z) for n, z in inputs.items()}).items()}
    a = {n: nc.dram_tensor(n, z.shape, mybir.dt.from_np(z.dtype), kind="ExternalInput").ap() for n, z in arrays.items()}
    for n, shape in _OUTS.items():
        a[n] = nc.dram_tensor(n, shape, F32, kind="ExternalOutput").ap()
    a["gates"] = nc.dram_tensor("gates", (NK, NK, T), F32).ap()
    build(nc, a)
    o = run_bass_kernel_spmd(nc, [arrays], core_ids=[0]).results[0]
    tok = [o[n].transpose(2, 1, 0).reshape(T, -1) for n in ("y", "new_lat")] + [o["new_kpe"].T]
    prompt = [z[:TP] for z in tok]
    sample = [z[TP:].reshape(TS, 1, -1) for z in tok]
    out = (prompt[0][None], sample[0], prompt[1][None, None], prompt[2][None, None],
           o["new_hgrn_p"].transpose(1, 0, 2)[None, None],
           o["new_conv_p"].transpose(2, 1, 0).reshape(1, 1, CW - 1, D),
           sample[1][None], sample[2][None], o["new_hgrn_s"].transpose(0, 2, 1, 3)[None],
           o["new_conv_s"].transpose(2, 3, 1, 0).reshape(1, TS, CW - 1, D))
    return tuple(np.ascontiguousarray(z) for z in out)
```

```python
from contextlib import ExitStack

import concourse.bass as bass
import numpy as np
from concourse import mybir

F32 = mybir.dt.float32
F32R = mybir.dt.float32r
U32 = mybir.dt.uint32
I32 = mybir.dt.int32
ALU = mybir.AluOpType
ACT = mybir.ActivationFunctionType
AX = mybir.AxisListType

P = 128
D = 1024
KC = D // P
TP, TS = 512, 8
T = TP + TS
TH = T // 2
TT, NT = 104, 5
H = 4
CL, NCH = 128, 4
QL, KVL, ROPE = 384, 256, 64
QC, CC = QL // P, KVL // P
PAST, PAGE = 2048, 128
NPG = PAST // PAGE
POOL_PAGES = 160
CW = 31
PH = 8
NK = 128
HP = 2 * PH
TOPK = 16
CANDA, CANDB = 4, 12
NCAND = CANDA * 16 + CANDB * 4
NEG = -3.0e38
ALPHA = 4.0 ** 0.25
SCALE = float(128 + ROPE) ** -0.5
LN_EPS, RMS_EPS = 1e-5, 1e-6
LEVELS = 8
GB = 4
NG = NK // GB
SELECT, PER_TILE = 8, 20
EXTRA = SELECT
AHEAD = PER_TILE * NT + EXTRA
FRESH = (NK - AHEAD) // GB

VEC = {}
_at = 0
for _name, _n in (("ln_g00", KC), ("ln_g01", KC), ("ln_g10", KC), ("ln_g11", KC),
                  ("ln_b00", KC), ("ln_b01", KC), ("ln_b10", KC), ("ln_b11", KC),
                  ("b_pw1", 2 * KC), ("b_dw", KC), ("cln_g", KC), ("cln_b", KC), ("b_pw2", KC),
                  ("q_norm", QC), ("kv_norm", CC), ("out_norm", 1), ("lb", 3 * H), ("w_dw", CW * KC)):
    VEC[_name] = _at
    _at += _n
NVEC = _at


def bc(ap, axis, n):
    a = ap.unsqueeze(axis)
    shape = list(a.shape)
    shape[axis] = n
    return a.broadcast_to(shape)


def halves(ap):
    return ap.rearrange("p (a t) -> p a t", a=2)


def wait(eng, sem, value):
    eng.wait_ge(sem, value)
    if not isinstance(value, int):
        eng.nop(nofuse=True)


class Chain:

    def __init__(self, eng, sem):
        self.eng, self.sem, self.n = eng, sem, 0

    def __call__(self, ins, base=0):
        self.n += 1
        ins.then_inc(self.sem, 1)
        wait(self.eng, self.sem, base + self.n)


class Stage:

    def __init__(self, nc, name):
        self.nc, self.name, self.ctx, self.sems = nc, name, ExitStack(), []

    def __enter__(self):
        self.ctx.__enter__()
        return self

    def __exit__(self, *a):
        if self.sems and a[0] is None:
            self.nc.clear_and_free_semaphores(self.sems)
            self.nc.all_engine_barrier()
        return self.ctx.__exit__(*a)

    def sb(self, name, shape, dt=F32):
        return self.ctx.enter_context(self.nc.sbuf_tensor(f"{self.name}_{name}", shape, dt))

    def sem(self, name):
        self.sems.append(self.nc.alloc_semaphore(name=f"{self.name}_{name}"))
        return self.sems[-1]

    def block(self):
        return self.nc.Block()


def load_constants(nc, a, k):
    with Stage(nc, "load") as s:
        landed = s.sem("landed")
        zeroed = s.sem("zeroed")
        filled = s.sem("filled")
        with s.block() as block:
            @block.sync
            def _(sp):
                sp.dma_start(k.x[:], a["x_t"]).then_inc(landed, 16)
                sp.dma_start(k.vec[:], a["vecs"]).then_inc(landed, 16)
                sp.wait_ge(landed, 32)

            @block.vector
            def _(v):
                v.memset(k.mean_d[:], 1.0 / D)
                v.memset(k.ones[:], 1.0)
                v.memset(k.mean_p[:], 1.0 / P)
                v.memset(k.mean_q[:], 1.0 / QL)
                v.memset(k.mean_kv[:], 1.0 / KVL)

            @block.gpsimd
            def _(g):
                g.memset(k.ident[:], 0.0).then_inc(zeroed, 1)
                g.wait_ge(zeroed, 1)
                g.affine_select(out=k.ident[:], in_=k.ident[:], compare_op=ALU.not_equal, fill=1.0, base=0,
                                pattern=[[-1, P]], channel_multiplier=1).then_inc(filled, 1)
                g.iota(k.iota[:], pattern=[[1, P]], base=0, channel_multiplier=0,
                       allow_small_or_imprecise_dtypes=True).then_inc(filled, 1)
                g.wait_ge(filled, 2)


def linear(nc, k, name, w, rhs, out, m, kc, residual=False, bias=None):
    with Stage(nc, name) as s:
        slab = s.sb("slab", [P, 2, kc, P])
        slab_h = s.sb("slab_h", [P, 2, kc, P], F32R)
        slab_l = s.sb("slab_l", [P, 2, kc, P], F32R)
        rhs_h = s.sb("rhs_h", [P, kc, T], F32R)
        rhs_l = s.sb("rhs_l", [P, kc, T], F32R)
        landed = [s.sem(f"landed{b}") for b in range(2)]
        rhs_high = s.sem("rhs_high")
        rhs_split = s.sem("rhs_split")
        slab_high = s.sem("slab_high")
        slab_split = s.sem("slab_split")
        summed = s.sem("summed")
        psum_free = s.sem("psum_free")
        scaled = s.sem("scaled")
        with s.block() as block:
            @block.sync
            def _(sp):
                for b in range(2):
                    sp.dma_start(slab[:, b], w[b]).then_inc(landed[b], 16)
                with sp.Fori(0, m // 2 - 1) as i:
                    for b in range(2):
                        wait(sp, slab_split, 2 * i + b + 1)
                        sp.dma_start(slab[:, b], w[bass.ds(2 * i + 2 + b, 1)].rearrange("o p k m -> (o p) k m")
                                     ).then_inc(landed[b], 16)

            @block.tensor
            def _(pe):
                with pe.Fori(0, m // 2) as i:
                    for b in range(2):
                        pe.wait_ge(slab_split, 2 * i + b + 1)
                        pe.wait_ge(psum_free, 2 * i + b + 1)
                        for h in range(2):
                            o = k.ps[:, 2 * b + h, 0:TH]
                            t = slice(h * TH, (h + 1) * TH)
                            for c in range(kc):
                                if b == 0 and h == 0:
                                    pe.wait_ge(rhs_split, c + 1)
                                pe.matmul(o, slab_l[:, b, c], rhs_h[:, c, t], start=(c == 0), stop=False)
                                pe.matmul(o, slab_h[:, b, c], rhs_l[:, c, t], start=False, stop=False)
                                mm = pe.matmul(o, slab_h[:, b, c], rhs_h[:, c, t], start=False, stop=(c == kc - 1))
                        mm.then_inc(summed, 1)

            @block.scalar
            def _(act):
                def high(i, b):
                    act.wait_ge(landed[b], 16 * i + 16)
                    act.activation(slab_h[:, b], slab[:, b], ACT.Copy).then_inc(slab_high, 1)

                high(0, 0)
                for c in range(kc):
                    act.activation(rhs_h[:, c], rhs[:, c], ACT.Copy).then_inc(rhs_high, 1)
                if residual:
                    act.activation(out[:], k.x[:], ACT.Copy, scale=ALPHA).then_inc(scaled, 1)
                high(0, 1)
                with act.Fori(1, m // 2) as i:
                    for b in range(2):
                        act.wait_ge(summed, 2 * i + b - 1)
                        high(i, b)

            @block.vector
            def _(v):
                def low(i, b):
                    v.wait_ge(slab_high, 2 * i + b + 1)
                    v.tensor_tensor(slab_l[:, b], slab[:, b], slab_h[:, b].bitcast(F32), ALU.subtract
                                    ).then_inc(slab_split, 1)

                def collect(i, b):
                    o = halves(out[:, bass.ds(2 * i + b, 1), :].rearrange("p o t -> p (o t)"))
                    banks = k.ps[:, 2 * b:2 * b + 2, 0:TH]
                    v.wait_ge(summed, 2 * i + b + 1)
                    if bias is not None:
                        at = VEC[bias] + 2 * i + b
                        ins = v.scalar_tensor_tensor(o, banks, k.vec[:, bass.ds(at, 1)], o, ALU.add, ALU.add)
                    elif residual:
                        ins = v.tensor_tensor(o, banks, o, ALU.add)
                    else:
                        ins = v.tensor_copy(o, banks)
                    ins.then_inc(psum_free, 1)

                v.sem_inc(psum_free, 2)
                low(0, 0)
                for c in range(kc):
                    v.wait_ge(rhs_high, c + 1)
                    v.tensor_tensor(rhs_l[:, c], rhs[:, c], rhs_h[:, c].bitcast(F32), ALU.subtract).then_inc(rhs_split, 1)
                low(0, 1)
                if residual:
                    v.wait_ge(scaled, 1)
                with v.Fori(0, m // 2 - 1) as i:
                    for b in range(2):
                        collect(i, b)
                        low(i + 1, b)
                for b in range(2):
                    collect(m // 2 - 1, b)


def inverse_root(chain, var, root, tmp):
    v = chain.eng
    chain(v.reciprocal(root, root))
    chain(v.scalar_tensor_tensor(tmp, root, -0.5, root, ALU.mult, ALU.mult))
    chain(v.tensor_tensor(tmp, tmp, var, ALU.mult))
    chain(v.scalar_tensor_tensor(root, tmp, 1.5, root, ALU.add, ALU.mult))


def layer_norm(nc, k, name, r, g, b, out, func):
    with Stage(nc, name) as s:
        sq = s.sb("sq", [P, KC, T])
        var = s.sb("var", [P, T])
        rstd = s.sb("rstd", [P, T])
        newton = s.sb("newton", [P, T])
        mean_ready = s.sem("mean_ready")
        centred = s.sem("centred")
        squared = s.sem("squared")
        var_ready = s.sem("var_ready")
        var_copied = s.sem("var_copied")
        rooted = s.sem("rooted")
        link = s.sem("link")
        normed = s.sem("normed")
        with s.block() as block:
            @block.tensor
            def _(pe):
                for h in range(2):
                    for c in range(KC):
                        mm = pe.matmul(k.ps[:, h, 0:TH], k.mean_d[:], r[:, c, h * TH:(h + 1) * TH],
                                       start=(c == 0), stop=(c == KC - 1))
                    mm.then_inc(mean_ready, 1)
                for h in range(2):
                    pe.wait_ge(squared, h + 1)
                    for c in range(KC):
                        mm = pe.matmul(k.ps[:, 2 + h, 0:TH], k.mean_d[:], sq[:, c, h * TH:(h + 1) * TH],
                                       start=(c == 0), stop=(c == KC - 1))
                    mm.then_inc(var_ready, 1)

            @block.vector
            def _(v):
                for h in range(2):
                    rh = r[:, :, h * TH:(h + 1) * TH]
                    v.wait_ge(mean_ready, h + 1)
                    v.tensor_tensor(rh, rh, bc(k.ps[:, h, 0:TH], 1, KC), ALU.subtract).then_inc(centred, 1)
                for h in range(2):
                    v.wait_ge(var_ready, h + 1)
                    v.tensor_scalar(var[:, h * TH:(h + 1) * TH], k.ps[:, 2 + h, 0:TH], LN_EPS, None, ALU.add
                                    ).then_inc(var_copied, 1)
                v.wait_ge(rooted, 1)
                inverse_root(Chain(v, link), var[:], rstd[:], newton[:])
                for h in range(2):
                    rh = r[:, :, h * TH:(h + 1) * TH]
                    v.tensor_tensor(rh, rh, bc(rstd[:, h * TH:(h + 1) * TH], 1, KC), ALU.mult).then_inc(normed, 1)

            @block.scalar
            def _(act):
                for h in range(2):
                    act.wait_ge(centred, h + 1)
                    act.activation(sq[:, :, h * TH:(h + 1) * TH], r[:, :, h * TH:(h + 1) * TH], ACT.Square
                                   ).then_inc(squared, 1)
                act.wait_ge(var_copied, 2)
                act.activation(rstd[:], var[:], ACT.Sqrt).then_inc(rooted, 1)
                for h in range(2):
                    act.wait_ge(normed, h + 1)
                    for c in range(KC):
                        act.activation(out[:, c, h * TH:(h + 1) * TH], r[:, c, h * TH:(h + 1) * TH], func,
                                       bias=k.col(b, c), scale=k.col(g, c))


class Kept:

    def __init__(self, nc, ctx):
        def sb(name, shape, dt=F32):
            return ctx.enter_context(nc.sbuf_tensor(name, shape, dt))

        self.x = sb("x", [P, KC, T])
        self.vec = sb("vec", [P, NVEC])
        self.mean_d = sb("mean_d", [P, P])
        self.ones = sb("ones", [P, P])
        self.mean_p = sb("mean_p", [P, P])
        self.mean_q = sb("mean_q", [P, P])
        self.mean_kv = sb("mean_kv", [P, P])
        self.ident = sb("ident", [P, P])
        self.iota = sb("iota", [P, P])
        self.ps = ctx.enter_context(nc.psum_tensor("ps", [P, 8, 512], F32))

    def col(self, name, j=0):
        at = VEC[name] + j
        return self.vec[:, at:at + 1]


def mix_values(nc, k, a, vt, vs):
    with Stage(nc, "values") as s:
        w = s.sb("w", [P, KC, H * P])
        landed = s.sem("landed")
        ready = s.sem("ready")
        with s.block() as block:
            @block.sync
            def _(sp):
                sp.dma_start(w[:], a["w_val"]).then_inc(landed, 16)

            @block.tensor
            def _(pe):
                pe.wait_ge(landed, 16)
                for t in range(NCH + 1):
                    n = CL if t < NCH else TS
                    for c in range(KC):
                        mm = pe.matmul(k.ps[0:n, t, :], k.x[:, c, t * CL:t * CL + n], w[:, c, :],
                                       start=(c == 0), stop=(c == KC - 1))
                    mm.then_inc(ready, 1)

            @block.vector
            def _(v):
                for t in range(NCH):
                    v.wait_ge(ready, t + 1)
                    v.tensor_copy(vt[:, t, :], k.ps[:, t, :])
                v.wait_ge(ready, NCH + 1)
                v.tensor_copy(vs[:], k.ps[0:TS, NCH, :])


def recurrence(nc, k, a, proj, vt, vs, cat):
    with Stage(nc, "rec") as s:
        f = s.sb("f", [P, H, T])
        kk = s.sb("k", [P, H, T])
        pre = s.sb("pre", [P, H, TP])
        suf = s.sb("suf", [P, H, TP])
        kd = s.sb("kd", [P, 2, H, TP])
        qd = s.sb("qd", [P, 2, H, TP])
        attn = s.sb("attn", [P, H, NCH, CL])
        masks = s.sb("masks", [P, LEVELS, CL], U32)
        lb = s.sb("lb", [P, 6, H])
        kt = s.sb("kt", [P, H, NCH, P])
        state = s.sb("state", [P, H, P])
        q = proj[:, 0:H]
        gate = proj[:, 2 * H:3 * H]
        landed = s.sem("landed")
        link = s.sem("link")
        lb_e = s.sem("lb_e")
        lb_m = s.sem("lb_m")
        sig = s.sem("sig")
        decayed = s.sem("decayed")
        level_ready = s.sem("level_ready")
        level_read = s.sem("level_read")
        turned = s.sem("turned")
        kt_ready = s.sem("kt_ready")
        chunk_ready = s.sem("chunk_ready")
        chunk_read = s.sem("chunk_read")
        stored = s.sem("stored")
        with s.block() as block:
            @block.sync
            def _(sp):
                sp.dma_start(masks[:], a["masks"]).then_inc(landed, 16)
                sp.wait_ge(chunk_read, NCH)
                sp.dma_start(a["new_hgrn_p"], state[:]).then_inc(stored, 16)
                sp.wait_ge(stored, 16)

            @block.scalar
            def _(act):
                act.activation(f[:], proj[:, H:2 * H], ACT.Sigmoid).then_inc(sig, 1)
                act.activation(kk[:], proj[:, H:2 * H], ACT.Sigmoid, scale=-1.0).then_inc(sig, 1)
                act.activation(gate, gate, ACT.Silu)
                act.wait_ge(lb_m, 1)
                act.activation(lb[:, 0:3], lb[:, 0:3], ACT.Exp).then_inc(lb_e, 1)

            @block.vector
            def _(v):
                chain = Chain(v, link)
                logit = k.vec[:, VEC["lb"]:VEC["lb"] + 3 * H].rearrange("p (l h) -> p l h", l=3)
                chain(v.tensor_tensor(lb[:, 3], logit[:, 0], logit[:, 1], ALU.max))
                chain(v.tensor_tensor(lb[:, 3], lb[:, 3], logit[:, 2], ALU.max))
                v.tensor_tensor(lb[:, 0:3], logit, bc(lb[:, 3], 1, 3), ALU.subtract).then_inc(lb_m, 1)
                v.wait_ge(lb_e, 1)
                chain(v.tensor_tensor(lb[:, 3], lb[:, 0], lb[:, 1], ALU.add))
                chain(v.tensor_tensor(lb[:, 3], lb[:, 3], lb[:, 2], ALU.add))
                chain(v.reciprocal(lb[:, 3], lb[:, 3]))
                chain(v.tensor_tensor(lb[:, 4], lb[:, 0], lb[:, 3], ALU.mult))
                chain(v.tensor_scalar(lb[:, 5], lb[:, 4], -1.0, 1.0, ALU.mult, ALU.add))
                v.wait_ge(sig, 2)
                for h in range(H):
                    v.tensor_scalar(f[:, h], f[:, h], lb[:, 5, h:h + 1], lb[:, 4, h:h + 1], ALU.mult, ALU.add)
                    ins = v.tensor_scalar(kk[:, h], kk[:, h], lb[:, 5, h:h + 1], None, ALU.mult)
                chain(ins)
                v.tensor_copy(pre[:], f[:, :, 0:TP])
                v.memset(suf[:], 1.0)
                v.memset(attn[:], 0.0)
                chain(v.tensor_copy(kd[:, 0], kk[:, :, 0:TP]))
                v.tensor_copy(qd[:, 0], q[:, :, 0:TP]).then_inc(decayed, 1)
                v.wait_ge(landed, 16)

                def take(level):
                    v.wait_ge(level_ready, level + 1)
                    v.copy_predicated(attn[:].rearrange("s h c t -> s (h c) t"), bc(masks[:, level], 1, H * NCH),
                                      k.ps[:, 4 * (level % 2):4 * (level % 2) + 4, :]
                                      .rearrange("s h (c t) -> s (h c) t", t=CL)).then_inc(level_read, 1)

                for level in range(1, LEVELS + 1):
                    m = 1 << (level - 1)
                    if level > 1:
                        hf = m // 2
                        v.wait_ge(decayed, level)
                        p2 = pre[:].rearrange("p h (n m) -> p (h n) m", m=m)
                        s2 = suf[:].rearrange("p h (n m) -> p (h n) m", m=m)
                        chain(v.tensor_tensor(s2[:, :, 0:hf], s2[:, :, 0:hf], bc(p2[:, :, m - 1], 2, hf), ALU.mult))
                        chain(v.tensor_tensor(p2[:, :, hf:m], p2[:, :, hf:m], bc(p2[:, :, hf - 1], 2, hf), ALU.mult))
                    if level >= 2:
                        v.wait_ge(level_ready, level - 1)
                    v.tensor_tensor(kd[:, level % 2], kk[:, :, 0:TP], suf[:], ALU.mult)
                    v.tensor_tensor(qd[:, level % 2], q[:, :, 0:TP], pre[:], ALU.mult).then_inc(decayed, 1)
                    take(level - 1)
                v.wait_ge(turned, 1)
                v.tensor_copy(kt[:].rearrange("s h c d -> s (h c d)"), k.ps[:, 0:4, :].rearrange("s b d -> s (b d)")
                              ).then_inc(kt_ready, 1)
                for c in range(NCH):
                    v.wait_ge(chunk_ready, c + 1)
                    bank = 4 + 2 * (c % 2)
                    v.tensor_copy(cat[:, 0:H, c * CL:(c + 1) * CL], k.ps[:, bank, :].rearrange("p (h t) -> p h t", h=H))
                    new = k.ps[:, bank + 1, :].rearrange("p (h d) -> p h d", h=H)
                    if c == 0:
                        v.tensor_copy(state[:], new).then_inc(chunk_read, 1)
                    else:
                        last = pre[:].rearrange("p h (c t) -> p h c t", t=CL)[:, :, c, CL - 1]
                        chain(v.tensor_tensor(state[:], state[:], bc(last, 2, P), ALU.mult))
                        v.tensor_tensor(state[:], state[:], new, ALU.add).then_inc(chunk_read, 1)
                    v.wait_ge(chunk_read, c + 1)

            @block.tensor
            def _(pe):
                for level in range(LEVELS):
                    pe.wait_ge(decayed, level + 1)
                    if level >= 2:
                        pe.wait_ge(level_read, level - 1)
                    for h in range(H):
                        for c in range(NCH):
                            t = slice(c * CL, (c + 1) * CL)
                            mm = pe.matmul(k.ps[:, 4 * (level % 2) + h, t], kd[:, level % 2, h, t], qd[:, level % 2, h, t],
                                           start=True, stop=True)
                    mm.then_inc(level_ready, 1)
                pe.wait_ge(decayed, LEVELS + 1)
                pe.wait_ge(level_read, LEVELS)
                for h in range(H):
                    for c in range(NCH):
                        t = slice(c * CL, (c + 1) * CL)
                        mm = pe.transpose(k.ps[:, h, t], kd[:, 0, h, t], k.ident[:])
                mm.then_inc(turned, 1)
                pe.wait_ge(kt_ready, 1)
                for c in range(NCH):
                    bank = 4 + 2 * (c % 2)
                    if c:
                        pe.wait_ge(chunk_read, c)
                    for h in range(H):
                        o = k.ps[:, bank, h * CL:(h + 1) * CL]
                        pe.matmul(o, vt[:, c, h * P:(h + 1) * P], attn[:, h, c], start=True, stop=(c == 0))
                        if c:
                            pe.matmul(o, state[:, h], qd[:, 0, h, c * CL:(c + 1) * CL], start=False, stop=True)
                        mm = pe.matmul(k.ps[:, bank + 1, h * P:(h + 1) * P], kt[:, h, c], vt[:, c, h * P:(h + 1) * P],
                                       start=True, stop=True)
                    mm.then_inc(chunk_ready, 1)

        old = s.sb("old", [P, 2, H, P])
        new = s.sb("new", [P, 2, H, P])
        kv = s.sb("kv", [P, H, P])
        old_landed = [s.sem(f"old_landed{b}") for b in range(2)]
        new_stored = [s.sem(f"new_stored{b}") for b in range(2)]
        v_spread = s.sem("v_spread")
        step = s.sem("step")
        new_ready = s.sem("new_ready")
        read_out = s.sem("read_out")
        with s.block() as block:
            @block.sync
            def _(sp):
                for b in range(2):
                    sp.dma_start(old[:, b], a["state_hgrn"][b]).then_inc(old_landed[b], 16)
                for n in range(TS):
                    sp.wait_ge(new_ready, n + 1)
                    sp.dma_start(a["new_hgrn_s"][n], new[:, n % 2]).then_inc(new_stored[n % 2], 16)
                    if n + 2 < TS:
                        sp.dma_start(old[:, n % 2], a["state_hgrn"][n + 2]).then_inc(old_landed[n % 2], 16)
                for b in range(2):
                    sp.wait_ge(new_stored[b], 16 * TS // 2)

            @block.tensor
            def _(pe):
                def spread(n):
                    pe.matmul(k.ps[:, n % 2, :], k.ident[0:TS, n:n + 1].broadcast_to([TS, P]), vs[:],
                              start=True, stop=True).then_inc(v_spread, 1)

                spread(0)
                spread(1)
                for n in range(TS):
                    pe.wait_ge(new_ready, n + 1)
                    if n + 2 < TS:
                        spread(n + 2)
                    for h in range(H):
                        mm = pe.matmul(k.ps[:, 2, n * H + h:n * H + h + 1], new[:, n % 2, h],
                                       q[:, h, TP + n:TP + n + 1], start=True, stop=True)
                    mm.then_inc(read_out, 1)

            @block.vector
            def _(v):
                chain = Chain(v, step)
                for n in range(TS):
                    v.wait_ge(v_spread, n + 1)
                    v.wait_ge(old_landed[n % 2], n // 2 * 16 + 16)
                    if n >= 2:
                        v.wait_ge(new_stored[n % 2], (n // 2) * 16)
                        v.wait_ge(read_out, n - 1)
                    chain(v.tensor_tensor(kv[:], k.ps[:, n % 2, :].rearrange("p (h d) -> p h d", h=H),
                                          bc(kk[:, :, TP + n], 2, P), ALU.mult))
                    chain(v.tensor_tensor(new[:, n % 2], old[:, n % 2], bc(f[:, :, TP + n], 2, P), ALU.mult))
                    v.tensor_tensor(new[:, n % 2], new[:, n % 2], kv[:], ALU.add).then_inc(new_ready, 1)
                    v.wait_ge(new_ready, n + 1)
                v.wait_ge(read_out, TS)
                v.tensor_copy(cat[:, 0:H, TP:T], k.ps[:, 2, 0:TS * H].rearrange("p (n h) -> p h n", h=H))

        sq = kd[:].rearrange("p a h t -> p (a h t)")[:, 0:H * T].rearrange("p (h t) -> p h t", h=H)
        var, rstd, tmp = (z[:].rearrange("p h t -> p (h t)")[:, 0:2 * T] for z in (pre, suf, kk))
        squared = s.sem("squared")
        rms_ready = s.sem("rms_ready")
        copied = s.sem("copied")
        rooted = s.sem("rooted")
        rlink = s.sem("rlink")
        with s.block() as block:
            @block.scalar
            def _(act):
                act.activation(sq, cat[:, 0:H], ACT.Square).then_inc(squared, 1)
                for g in range(2):
                    act.wait_ge(copied, g + 1)
                    act.activation(rstd, var, ACT.Sqrt).then_inc(rooted, 1)

            @block.tensor
            def _(pe):
                pe.wait_ge(squared, 1)
                for h in range(H):
                    for b in range(2):
                        mm = pe.matmul(k.ps[:, 2 * h + b, 0:TH], k.mean_p[:], sq[:, h, b * TH:(b + 1) * TH],
                                       start=True, stop=True)
                mm.then_inc(rms_ready, 1)

            @block.vector
            def _(v):
                chain = Chain(v, rlink)
                v.wait_ge(rms_ready, 1)
                for g in range(2):
                    v.tensor_scalar(var.rearrange("p (b t) -> p b t", b=4), k.ps[:, 4 * g:4 * g + 4, 0:TH], RMS_EPS,
                                    None, ALU.add).then_inc(copied, 1)
                    v.wait_ge(rooted, g + 1)
                    inverse_root(chain, var, rstd, tmp)
                    for h in range(2):
                        o = cat[:, 2 * g + h]
                        chain(v.scalar_tensor_tensor(o, o, k.col("out_norm"), rstd[:, h * T:(h + 1) * T], ALU.mult, ALU.mult))
                        chain(v.tensor_tensor(o, o, gate[:, 2 * g + h], ALU.mult))


def rms(nc, k, name, x, n, mean, g, out):
    with Stage(nc, name) as s:
        sq = s.sb("sq", [P, n, T])
        var = s.sb("var", [P, T])
        rstd = s.sb("rstd", [P, T])
        tmp = s.sb("tmp", [P, T])
        squared = s.sem("squared")
        ready = s.sem("ready")
        copied = s.sem("copied")
        rooted = s.sem("rooted")
        link = s.sem("link")
        with s.block() as block:
            @block.scalar
            def _(act):
                act.activation(sq[:], x, ACT.Square).then_inc(squared, 1)
                act.wait_ge(copied, 1)
                act.activation(rstd[:], var[:], ACT.Sqrt).then_inc(rooted, 1)

            @block.tensor
            def _(pe):
                pe.wait_ge(squared, 1)
                for h in range(2):
                    for c in range(n):
                        mm = pe.matmul(k.ps[:, h, 0:TH], mean[:], sq[:, c, h * TH:(h + 1) * TH],
                                       start=(c == 0), stop=(c == n - 1))
                mm.then_inc(ready, 1)

            @block.vector
            def _(v):
                chain = Chain(v, link)
                v.wait_ge(ready, 1)
                v.tensor_scalar(halves(var[:]), k.ps[:, 0:2, 0:TH], RMS_EPS, None, ALU.add).then_inc(copied, 1)
                v.wait_ge(rooted, 1)
                inverse_root(chain, var[:], rstd[:], tmp[:])
                for c in range(n):
                    v.scalar_tensor_tensor(out[:, c], x[:, c], k.col(g, c), rstd[:], ALU.mult, ALU.mult)


def latent_queries(nc, k, a, proj, qabs, qpe, kpe, ckv):
    with Stage(nc, "lq") as s:
        cq = s.sb("cq", [P, QC, T])
        rms(nc, k, "rms_q", proj[:, 3 * H:3 * H + QC], QC, k.mean_q, "q_norm", cq)
        rms(nc, k, "rms_kv", proj[:, 3 * H + QC:3 * H + QC + CC], CC, k.mean_kv, "kv_norm", ckv)
        wuq = s.sb("wuq", [P, QC, 2 * H * P])
        wuk = s.sb("wuk", [P, H, KVL])
        qn = s.sb("qn", [P, H, T])
        cos = s.sb("cos", [ROPE, T])
        sin = s.sb("sin", [ROPE, T])
        swapped = s.sb("swapped", [ROPE, T])
        rot = s.sb("rot", [ROPE, T])
        landed = s.sem("landed")
        tables = s.sem("tables")
        ready = s.sem("ready")
        free = s.sem("free")
        link = s.sem("link")
        abs_ready = s.sem("abs_ready")
        abs_free = s.sem("abs_free")
        k_ready = s.sem("k_ready")
        stored = s.sem("stored")
        with s.block() as block:
            @block.sync
            def _(sp):
                sp.dma_start(wuq[:], a["w_uq"]).then_inc(landed, 16)
                sp.dma_start(wuk[:], a["w_uk"]).then_inc(landed, 16)
                sp.dma_start(cos[:], a["cos"]).then_inc(tables, 16)
                sp.dma_start(sin[:], a["sin"]).then_inc(tables, 16)
                sp.dma_start(swapped[:], proj[ROPE:P, 3 * H + QC + CC, :]).then_inc(tables, 16)
                sp.dma_start(a["new_lat"], ckv[:]).then_inc(stored, 16)
                sp.wait_ge(k_ready, 1)
                sp.dma_start(a["new_kpe"], kpe[:]).then_inc(stored, 16)
                sp.wait_ge(stored, 32)

            @block.tensor
            def _(pe):
                pe.wait_ge(landed, 32)
                n = 0
                for h in range(H):
                    if n >= 2:
                        pe.wait_ge(free, n - 1)
                    for b in range(2):
                        for c in range(QC):
                            mm = pe.matmul(k.ps[:, 2 * (n % 2) + b, 0:TH], wuq[:, c, h * P:(h + 1) * P],
                                           cq[:, c, b * TH:(b + 1) * TH], start=(c == 0), stop=(c == QC - 1))
                    mm.then_inc(ready, 1)
                    n += 1
                for h in range(H):
                    for sw in range(2):
                        pe.wait_ge(free, n - 1)
                        at = H * P + sw * H * ROPE + h * ROPE
                        for b in range(2):
                            for c in range(QC):
                                mm = pe.matmul(k.ps[0:ROPE, 2 * (n % 2) + b, 0:TH], wuq[:, c, at:at + ROPE],
                                               cq[:, c, b * TH:(b + 1) * TH], start=(c == 0), stop=(c == QC - 1))
                        mm.then_inc(ready, 1)
                        n += 1
                pe.wait_ge(free, H)
                for h in range(H):
                    for c in range(CC):
                        m = CC * h + c
                        if m >= 2:
                            pe.wait_ge(abs_free, m - 1)
                        for b in range(2):
                            mm = pe.matmul(k.ps[:, 4 + 2 * (m % 2) + b, 0:TH], wuk[:, h, c * P:(c + 1) * P],
                                           qn[:, h, b * TH:(b + 1) * TH], start=True, stop=True)
                        mm.then_inc(abs_ready, 1)

            @block.scalar
            def _(act):
                for m in range(H * CC):
                    act.wait_ge(abs_ready, m + 1)
                    act.copy(halves(qabs[:, m // CC, m % CC]), k.ps[:, 4 + 2 * (m % 2):6 + 2 * (m % 2), 0:TH]
                             ).then_inc(abs_free, 1)

            @block.vector
            def _(v):
                chain = Chain(v, link)
                v.wait_ge(tables, 48)
                kr = proj[0:ROPE, 3 * H + QC + CC]
                v.tensor_tensor(kpe[:], kr, cos[:], ALU.mult)
                chain(v.tensor_tensor(rot[:], swapped[:], sin[:], ALU.mult))
                v.tensor_tensor(kpe[:], kpe[:], rot[:], ALU.add).then_inc(k_ready, 1)
                for h in range(H):
                    v.wait_ge(ready, h + 1)
                    v.tensor_copy(halves(qn[:, h]), k.ps[:, 2 * (h % 2):2 * (h % 2) + 2, 0:TH]).then_inc(free, 1)
                for h in range(H):
                    v.wait_ge(ready, H + 2 * h + 1)
                    v.tensor_tensor(halves(qpe[:, h]), k.ps[0:ROPE, 0:2, 0:TH], halves(cos[:]), ALU.mult).then_inc(free, 1)
                    v.wait_ge(ready, H + 2 * h + 2)
                    v.tensor_tensor(halves(rot[:]), k.ps[0:ROPE, 2:4, 0:TH], halves(sin[:]), ALU.mult).then_inc(free, 1)
                    v.wait_ge(free, H + 2 * h + 2)
                    chain(v.tensor_tensor(qpe[:, h], qpe[:, h], rot[:], ALU.add))


def attention(nc, k, a, qabs, qpe, kpe, ckv, proj):
    olat = proj[:, 0:H * CC].rearrange("p (h c) t -> p h c t", h=H)
    sc = proj[:, 2 * H:3 * H, 0:512]
    prob = proj[:, 3 * H:4 * H, 0:512]
    NS = TS * H
    WT = KVL + PAGE
    with Stage(nc, "pa") as s:
        ctok = s.sb("ctok", [P, NCH, KVL])
        mask = s.sb("mask", [P, 512])
        pt = s.sb("pt", [P, H, 512])
        mx = s.sb("mx", [P, H])
        total = s.sb("total", [P, H])
        pages = s.sb("pages", [1, TS * NPG], I32)
        ct = s.sb("ct", [P, 2, NPG, WT + KVL])
        qa = s.sb("qa", [P, CC, TS, H])
        qp = s.sb("qp", [ROPE, TS, H])
        prod = s.sb("prod", [P, CC + 1, TS, H])
        snew = s.sb("snew", [P, TS, H])
        smx = s.sb("smx", [P, 2, H])
        mrow = s.sb("mrow", [2 * H, 1])
        mdiag = s.sb("mdiag", [2 * H, 2 * H])
        sprob = s.sb("sprob", [P, 2, NPG, H])
        pnew = s.sb("pnew", [P, 2, H])
        part = s.sb("part", [P, 2, H])
        rec = s.sb("rec", [P, 2, H])
        add = s.sb("add", [P, CC, 2, H])
        zeroed = s.sem("zeroed")
        masked = s.sem("masked")
        c_turned = s.sem("c_turned")
        c_ready = s.sem("c_ready")
        s_ready = s.sem("s_ready")
        s_read = s.sem("s_read")
        mx_ready = s.sem("mx_ready")
        exped = s.sem("exped")
        p_ready = s.sem("p_ready")
        p_turned = s.sem("p_turned")
        pt_ready = s.sem("pt_ready")
        o_ready = s.sem("o_ready")
        o_read = s.sem("o_read")
        link = s.sem("link")
        page_list = s.sem("page_list")
        pages_landed = [s.sem(f"pages_landed{b}") for b in range(2)]
        q_ready = s.sem("q_ready")
        prod_ready = s.sem("prod_ready")
        new_ready = s.sem("new_ready")
        new_read = s.sem("new_read")
        scored = s.sem("scored")
        smx_ready = s.sem("smx_ready")
        mx_turned = s.sem("mx_turned")
        diag_ready = s.sem("diag_ready")
        spread = s.sem("spread")
        shifted = s.sem("shifted")
        sexped = s.sem("sexped")
        part_ready = s.sem("part_ready")
        sum_ready = s.sem("sum_ready")
        weighed = s.sem("weighed")
        pair_done = s.sem("pair_done")
        UNR = 4

        def fetch(eng, n):
            b = n % 2
            if n >= 2:
                eng.wait_ge(weighed, n - 1)
            with eng.Fori(0, NPG // UNR) as p:
                page = [eng.value_load(pages[0:1, bass.ds(UNR * p + (NPG * n + j), 1)], min_val=0, max_val=POOL_PAGES - 1)
                        for j in range(UNR)]
                for j in range(UNR):
                    eng.dma_start(ct[:, b, bass.ds(UNR * p + j, 1)].rearrange("k o f -> k (o f)"),
                                  a["cache"][bass.ds(page[j], 1)].rearrange("o k f -> (o k) f")
                                  ).then_inc(pages_landed[b], 16)

        with s.block() as block:
            @block.gpsimd
            def _(pool):
                pool.memset(mask[:], 0.0).then_inc(zeroed, 1)
                pool.wait_ge(zeroed, 1)
                pool.affine_select(out=mask[:, 384:512], in_=mask[:, 384:512], compare_op=ALU.is_ge, fill=NEG, base=0,
                                   pattern=[[-1, P]], channel_multiplier=1).then_inc(masked, 1)

            @block.sync
            def _(sp):
                sp.dma_start(pages[:], a["page_table"]).then_inc(page_list, 16)
                sp.wait_ge(page_list, 16)
                for n in range(0, TS, 2):
                    fetch(sp, n)

            @block.tensor
            def _(pe):
                def prompt_scores(qb):
                    w = (qb + 1) * P
                    qs = slice(qb * P, w)
                    if qb:
                        pe.wait_ge(o_read, qb)
                    for h in range(H):
                        o = k.ps[:, h, 0:w]
                        for c in range(CC):
                            pe.matmul(o, qabs[:, h, c, qs], ckv[:, c, 0:w], start=(c == 0), stop=False)
                        mm = pe.matmul(o, qpe[:, h, qs], kpe[:, 0:w], start=False, stop=True)
                    mm.then_inc(s_ready, 1)

                def pair(qb):
                    for b in range(2):
                        n = 2 * qb + b
                        pe.wait_ge(pages_landed[b], 16 * NPG * (qb + 1))
                        for p in range(NPG):
                            at = (b * NPG + p) * H
                            o = k.ps[:, 4, at:at + H]
                            for c in range(CC):
                                pe.matmul(o, ct[:, b, p, c * PAGE:(c + 1) * PAGE], qa[:, c, n, :], start=(c == 0), stop=False)
                            mm = pe.matmul(o, ct[0:ROPE, b, p, KVL:WT], qp[:, n, :], start=False, stop=True)
                    mm.then_inc(scored, 1)
                    pe.wait_ge(smx_ready, qb + 1)
                    pe.transpose(k.ps[0:2 * H, 5, 0:P], smx[:].rearrange("p n h -> p (n h)"), k.ident[:]).then_inc(mx_turned, 1)
                    pe.wait_ge(diag_ready, qb + 1)
                    pe.matmul(k.ps[:, 5, P:P + 2 * H], k.ones[0:2 * H, :], mdiag[:], start=True, stop=True).then_inc(spread, 1)
                    pe.wait_ge(sexped, 2 * qb + 2)
                    for b in range(2):
                        for c in range(CC):
                            at = (c * 2 + b) * H
                            for p in range(NPG):
                                mm = pe.matmul(k.ps[:, 6, at:at + H], ct[:, b, p, WT + c * P:WT + (c + 1) * P],
                                               sprob[:, b, p, :], start=(p == 0), stop=(p == NPG - 1))
                        mm.then_inc(weighed, 1)
                    pe.wait_ge(part_ready, qb + 1)
                    pe.matmul(k.ps[:, 7, 0:2 * H], k.ones[:], part[:].rearrange("p n h -> p (n h)"), start=True, stop=True
                              ).then_inc(sum_ready, 1)

                for c in range(CC):
                    for t in range(NCH):
                        mm = pe.transpose(k.ps[:, 4 + c, t * P:(t + 1) * P], ckv[:, c, t * P:(t + 1) * P], k.ident[:])
                mm.then_inc(c_turned, 1)
                prompt_scores(0)
                pe.wait_ge(prod_ready, 1)
                for c in range(CC):
                    pe.matmul(k.ps[:, 6, 0:NS], k.ones[:], prod[:, c].rearrange("p n h -> p (n h)"),
                              start=(c == 0), stop=False)
                pe.matmul(k.ps[:, 6, 0:NS], k.ones[0:ROPE, :], prod[0:ROPE, CC].rearrange("p n h -> p (n h)"),
                          start=False, stop=True).then_inc(new_ready, 1)
                for qb in range(NCH):
                    pe.wait_ge(p_ready, qb + 1)
                    pe.wait_ge(c_ready, 1)
                    pe.wait_ge(new_read, 1)
                    if qb:
                        pe.wait_ge(pair_done, qb)
                    for h in range(H):
                        for kb in range(qb + 1):
                            mm = pe.transpose(k.ps[:, 4 + h, kb * P:(kb + 1) * P], prob[:, h, kb * P:(kb + 1) * P], k.ident[:])
                    mm.then_inc(p_turned, 1)
                    pe.wait_ge(pt_ready, qb + 1)
                    for h in range(H):
                        for c in range(CC):
                            for kb in range(qb + 1):
                                mm = pe.matmul(k.ps[:, h, c * P:(c + 1) * P], ctok[:, kb, c * P:(c + 1) * P],
                                               pt[:, h, kb * P:(kb + 1) * P], start=(kb == 0), stop=(kb == qb))
                    mm.then_inc(o_ready, 1)
                    if qb < NCH - 1:
                        prompt_scores(qb + 1)
                    pair(qb)

            @block.vector
            def _(v):
                chain = Chain(v, link)

                def prompt_max(qb):
                    w = (qb + 1) * P
                    v.wait_ge(s_ready, qb + 1)
                    v.tensor_tensor(sc[:, :, 0:w], k.ps[:, 0:H, 0:w], bc(mask[:, 512 - w:512], 1, H), ALU.add
                                    ).then_inc(s_read, 1)
                    v.wait_ge(s_read, qb + 1)
                    chain(v.tensor_reduce(mx[:], sc[:, :, 0:w], AX.X, ALU.max))
                    v.tensor_scalar(mx[:], mx[:], -SCALE, None, ALU.mult).then_inc(mx_ready, 1)

                def prompt_probs(qb):
                    w = (qb + 1) * P
                    v.wait_ge(exped, qb + 1)
                    chain(v.reciprocal(total[:], total[:]))
                    v.tensor_tensor(prob[:, :, 0:w], prob[:, :, 0:w], bc(total[:], 2, w), ALU.mult).then_inc(p_ready, 1)

                def pair(qb):
                    sscore = k.ps[:, 4, 0:2 * NPG * H].rearrange("p (n g h) -> p n g h", n=2, g=NPG)
                    new = snew[:, 2 * qb:2 * qb + 2]
                    v.wait_ge(scored, qb + 1)
                    v.tensor_reduce(smx[:], sscore.rearrange("p n g h -> p n h g"), AX.X, ALU.max).then_inc(smx_ready, 1)
                    v.wait_ge(mx_turned, qb + 1)
                    chain(v.tensor_reduce(mrow[:], k.ps[0:2 * H, 5, 0:P], AX.X, ALU.max))
                    v.tensor_scalar(mdiag[:], k.ident[0:2 * H, 0:2 * H], mrow[:], None, ALU.mult).then_inc(diag_ready, 1)
                    v.wait_ge(spread, qb + 1)
                    chain(v.tensor_tensor(smx[:], new, k.ps[:, 5, P:P + 2 * H].rearrange("p (n h) -> p n h", n=2), ALU.max))
                    v.tensor_tensor(sprob[:], sscore, bc(smx[:], 2, NPG), ALU.subtract)
                    v.tensor_tensor(pnew[:], new, smx[:], ALU.subtract).then_inc(shifted, 1)
                    if qb < NCH - 1:
                        prompt_probs(qb + 1)
                    v.wait_ge(sexped, 2 * qb + 2)
                    v.tensor_reduce(part[:], sprob[:].rearrange("p n g h -> p n h g"), AX.X, ALU.add).then_inc(part_ready, 1)
                    for c in range(CC):
                        ins = v.tensor_tensor(add[:, c], pnew[:], bc(ckv[:, c, TP + 2 * qb:TP + 2 * qb + 2], 2, H), ALU.mult)
                    chain(ins)
                    v.wait_ge(weighed, 2 * qb + 2)
                    chain(v.tensor_tensor(add[:], add[:], k.ps[:, 6, 0:2 * CC * H]
                                          .rearrange("p (c n h) -> p c n h", c=CC, h=H), ALU.add))
                    v.wait_ge(sum_ready, qb + 1)
                    chain(v.tensor_tensor(rec[:], pnew[:], k.ps[:, 7, 0:2 * H].rearrange("p (n h) -> p n h", n=2), ALU.add))
                    chain(v.reciprocal(rec[:], rec[:]))
                    v.tensor_tensor(olat.rearrange("p h c t -> p c t h")[:, :, TP + 2 * qb:TP + 2 * qb + 2, :], add[:],
                                    bc(rec[:], 1, CC), ALU.mult).then_inc(pair_done, 1)

                v.wait_ge(c_turned, 1)
                v.tensor_copy(ctok[:].rearrange("t n (c f) -> t c n f", c=CC),
                              k.ps[:, 4:6, :].rearrange("t c (n f) -> t c n f", n=NCH)).then_inc(c_ready, 1)
                v.tensor_copy(qa[:].rearrange("p c n h -> p c h n"),
                              qabs[:].rearrange("p h c t -> p c h t")[:, :, :, TP:T])
                v.tensor_copy(qp[:].rearrange("p n h -> p h n"), qpe[:, :, TP:T]).then_inc(q_ready, 1)
                v.wait_ge(q_ready, 1)
                for c in range(CC):
                    v.tensor_tensor(prod[:, c], qa[:, c], bc(ckv[:, c, TP:T], 2, H), ALU.mult)
                v.tensor_tensor(prod[0:ROPE, CC], qp[:], bc(kpe[:, TP:T], 2, H), ALU.mult).then_inc(prod_ready, 1)
                v.wait_ge(masked, 1)
                prompt_max(0)
                v.wait_ge(new_ready, 1)
                v.tensor_copy(snew[:].rearrange("p n h -> p (n h)"), k.ps[:, 6, 0:NS]).then_inc(new_read, 1)
                prompt_probs(0)
                for qb in range(NCH):
                    w = (qb + 1) * P
                    v.wait_ge(p_turned, qb + 1)
                    v.tensor_copy(pt[:, :, 0:w], k.ps[:, 4:4 + H, 0:w]).then_inc(pt_ready, 1)
                    v.wait_ge(o_ready, qb + 1)
                    v.tensor_copy(olat[:, :, :, qb * P:(qb + 1) * P],
                                  k.ps[:, 0:H, 0:CC * P].rearrange("p h (c q) -> p h c q", c=CC)).then_inc(o_read, 1)
                    if qb < NCH - 1:
                        prompt_max(qb + 1)
                    pair(qb)

            @block.scalar
            def _(act):
                def prompt_exp(qb):
                    w = (qb + 1) * P
                    act.wait_ge(mx_ready, qb + 1)
                    if qb:
                        act.wait_ge(p_turned, qb)
                    for h in range(H):
                        ins = act.activation(prob[:, h, 0:w], sc[:, h, 0:w], ACT.Exp, bias=mx[:, h:h + 1], scale=SCALE,
                                             accum_out=total[:, h:h + 1])
                    ins.then_inc(exped, 1)

                act.wait_ge(page_list, 16)
                fetch(act, 1)
                prompt_exp(0)
                for qb in range(NCH):
                    if qb < NCH - 1:
                        prompt_exp(qb + 1)
                    act.wait_ge(shifted, qb + 1)
                    act.activation(sprob[:], sprob[:], ACT.Exp, scale=SCALE).then_inc(sexped, 1)
                    act.activation(pnew[:], pnew[:], ACT.Exp, scale=SCALE).then_inc(sexped, 1)
                    if qb < NCH - 1:
                        fetch(act, 2 * qb + 3)


def latent_values(nc, k, a, olat, cat):
    with Stage(nc, "lv") as s:
        w = s.sb("w", [P, H, CC, P])
        landed = s.sem("landed")
        ready = s.sem("ready")
        with s.block() as block:
            @block.sync
            def _(sp):
                sp.dma_start(w[:], a["w_uv"]).then_inc(landed, 16)

            @block.tensor
            def _(pe):
                pe.wait_ge(landed, 16)
                for h in range(H):
                    for b in range(2):
                        for c in range(CC):
                            mm = pe.matmul(k.ps[:, 2 * h + b, 0:TH], w[:, h, c], olat[:, h, c, b * TH:(b + 1) * TH],
                                           start=(c == 0), stop=(c == CC - 1))
                    mm.then_inc(ready, 1)

            @block.vector
            def _(v):
                for h in range(H):
                    v.wait_ge(ready, h + 1)
                    v.tensor_copy(halves(cat[:, H + h]), k.ps[:, 2 * h:2 * h + 2, 0:TH])


def mixer(nc, k, a, proj, r):
    with Stage(nc, "mixer") as s:
        cat = s.sb("cat", [P, 2 * H, T])
        linear(nc, k, "mix_in", a["w_mix"], k.x, proj, 18, KC)
        with Stage(nc, "hg") as t:
            vt = t.sb("vt", [P, NCH, H * P])
            vs = t.sb("vs", [TS, H * P])
            mix_values(nc, k, a, vt, vs)
            recurrence(nc, k, a, proj, vt, vs, cat)
        with Stage(nc, "mla") as t:
            ckv = t.sb("ckv", [P, CC, T])
            kpe = t.sb("kpe", [ROPE, T])
            qabs = t.sb("qabs", [P, H, CC, T])
            qpe = t.sb("qpe", [ROPE, H, T])
            latent_queries(nc, k, a, proj, qabs, qpe, kpe, ckv)
            olat = proj[:, 0:H * CC].rearrange("p (h c) t -> p h c t", h=H)
            attention(nc, k, a, qabs, qpe, kpe, ckv, proj)
            latent_values(nc, k, a, olat, cat)
        linear(nc, k, "mix_out", a["w_mix_out"], cat, r, KC, KC, residual=True)


class Split:

    def __init__(self, s):
        self.xh = s.sb("xh", [P, KC, T], F32R)
        self.xl = s.sb("xl", [P, KC, T], F32R)
        self.u = s.sb("u", [P, 2, KC, P])
        self.uh = s.sb("uh", [P, 2, KC, P], F32R)
        self.ul = s.sb("ul", [P, 2, KC, P], F32R)

    def product(self, pe, k, bank, b):
        for h in range(2):
            o = k.ps[:, bank + h, 0:TH]
            t = slice(h * TH, (h + 1) * TH)
            for c in range(KC):
                pe.matmul(o, self.ul[:, b, c], self.xh[:, c, t], start=(c == 0), stop=False)
                pe.matmul(o, self.uh[:, b, c], self.xl[:, c, t], start=False, stop=False)
                mm = pe.matmul(o, self.uh[:, b, c], self.xh[:, c, t], start=False, stop=(c == KC - 1))
        return mm


def peer_retrieve(nc, k, a, layer, sp_x, values, ranks):
    with Stage(nc, f"retrieve{layer}") as s:
        w = a["peer_wq"][layer]
        slab = s.sb("slab", [P, 2, KC, P])
        q = s.sb("q", [P, 2, T])
        keys = s.sb("keys", [P, HP, NK])
        rest = s.sb("rest", [TT, NT, NK])
        top = s.sb("top", [TT, NT, TOPK])
        topi = s.sb("topi", [TT, NT, TOPK], U32)
        landed = [s.sem(f"landed{b}") for b in range(2)]
        keys_landed = s.sem("keys_landed")
        slab_free = s.sem("slab_free")
        q_copied = s.sem("q_copied")
        score_free = s.sem("score_free")
        score_ready = s.sem("score_ready")
        link = s.sem("link")
        x_split = s.sem("x_split")
        score = [k.ps[0:TT, 4 + 2 * b:6 + 2 * b, :].rearrange("t a n -> t (a n)")[:, 0:NT * NK]
                 .rearrange("t (n m) -> t n m", m=NK) for b in range(2)]
        with s.block() as block:
            @block.sync
            def _(sp):
                for b in range(2):
                    sp.dma_start(slab[:, b], w[b]).then_inc(landed[b], 16)
                sp.dma_start(keys[:], a["peer_keys"][layer]).then_inc(keys_landed, 16)
                with sp.Fori(0, HP // 2 - 1) as i:
                    for b in range(2):
                        wait(sp, slab_free, 2 * i + b + 1)
                        sp.dma_start(slab[:, b], w[bass.ds(2 * i + 2 + b, 1)].rearrange("o p k m -> (o p) k m")
                                     ).then_inc(landed[b], 16)

            @block.tensor
            def _(pe):
                def project(i, b):
                    pe.wait_ge(landed[b], 16 * i + 16)
                    pe.wait_ge(q_copied, 2 * i + b + 1)
                    for h in range(2):
                        for c in range(KC):
                            mm = pe.matmul(k.ps[:, 2 * b + h, 0:TH], slab[:, b, c], k.x[:, c, h * TH:(h + 1) * TH],
                                           start=(c == 0), stop=(c == KC - 1))
                    mm.then_inc(slab_free, 1)

                def scores(i, b):
                    n = 2 * i + b
                    pe.wait_ge(q_copied, n + 3)
                    pe.wait_ge(score_free, n + 1)
                    for t in range(NT):
                        mm = pe.matmul(score[b][:, t], q[:, b, t * TT:(t + 1) * TT],
                                       keys[:, bass.ds(n, 1) if not isinstance(n, int) else slice(n, n + 1), :]
                                       .rearrange("p o n -> p (o n)"), start=True, stop=True)
                    mm.then_inc(score_ready, 1)

                pe.wait_ge(keys_landed, 16)
                project(0, 0)
                with pe.Fori(0, HP // 2 - 1) as i:
                    project(i, 1)
                    scores(i, 0)
                    project(i + 1, 0)
                    scores(i, 1)
                project(HP // 2 - 1, 1)
                scores(HP // 2 - 1, 0)
                scores(HP // 2 - 1, 1)

            @block.scalar
            def _(act):
                act.sem_inc(q_copied, 2)
                act.sem_inc(score_ready, 2)
                with act.Fori(0, HP // 2) as i:
                    for b in range(2):
                        act.wait_ge(slab_free, 2 * i + b + 1)
                        act.wait_ge(score_ready, 2 * i + b + 1)
                        act.copy(halves(q[:, b]), k.ps[:, 2 * b:2 * b + 2, 0:TH]).then_inc(q_copied, 1)

            @block.vector
            def _(v):
                v.sem_inc(score_free, 2)
                v.tensor_copy(sp_x.xh[:], k.x[:]).then_inc(x_split, 1)
                v.wait_ge(x_split, 1)
                v.tensor_tensor(sp_x.xl[:], k.x[:], sp_x.xh[:].bitcast(F32), ALU.subtract)
                with v.Fori(0, HP // 2) as i:
                    chain = Chain(v, link)
                    base = 8 * i
                    for b in range(2):
                        sc = score[b]
                        wait(v, score_ready, 2 * i + b + 3)
                        for t in range(NT):
                            ins = v.max(top[:, t, 0:8], sc[:, t])
                        chain(ins, base)
                        for t in range(NT):
                            v.max_index(topi[:, t, 0:8], top[:, t, 0:8], sc[:, t])
                            ins = v.match_replace(rest[:, t], top[:, t, 0:8], sc[:, t], NEG)
                            if t == NT - 1:
                                ins.then_inc(score_free, 1)
                        wait(v, score_free, 2 * i + b + 3)
                        for t in range(NT):
                            ins = v.max(top[:, t, 8:16], rest[:, t])
                        chain(ins, base)
                        for t in range(NT):
                            ins = v.max_index(topi[:, t, 8:16], top[:, t, 8:16], rest[:, t])
                        chain(ins, base)
                        n = bass.ds(2 * i + b, 1)
                        v.tensor_copy(values[:, :, n, :].rearrange("t n o r -> t n (o r)"), top[:])
                        chain(v.tensor_copy(ranks[:, :, n, :].rearrange("t n o r -> t n (o r)"), topi[:]), base)
                    assert chain.n == 8


def peer_gates(nc, k, a, layer, sp_x, values, ranks):
    with Stage(nc, f"gates{layer}") as s:
        cand = s.sb("cand", [TT, PH, NCAND])
        rest = s.sb("rest", [TT, PH, NCAND])
        best = s.sb("best", [TT, PH, TOPK])
        expd = s.sb("expd", [TT, PH, TOPK])
        pos = s.sb("pos", [TT, PH, TOPK], U32)
        part = s.sb("part", [TT, PH, TOPK], U32)
        shift = s.sb("shift", [TT, 2, PH, TOPK], U32)
        is_b = s.sb("is_b", [TT, PH, TOPK])
        ra = s.sb("ra", [TT, PH, TOPK])
        rb = s.sb("rb", [TT, PH, TOPK])
        pick = s.sb("pick", [TT, 2, PH * TOPK, TOPK])
        ijg = s.sb("ijg", [TT, 3, PH * TOPK])
        total = s.sb("total", [TT, PH])
        cols = s.sb("cols", [P, 3, TT])
        onej = s.sb("onej", [P, 2, 4, NK])
        onei = s.sb("onei", [P, 2, 4, NK])
        g = s.sb("g", [P, NK, TT])
        hid = s.sb("hid", [P, 2, T])
        link = s.sem("link")
        centred = s.sem("centred")
        exped = s.sem("exped")
        ijg_ready = s.sem("ijg_ready")
        turned = s.sem("turned")
        one_ready = s.sem("one_ready")
        g_ready = s.sem("g_ready")
        g_free = s.sem("g_free")
        g_stored = s.sem("g_stored")
        u_landed = [s.sem(f"u_landed{b}") for b in range(2)]
        u_high = s.sem("u_high")
        u_split = s.sem("u_split")
        h_ready = s.sem("h_ready")
        gelu_ready = s.sem("gelu_ready")
        hid_stored = [s.sem(f"hid_stored{b}") for b in range(2)]
        turn = k.ps[:, 2, 0:3 * TT].rearrange("p (c t) -> p c t", c=3)
        iota16 = k.iota[0:TT, 0:TOPK]
        banks = TT // 4
        rounds = (PER_TILE - SELECT) // 2
        assert banks == 4 * rounds + 2
        with s.block() as block:
            @block.vector
            def _(v):
                def split(s, b):
                    v.wait_ge(u_high, s + 1)
                    v.tensor_tensor(sp_x.ul[:, b % 2], sp_x.u[:, b % 2], sp_x.uh[:, b % 2].bitcast(F32), ALU.subtract
                                    ).then_inc(u_split, 1)

                def one_hot(t, at, b):
                    v.wait_ge(g_ready, banks * t + at + b + 1)
                    for n in range(4):
                        tok = bass.ds(4 * at + 4 * b + n, 1)
                        v.tensor_scalar(onej[:, b % 2, n], k.iota[:], cols[:, 1, tok], None, ALU.is_equal)
                        ins = v.tensor_scalar(onei[:, b % 2, n], k.iota[:], cols[:, 0, tok], cols[:, 2, tok],
                                              ALU.is_equal, ALU.mult)
                    ins.then_inc(one_ready, 1)

                split(0, 0)
                split(1, 1)
                with v.Fori(0, NT) as t:
                    chain = Chain(v, link)
                    base = 15 * t
                    ahead = PER_TILE * t + 2
                    tile = bass.ds(t, 1)
                    val = values[:, tile].rearrange("t o (h p) r -> t (o h) p r", p=2)
                    rank = ranks[:, tile].rearrange("t o (h p) r -> t (o h) p r", p=2)
                    v.tensor_tensor(cand[:, :, 0:CANDA * 16].rearrange("t h (x y) -> t h x y", y=16),
                                    bc(val[:, :, 0, 0:CANDA], 3, 16), bc(val[:, :, 1, :], 2, CANDA), ALU.add)
                    chain(v.tensor_tensor(cand[:, :, CANDA * 16:NCAND].rearrange("t h (x y) -> t h x y", y=4),
                                          bc(val[:, :, 0, CANDA:16], 3, 4), bc(val[:, :, 1, 0:4], 2, CANDB), ALU.add), base)
                    for h in range(PH):
                        ins = v.max(best[:, h, 0:8], cand[:, h])
                    chain(ins, base)
                    for h in range(PH):
                        v.max_index(pos[:, h, 0:8], best[:, h, 0:8], cand[:, h])
                        ins = v.match_replace(rest[:, h], best[:, h, 0:8], cand[:, h], NEG)
                    split(ahead, 0)
                    chain(ins, base)
                    for h in range(PH):
                        ins = v.max(best[:, h, 8:16], rest[:, h])
                    chain(ins, base)
                    for h in range(PH):
                        ins = v.max_index(pos[:, h, 8:16], best[:, h, 8:16], rest[:, h])
                    split(ahead + 1, 1)
                    chain(ins, base)
                    v.tensor_tensor(expd[:], best[:], bc(best[:, :, 0], 2, TOPK), ALU.subtract).then_inc(centred, 1)
                    v.tensor_single_scalar(shift[:, 0], pos[:], 4, ALU.logical_shift_right)
                    v.tensor_single_scalar(shift[:, 1], pos[:], 2, ALU.logical_shift_right)
                    v.tensor_single_scalar(is_b[:], pos[:], float(CANDA * 16), ALU.is_ge)
                    chain(v.tensor_single_scalar(part[:], pos[:], 3, ALU.bitwise_and), base)
                    v.tensor_tensor(ra[:], shift[:, 1], shift[:, 0], ALU.subtract)
                    chain(v.tensor_single_scalar(pos[:], pos[:], 15, ALU.bitwise_and), base)
                    v.tensor_scalar(ra[:], ra[:], -12.0, None, ALU.add)
                    chain(v.tensor_tensor(rb[:], part[:], pos[:], ALU.subtract), base)
                    split(ahead + 2, 2)
                    v.tensor_tensor(ra[:], ra[:], is_b[:], ALU.mult)
                    chain(v.tensor_tensor(rb[:], rb[:], is_b[:], ALU.mult), base)
                    v.tensor_tensor(ra[:], ra[:], shift[:, 0], ALU.add)
                    chain(v.tensor_tensor(rb[:], rb[:], pos[:], ALU.add), base)
                    for p, r in enumerate((ra, rb)):
                        ins = v.tensor_tensor(pick[:, p], bc(r[:].rearrange("t h r -> t (h r)"), 2, TOPK),
                                              bc(iota16, 1, PH * TOPK), ALU.is_equal)
                    chain(ins, base)
                    split(ahead + 3, 3)
                    for p in range(2):
                        ins = v.tensor_tensor(pick[:, p].rearrange("t (h r) x -> t h r x", h=PH),
                                              pick[:, p].rearrange("t (h r) x -> t h r x", h=PH),
                                              bc(rank[:, :, p, :], 2, TOPK), ALU.mult)
                    split(ahead + 4, 4)
                    chain(ins, base)
                    for p in range(2):
                        v.tensor_reduce(ijg[:, p], pick[:, p], AX.X, ALU.add)
                    v.wait_ge(exped, t + 1)
                    chain(v.tensor_reduce(total[:], expd[:], AX.X, ALU.add), base)
                    split(ahead + 5, 5)
                    chain(v.reciprocal(total[:], total[:]), base)
                    v.tensor_tensor(ijg[:, 2].rearrange("t (h r) -> t h r", h=PH), expd[:], bc(total[:], 2, TOPK),
                                    ALU.mult).then_inc(ijg_ready, 1)
                    v.wait_ge(turned, t + 1)
                    v.wait_ge(g_ready, banks * t + 2)
                    chain(v.tensor_copy(cols[:], turn), base)
                    assert chain.n == 15
                    split(ahead + 6, 6)
                    with v.Fori(0, rounds) as u:
                        for b in range(0, 4, 2):
                            one_hot(t, 4 * u, b)
                            one_hot(t, 4 * u, b + 1)
                            split(ahead + 2 * u + 7 + b // 2, 7 + b // 2)
                    one_hot(t, 4 * rounds, 0)
                    one_hot(t, 4 * rounds, 1)
                    split(ahead + PER_TILE - 1, PER_TILE - 1)
                for b in range(EXTRA):
                    split(PER_TILE * NT + 2 + b, b)

            @block.tensor
            def _(pe):
                def hidden(s, b):
                    pe.wait_ge(u_split, s + 1)
                    pe.wait_ge(gelu_ready, s + 1)
                    sp_x.product(pe, k, 4 + 2 * (b % 2), b % 2).then_inc(h_ready, 1)

                def gates(t, at, b):
                    n = banks * t + at + b
                    pe.wait_ge(one_ready, n + 1)
                    pe.wait_ge(g_free, n + 1)
                    for m in range(4):
                        mm = pe.matmul(k.ps[:, b % 2, m * NK:(m + 1) * NK], onej[:, b % 2, m], onei[:, b % 2, m],
                                       start=True, stop=True)
                    mm.then_inc(g_ready, 1)

                pe.sem_inc(g_ready, 2)
                with pe.Fori(0, NT) as t:
                    first = PER_TILE * t
                    for b in range(SELECT - 1):
                        hidden(first + b, b)
                    pe.wait_ge(ijg_ready, t + 1)
                    for c in range(3):
                        mm = pe.transpose(turn[:, c], ijg[:, c], k.ident[0:TT, 0:TT])
                    mm.then_inc(turned, 1)
                    hidden(first + SELECT - 1, SELECT - 1)
                    with pe.Fori(0, rounds) as u:
                        for b in range(0, 4, 2):
                            gates(t, 4 * u, b)
                            gates(t, 4 * u, b + 1)
                            hidden(first + SELECT + 2 * u + b // 2, SELECT + b // 2)
                    gates(t, 4 * rounds, 0)
                    gates(t, 4 * rounds, 1)
                for b in range(EXTRA):
                    hidden(PER_TILE * NT + b, b)

            @block.scalar
            def _(act):
                def split(s, b, first=False):
                    act.wait_ge(u_landed[b % 2], 8 * (s - b % 2) + 16)
                    if not first:
                        act.wait_ge(h_ready, s - 1)
                    act.activation(sp_x.uh[:, b % 2], sp_x.u[:, b % 2], ACT.Copy).then_inc(u_high, 1)

                def step(s, b):
                    split(s + 2, b)
                    act.wait_ge(h_ready, s + 1)
                    act.wait_ge(hid_stored[b % 2], 8 * (s - b % 2) + 16)
                    act.activation(halves(hid[:, b % 2]), k.ps[:, 4 + 2 * (b % 2):6 + 2 * (b % 2), 0:TH], ACT.Gelu
                                   ).then_inc(gelu_ready, 1)

                def copy_gates(t, at, b):
                    act.wait_ge(g_ready, banks * t + at + b + 3)
                    act.activation(g[:, :, bass.ds(4 * at + 4 * b, 4)],
                                   k.ps[:, b % 2].rearrange("j (t i) -> j i t", t=4), ACT.Copy).then_inc(g_free, 1)

                act.sem_inc(g_free, 2)
                act.sem_inc(gelu_ready, 2)
                act.sem_inc(hid_stored[0], 16)
                act.sem_inc(hid_stored[1], 16)
                split(0, 0, True)
                split(1, 1, True)
                with act.Fori(0, NT) as t:
                    first = PER_TILE * t
                    for b in range(SELECT - 1):
                        step(first + b, b)
                        if b == 3:
                            act.wait_ge(centred, t + 1)
                            act.activation(expd[:], expd[:], ACT.Exp).then_inc(exped, 1)
                    with act.Fori(0, rounds) as u:
                        for b in range(0, 4, 2):
                            step(first + SELECT - 1 + 2 * u + b // 2, SELECT - 1 + b // 2)
                            if b == 0:
                                act.wait_ge(g_stored, 16 * SELECT * t + 16)
                            copy_gates(t, 4 * u, b)
                            copy_gates(t, 4 * u, b + 1)
                    step(first + PER_TILE - 1, PER_TILE - 1)
                    copy_gates(t, 4 * rounds, 0)
                    copy_gates(t, 4 * rounds, 1)
                for b in range(EXTRA):
                    step(PER_TILE * NT + b, b)

            @block.sync
            def _(sp):
                def load_u(n, b):
                    sp.dma_start(sp_x.u[:, b % 2], a["peer_u"][bass.ds(layer * NK + n, 1)]
                                 .rearrange("o p k e -> (o p) k e")).then_inc(u_landed[b % 2], 16)

                def step(s, b):
                    wait(sp, u_split, s + 3)
                    load_u(s + 4, b)
                    wait(sp, gelu_ready, s + 3)
                    sp.dma_start(a["hidden"][bass.ds(s, 1)].rearrange("o p t -> (o p) t"), hid[:, b % 2]
                                 ).then_inc(hid_stored[b % 2], 16)

                def store_gates(t, c):
                    n = NG // SELECT
                    sp.dma_start(a["gates"][n * c:n * c + n, bass.ds(t, 1)].rearrange("g o j i t -> (o j) g (i t)"),
                                 g[:, n * GB * c:n * GB * (c + 1)].rearrange("j (g i) t -> j g (i t)", i=GB)
                                 ).then_inc(g_stored, 16)

                sp.sem_inc(g_stored, 16)
                for b in range(2):
                    load_u(b, b)
                for b in range(2):
                    sp.wait_ge(u_split, b + 1)
                    load_u(b + 2, b)
                for b in range(SELECT):
                    step(b, b)
                with sp.Fori(0, NT - 1) as t:
                    with sp.Fori(0, rounds) as u:
                        for b in range(2):
                            step(PER_TILE * t + SELECT + 2 * u + b, b)
                    wait(sp, g_free, banks * t + banks + 2)
                    for b in range(SELECT):
                        store_gates(t, b)
                        step(PER_TILE * t + PER_TILE + b, b)
                with sp.Fori(0, rounds) as u:
                    for b in range(2):
                        step(PER_TILE * (NT - 1) + SELECT + 2 * u + b, b)
                sp.wait_ge(g_free, banks * NT + 2)
                for b in range(SELECT):
                    store_gates(NT - 1, b)
                    step(PER_TILE * NT + b, b)
                sp.wait_ge(g_stored, 16 * SELECT * NT + 16)
                for b in range(2):
                    sp.wait_ge(hid_stored[b], 8 * AHEAD + 16)
                    sp.wait_ge(u_landed[b], 8 * AHEAD + 32)


def peer_experts(nc, k, a, layer, sp_x, r):
    with Stage(nc, f"experts{layer}") as s:
        w = s.sb("v", [P, 2, D])
        wh = s.sb("vh", [P, GB, D], F32R)
        wl = s.sb("vl", [P, GB, D], F32R)
        g = s.sb("g", [P, 2, NT, GB, TT])
        act_out = s.sb("act", [P, 2, T])
        gated = s.sb("gated", [P, T])
        gh = s.sb("gh", [P, 2, GB, T], F32R)
        gl = s.sb("gl", [P, 2, GB, T], F32R)
        u, uh, ul = sp_x.u, sp_x.uh, sp_x.ul
        places = [[z[:].rearrange("p c t -> p (c t)")[:, 0:GB * D].rearrange("p (b d) -> p b d", b=GB)
                   for z in (sp_x.xh, sp_x.xl)], [wh[:], wl[:]]]
        u_landed = [s.sem(f"u_landed{b}") for b in range(2)]
        g_landed = [s.sem(f"g_landed{b}") for b in range(2)]
        v_landed = [s.sem(f"v_landed{b}") for b in range(2)]
        hid_landed = [s.sem(f"hid_landed{b}") for b in range(2)]
        started = s.sem("started")
        u_high = s.sem("u_high")
        u_split = s.sem("u_split")
        v_high = s.sem("v_high")
        v_split = s.sem("v_split")
        h_ready = s.sem("h_ready")
        gelu_ready = s.sem("gelu_ready")
        gated_ready = s.sem("gated_ready")
        a_high = s.sem("a_high")
        a_ready = s.sem("a_ready")
        y_ready = s.sem("y_ready")
        y_free = s.sem("y_free")
        with s.block() as block:
            @block.sync
            def _(sp):
                def load_u(n, b):
                    sp.dma_start(u[:, b % 2], a["peer_u"][bass.ds(layer * NK + AHEAD + n, 1)]
                                 .rearrange("o p k e -> (o p) k e")).then_inc(u_landed[b % 2], 16)

                def load_g(grp, par):
                    at = grp + AHEAD // GB if isinstance(grp, int) and grp < FRESH else grp - FRESH
                    sp.dma_start(g[:, par], a["gates"][bass.ds(at, 1)].rearrange("o n j i t -> (o j) n (i t)")
                                 ).then_inc(g_landed[par], 16)

                def load_v(n, b, at):
                    sp.dma_start(w[:, b % 2], a["peer_v"][bass.ds(layer * NK + at, 1)].rearrange("o e d -> (o e) d")
                                 ).then_inc(v_landed[b % 2], 16)

                def load_hid(at, b):
                    sp.dma_start(act_out[:, b % 2], a["hidden"][bass.ds(at, 1)].rearrange("o p t -> (o p) t")
                                 ).then_inc(hid_landed[b % 2], 16)

                def next_v(n, b):
                    wait(sp, v_split, n + 1)
                    load_v(n + 2, b, n + 2 - GB * FRESH if not isinstance(n, int) or n + 2 >= GB * FRESH else n + 2 + AHEAD)

                load_g(0, 0)
                for b in range(2):
                    load_v(b, b, AHEAD + b)
                load_g(1, 1)
                for grp in range(FRESH):
                    for b in range(GB):
                        n = GB * grp + b
                        if n + 4 < GB * FRESH:
                            sp.wait_ge(u_split, n + 3)
                            load_u(n + 4, b)
                        if grp > 0:
                            next_v(n - GB, b)
                    sp.wait_ge(gated_ready, GB * (grp + 1))
                    load_g(grp + 2, grp % 2)
                    if grp == FRESH - 1:
                        load_hid(0, 0)
                        load_hid(1, 1)
                for b in range(GB):
                    next_v(GB * (FRESH - 1) + b, b)

                def stored(grp, par, last=False):
                    for b in range(GB):
                        n = GB * grp + b
                        if not (last and b >= 2):
                            next_v(n, b)
                            wait(sp, gated_ready, n + 1)
                            load_hid(n + 2 - GB * FRESH, b)
                    if not last:
                        load_g(grp + 2, par)

                stored(FRESH, FRESH % 2)
                with sp.Fori(FRESH // 2, NG // 2 - 2) as i:
                    stored(2 * i + 2, 0)
                    stored(2 * i + 3, 1)
                for grp in (NG - 2, NG - 1):
                    for b in range(GB):
                        n = GB * grp + b
                        if n + 2 < NK:
                            next_v(n, b)
                            sp.wait_ge(gated_ready, n + 1)
                            load_hid(n + 2 - GB * FRESH, b)

            @block.tensor
            def _(pe):
                def hidden(grp):
                    for b in range(GB):
                        n = GB * grp + b
                        pe.wait_ge(u_split, n + 1)
                        pe.wait_ge(gelu_ready, n + 1)
                        sp_x.product(pe, k, 2 * (b % 2), b % 2).then_inc(h_ready, 1)

                def output(grp, par, place):
                    vh, vl = places[place]
                    pe.wait_ge(v_split, GB * grp + GB)
                    pe.wait_ge(a_ready, GB * grp + GB)
                    for c in range(KC):
                        pe.wait_ge(y_free, KC * grp + c + 1)
                        for h in range(2):
                            o = k.ps[:, 4 + 2 * (c % 2) + h, 0:TH]
                            t = slice(h * TH, (h + 1) * TH)
                            f = slice(c * P, (c + 1) * P)
                            for b in range(GB):
                                pe.matmul(o, vl[:, b, f], gh[:, par, b, t], start=(b == 0), stop=False)
                                pe.matmul(o, vh[:, b, f], gl[:, par, b, t], start=False, stop=False)
                                mm = pe.matmul(o, vh[:, b, f], gh[:, par, b, t], start=False, stop=(b == GB - 1))
                        mm.then_inc(y_ready, 1)

                hidden(0)
                with pe.Fori(0, FRESH // 2) as i:
                    hidden(2 * i + 1)
                    output(2 * i, 0, 1)
                    hidden(2 * i + 2)
                    output(2 * i + 1, 1, 1)
                output(FRESH - 1, 0, 0)
                output(FRESH, 1, 1)
                with pe.Fori(FRESH // 2, NG // 2 - 1) as i:
                    output(2 * i + 2, 0, 0)
                    output(2 * i + 3, 1, 1)

            @block.scalar
            def _(act):
                def split_u(n, b):
                    if not isinstance(n, int) or n >= GB:
                        act.wait_ge(u_landed[b % 2], 8 * (n - b % 2) - 16)
                    act.wait_ge(h_ready, n - 1)
                    act.activation(uh[:, b % 2], u[:, b % 2], ACT.Copy).then_inc(u_high, 1)

                def split_v(n, b, place):
                    act.wait_ge(v_landed[b % 2], 8 * (n - b % 2) + 16)
                    act.activation(places[place][0][:, b], w[:, b % 2], ACT.Copy).then_inc(v_high, 1)

                def gelu(n, b):
                    act.wait_ge(h_ready, n + 1)
                    if not isinstance(n, int) or n > 1:
                        act.wait_ge(gated_ready, n - 1)
                    act.activation(halves(act_out[:, b % 2]), k.ps[:, 2 * (b % 2):2 * (b % 2) + 2, 0:TH], ACT.Gelu
                                   ).then_inc(gelu_ready, 1)

                def group(grp):
                    for b in range(GB):
                        n = GB * grp + b
                        last = isinstance(grp, int) and grp == FRESH - 1 and b >= GB - 2
                        if not last:
                            split_u(n + 2, b)
                        if b == 0 and not (isinstance(grp, int) and grp == 1):
                            act.wait_ge(y_ready, KC * (grp - 1))
                        split_v(n - GB, b, 1)
                        gelu(n, b)

                def later(grp, place):
                    act.wait_ge(y_ready, KC * (grp - 1))
                    for b in range(GB):
                        split_v(GB * grp + b, b, place)

                act.sem_inc(gelu_ready, 2)
                act.sem_inc(u_high, 2)
                for b in range(GB):
                    split_u(b + 2, b)
                    gelu(b, b)
                group(1)
                with act.Fori(1, FRESH // 2) as i:
                    group(2 * i)
                    group(2 * i + 1)
                group(FRESH - 1)
                for b in range(GB):
                    split_v(GB * (FRESH - 1) + b, b, 0)
                later(FRESH, 1)
                with act.Fori(FRESH // 2, NG // 2 - 1) as i:
                    later(2 * i + 2, 0)
                    later(2 * i + 3, 1)

            @block.vector
            def _(v):
                def split_u(n, b):
                    v.wait_ge(u_high, n + 1)
                    v.tensor_tensor(ul[:, b % 2], u[:, b % 2], uh[:, b % 2].bitcast(F32), ALU.subtract
                                    ).then_inc(u_split, 1)

                def split_v(n, b, place):
                    v.wait_ge(v_high, n + 1)
                    vh, vl = places[place]
                    v.tensor_tensor(vl[:, b], w[:, b % 2], vh[:, b].bitcast(F32), ALU.subtract).then_inc(v_split, 1)

                def gate(n, b, par):
                    if not isinstance(n, int) or n > 0:
                        v.wait_ge(a_ready, n)
                    v.tensor_tensor(gated[:].rearrange("p (n t) -> p n t", n=NT),
                                    act_out[:, b % 2].rearrange("p (n t) -> p n t", n=NT), g[:, par, :, b], ALU.mult
                                    ).then_inc(gated_ready, 1)
                    v.wait_ge(gated_ready, n + 1)
                    v.tensor_copy(gh[:, par, b], gated[:]).then_inc(a_high, 1)
                    v.wait_ge(a_high, n + 1)
                    v.tensor_tensor(gl[:, par, b], gated[:], gh[:, par, b].bitcast(F32), ALU.subtract
                                    ).then_inc(a_ready, 1)

                def collect(grp, chunks):
                    for c in chunks:
                        v.wait_ge(y_ready, KC * grp + c + 1)
                        rc = halves(r[:, c])
                        v.tensor_tensor(rc, rc, k.ps[:, 4 + 2 * (c % 2):6 + 2 * (c % 2), 0:TH], ALU.add
                                        ).then_inc(y_free, 1)

                def group(grp, par):
                    v.wait_ge(g_landed[par], 8 * (grp - par) + 16)
                    for b in range(GB):
                        n = GB * grp + b
                        last = isinstance(grp, int) and grp == FRESH - 1 and b >= GB - 2
                        if not last:
                            split_u(n + 2, b)
                        if not isinstance(grp, int) or grp > 0:
                            split_v(n - GB, b, 1)
                        v.wait_ge(gelu_ready, n + 3)
                        gate(n, b, par)

                def later(grp, par, place):
                    v.wait_ge(g_landed[par], 8 * (grp - par) + 16)
                    for b in range(GB):
                        n = GB * grp + b
                        split_v(n, b, place)
                        v.wait_ge(hid_landed[b % 2], 8 * (n - GB * FRESH - b % 2) + 16)
                        gate(n, b, par)
                        collect(grp - 1, (2 * b, 2 * b + 1))

                v.sem_inc(y_free, 2)
                v.sem_inc(u_split, 2)
                v.tensor_scalar(r[:], k.x[:], ALPHA, None, ALU.mult).then_inc(started, 1)
                v.wait_ge(started, 1)
                group(0, 0)
                group(1, 1)
                collect(0, range(KC))
                with v.Fori(1, FRESH // 2) as i:
                    group(2 * i, 0)
                    collect(2 * i - 1, range(KC))
                    group(2 * i + 1, 1)
                    collect(2 * i, range(KC))
                group(FRESH - 1, 0)
                for b in range(GB):
                    split_v(GB * (FRESH - 1) + b, b, 0)
                    collect(FRESH - 2, (2 * b, 2 * b + 1))
                later(FRESH, 1, 1)
                with v.Fori(FRESH // 2, NG // 2 - 1) as i:
                    later(2 * i + 2, 0, 0)
                    later(2 * i + 3, 1, 1)
                collect(NG - 1, range(KC))


def peer_layer(nc, k, a, layer):
    with Stage(nc, f"peer{layer}") as s:
        sp_x = Split(s)
        with Stage(nc, f"ranks{layer}") as t:
            values = t.sb("values", [TT, NT, HP, TOPK])
            ranks = t.sb("ranks", [TT, NT, HP, TOPK])
            peer_retrieve(nc, k, a, layer, sp_x, values, ranks)
            peer_gates(nc, k, a, layer, sp_x, values, ranks)
        with Stage(nc, f"peer_out{layer}") as t:
            r = t.sb("r", [P, KC, T])
            peer_experts(nc, k, a, layer, sp_x, r)
            layer_norm(nc, k, f"ln{layer}1", r, f"ln_g{layer}1", f"ln_b{layer}1", k.x, ACT.Identity)


def conv_module(nc, k, a, h, r):
    LEFT = CW - 1
    ON_PE = 3
    with Stage(nc, "conv") as s:
        y = s.sb("y", [P, KC, T])
        with Stage(nc, "convin") as t:
            linear(nc, k, "pw1", a["w_pw1"], k.x, h, 2 * KC, KC)
            ext = t.sb("ext", [P, KC, LEFT + TP])
            exts = t.sb("exts", [P, KC, TS, CW])
            old = t.sb("old", [P, KC, TS, LEFT])
            tails = t.sb("tails", [P, KC, TS, LEFT])
            prod = t.sb("prod", [P, KC, TS, CW])
            diag = t.sb("diag", [P, 2, ON_PE, P])
            landed = t.sem("landed")
            sig = t.sem("sig")
            glu = t.sem("glu")
            done = t.sem("done")
            tails_ready = t.sem("tails_ready")
            link = t.sem("link")
            stored = t.sem("stored")
            diag_ready = t.sem("diag_ready")
            diag_used = t.sem("diag_used")
            with t.block() as block:
                @block.sync
                def _(sp):
                    sp.dma_start(old[:], a["state_conv"]).then_inc(landed, 16)
                    sp.wait_ge(tails_ready, 1)
                    sp.dma_start(a["new_conv_s"], tails[:]).then_inc(stored, 16)
                    sp.dma_start(a["new_conv_p"], ext[:, :, TP:TP + LEFT]).then_inc(stored, 16)
                    sp.wait_ge(stored, 32)

                @block.tensor
                def _(pe):
                    def tap(j, b, last=False):
                        for c in range(ON_PE):
                            pe.wait_ge(diag_ready, ON_PE * j + c + 1)
                            first = isinstance(j, int) and j == 0
                            if first:
                                pe.wait_ge(glu, c + 1)
                            pe.matmul(k.ps[:, c, :], diag[:, b, c], ext[:, c, bass.ds(j, TP)], start=first, stop=last
                                      ).then_inc(diag_used, 1)

                    tap(0, 0)
                    with pe.Fori(0, CW // 2 - 1) as i:
                        tap(2 * i + 1, 1)
                        tap(2 * i + 2, 0)
                    tap(CW - 2, 1)
                    tap(CW - 1, 0, True)

                @block.scalar
                def _(act):
                    def diagonals(j, b):
                        for c in range(ON_PE):
                            if not isinstance(j, int) or j > 1:
                                act.wait_ge(diag_used, ON_PE * (j - 2) + c + 1)
                            act.activation(diag[:, b, c], k.ident[:], ACT.Copy,
                                           scale=k.vec[:, bass.ds(j + (VEC["w_dw"] + c * CW), 1)]).then_inc(diag_ready, 1)

                    for c in range(KC):
                        act.activation(h[:, KC + c], h[:, KC + c], ACT.Sigmoid, bias=k.col("b_pw1", KC + c)).then_inc(sig, 1)
                        if c == ON_PE - 1:
                            diagonals(0, 0)
                            diagonals(1, 1)
                    with act.Fori(1, CW // 2) as i:
                        diagonals(2 * i, 0)
                        diagonals(2 * i + 1, 1)
                    diagonals(CW - 1, 0)
                    act.wait_ge(diag_used, ON_PE * CW)
                    for c in range(ON_PE):
                        act.activation(y[:, c, 0:TP], k.ps[:, c, :], ACT.Identity, bias=k.col("b_dw", c))

                @block.vector
                def _(v):
                    chain = Chain(v, link)
                    mine = range(ON_PE, KC)
                    v.memset(ext[:, :, 0:LEFT], 0.0)
                    for c in range(KC):
                        v.wait_ge(sig, c + 1)
                        b = k.col("b_pw1", c)
                        v.scalar_tensor_tensor(exts[:, c, :, LEFT], h[:, c, TP:T], b, h[:, KC + c, TP:T], ALU.add, ALU.mult)
                        v.scalar_tensor_tensor(ext[:, c, LEFT:LEFT + TP], h[:, c, 0:TP], b, h[:, KC + c, 0:TP], ALU.add, ALU.mult
                                               ).then_inc(glu, 1)
                    v.wait_ge(landed, 16)
                    chain(v.tensor_copy(exts[:, :, :, 0:LEFT], old[:]))
                    v.wait_ge(glu, KC)
                    v.tensor_copy(tails[:], exts[:, :, :, 1:CW]).then_inc(tails_ready, 1)
                    for c in range(KC):
                        w = k.vec[:, VEC["w_dw"] + c * CW:VEC["w_dw"] + (c + 1) * CW]
                        ins = v.tensor_tensor(prod[:, c], exts[:, c], bc(w, 1, TS), ALU.mult)
                    chain(ins)
                    chain(v.tensor_reduce(y[:, :, TP:T], prod[:], AX.X, ALU.add))
                    v.tensor_tensor(y[:, :, TP:T], y[:, :, TP:T], bc(k.vec[:, VEC["b_dw"]:VEC["b_dw"] + KC], 2, TS), ALU.add)
                    for c in mine:
                        v.tensor_scalar(y[:, c, 0:TP], ext[:, c, 0:TP], k.col("w_dw", c * CW), k.col("b_dw", c), ALU.mult, ALU.add
                                        ).then_inc(done, 1)
                    with v.Fori(1, CW) as j:
                        for c in mine:
                            o = y[:, c, 0:TP]
                            v.wait_ge(done, (KC - ON_PE) * (j - 1) + c - ON_PE + 1)
                            v.scalar_tensor_tensor(o, ext[:, c, bass.ds(j, TP)],
                                                   k.vec[:, bass.ds(j + (VEC["w_dw"] + c * CW), 1)], o, ALU.mult, ALU.add
                                                   ).then_inc(done, 1)
        act_in = s.sb("act", [P, KC, T])
        layer_norm(nc, k, "cln", y, "cln_g", "cln_b", act_in, ACT.Silu)
        linear(nc, k, "pw2", a["w_pw2"], act_in, r, KC, KC, residual=True, bias="b_pw2")


def build(nc, a):
    with ExitStack() as ctx:
        k = Kept(nc, ctx)
        load_constants(nc, a, k)
        for layer, mix in enumerate((mixer, conv_module)):
            with Stage(nc, f"layer{layer}") as s:
                wide = s.sb("wide", [P, 18, T])
                r = wide[:, 0:KC]
                mix(nc, k, a, wide, r)
                layer_norm(nc, k, f"ln{layer}0", r, f"ln_g{layer}0", f"ln_b{layer}0", k.x, ACT.Identity)
            peer_layer(nc, k, a, layer)
        with Stage(nc, "store") as s:
            stored = s.sem("stored")
            with s.block() as block:
                @block.sync
                def _(sp):
                    sp.dma_start(a["y"], k.x[:]).then_inc(stored, 16)
                    sp.wait_ge(stored, 16)


_OUTS = {"y": (P, KC, T), "new_lat": (P, CC, T), "new_kpe": (ROPE, T), "new_hgrn_p": (P, H, P),
         "new_hgrn_s": (TS, P, H, P), "new_conv_p": (P, KC, CW - 1), "new_conv_s": (P, KC, TS, CW - 1)}
_SCRATCH = {"gates": (NG, NT, NK, GB, TT), "hidden": (AHEAD, P, T)}


def _slabs(w):
    i, o = w.shape
    return w.reshape(i // P, P, o // P, P).transpose(2, 1, 0, 3)


def _rows(w):
    return w.reshape(w.shape[0] // P, P, -1).transpose(1, 0, 2)


def _layout(i):
    swap = np.r_[ROPE // 2:ROPE, 0:ROPE // 2]
    x = np.concatenate([i["x_prompt"].reshape(TP, D), i["x_sample"].reshape(TS, D)])
    w_in = i["mix_w_in"][0]
    kr = w_in[:, 2048 + QL + KVL:]
    w_mix = np.concatenate([w_in[:, 0:1024], w_in[:, 1536:2048], w_in[:, 2048:2048 + QL + KVL], kr, kr[:, swap]], axis=1)
    uq = i["mla_w_uq"][0].reshape(QL, H, P + ROPE)
    w_uq = np.concatenate([uq[:, :, :P].reshape(QL, -1), uq[:, :, P:].reshape(QL, -1), uq[:, :, P:][:, :, swap].reshape(QL, -1)], axis=1)
    ukv = i["mla_w_ukv"][0]
    half = ROPE // 2
    inv = np.float32(10000.0) ** (-np.arange(half, dtype=np.float32) / np.float32(half))
    pos = np.r_[0:TP, [PAST] * TS].astype(np.float32)
    ang = (pos[:, None] * inv[None, :]).astype(np.float32).astype(np.float64)
    cos, sin = np.cos(ang).T.astype(np.float32), np.sin(ang).T.astype(np.float32)
    s_, t_ = np.arange(P)[:, None], np.arange(P)[None, :]
    masks = [s_ == t_] + [(s_ // (2 * m) == t_ // (2 * m)) & (s_ % (2 * m) < m) & (t_ % (2 * m) >= m)
                          for m in (1 << n for n in range(LEVELS - 1))]

    lat_t = i["cache_mla_latent"][0].reshape(POOL_PAGES, PAGE, CC, P).transpose(0, 3, 2, 1).reshape(POOL_PAGES, P, KVL)
    rope_t = np.pad(i["cache_mla_krope"][0].transpose(0, 2, 1), ((0, 0), (0, P - ROPE), (0, 0)))

    def cols(w):
        return w.reshape(-1, P).T

    vec = [cols(i["ln_g"][l, j]) for l in range(2) for j in range(2)] + [cols(i["ln_b"][l, j]) for l in range(2) for j in range(2)]
    vec += [cols(i["conv_b_pw1"][0]), cols(i["conv_b_dw"][0]), cols(i["conv_ln_g"][0]), cols(i["conv_ln_b"][0]),
            cols(i["conv_b_pw2"][0]), cols(i["mla_q_norm"][0]), cols(i["mla_kv_norm"][0]), cols(i["hg_out_norm"][0]),
            cols(i["hg_lb_logits"]), i["conv_w_dw"][0].reshape(CW, KC, P).transpose(2, 1, 0).reshape(P, -1)]
    return {
        "x_t": _rows(x.T),
        "vecs": np.concatenate(vec, axis=1),
        "masks": np.stack(masks, axis=1).astype(np.uint32),
        "cos": np.concatenate([cos, cos]),
        "sin": np.concatenate([-sin, sin]),
        "w_mix": _slabs(w_mix),
        "w_val": _rows(w_in[:, 1024:1536]),
        "w_uq": _rows(w_uq),
        "w_uk": ukv[:, :, :P].transpose(2, 1, 0),
        "w_uv": ukv[:, :, P:].reshape(CC, P, H, P).transpose(1, 2, 0, 3),
        "w_mix_out": _slabs(i["mix_w_out"][0]),
        "page_table": i["page_table"].reshape(1, -1),
        "cache": np.concatenate([lat_t, rope_t, i["cache_mla_latent"][0]], axis=2),
        "state_hgrn": i["state_hgrn"][0].transpose(0, 2, 1, 3),
        "state_conv": i["state_conv"][0].reshape(TS, CW - 1, KC, P).transpose(3, 2, 0, 1),
        "w_pw1": _slabs(i["conv_w_pw1"][0]),
        "w_pw2": _slabs(i["conv_w_pw2"][0]),
        "peer_wq": np.stack([_slabs(w) for w in i["peer_w_q"]]),
        "peer_keys": i["peer_sub_keys"].transpose(0, 4, 2, 1, 3).reshape(2, P, HP, NK),
        "peer_u": i["peer_u"].reshape(2 * NK, P, KC, P).transpose(0, 3, 2, 1),
        "peer_v": i["peer_v"].reshape(2 * NK, P, D),
    }


def kernel(**inputs):
    import concourse.bacc as bacc
    from concourse.bass_utils import run_bass_kernel_spmd

    nc = bacc.Bacc("TRN2", target_bir_lowering=False, num_devices=1)
    arrays = {n: np.ascontiguousarray(z) for n, z in _layout({n: np.asarray(z) for n, z in inputs.items()}).items()}
    a = {n: nc.dram_tensor(n, z.shape, mybir.dt.from_np(z.dtype), kind="ExternalInput").ap() for n, z in arrays.items()}
    for n, shape in _OUTS.items():
        a[n] = nc.dram_tensor(n, shape, F32, kind="ExternalOutput").ap()
    for n, shape in _SCRATCH.items():
        a[n] = nc.dram_tensor(n, shape, F32).ap()
    build(nc, a)
    o = run_bass_kernel_spmd(nc, [arrays], core_ids=[0]).results[0]
    tok = [o[n].transpose(2, 1, 0).reshape(T, -1) for n in ("y", "new_lat")] + [o["new_kpe"].T]
    prompt = [z[:TP] for z in tok]
    sample = [z[TP:].reshape(TS, 1, -1) for z in tok]
    out = (prompt[0][None], sample[0], prompt[1][None, None], prompt[2][None, None],
           o["new_hgrn_p"].transpose(1, 0, 2)[None, None],
           o["new_conv_p"].transpose(2, 1, 0).reshape(1, 1, CW - 1, D),
           sample[1][None], sample[2][None], o["new_hgrn_s"].transpose(0, 2, 1, 3)[None],
           o["new_conv_s"].transpose(2, 3, 1, 0).reshape(1, TS, CW - 1, D))
    return tuple(np.ascontiguousarray(z) for z in out)
```

```python
from contextlib import ExitStack

import concourse.bass as bass
import numpy as np
from concourse import mybir

F32 = mybir.dt.float32
F32R = mybir.dt.float32r
U32 = mybir.dt.uint32
I32 = mybir.dt.int32
ALU = mybir.AluOpType
ACT = mybir.ActivationFunctionType
AX = mybir.AxisListType

P = 128
D = 1024
KC = D // P
TP, TS = 512, 8
T = TP + TS
TH = T // 2
TT, NT = 104, 5
H = 4
CL, NCH = 128, 4
QL, KVL, ROPE = 384, 256, 64
QC, CC = QL // P, KVL // P
PAST, PAGE = 2048, 128
NPG = PAST // PAGE
POOL_PAGES = 160
MIX = 4 * H + QC + CC + 1
CW = 31
PH = 8
NK = 128
HP = 2 * PH
TOPK = 16
CANDA, CANDB = 4, 12
NCAND = CANDA * 16 + CANDB * 4
NEG = -3.0e38
ALPHA = 4.0 ** 0.25
SCALE = float(128 + ROPE) ** -0.5
LN_EPS, RMS_EPS = 1e-5, 1e-6
LEVELS = 8
GB = 4
NG = NK // GB
SELECT, PER_TILE = 8, 20
EXTRA = SELECT
AHEAD = PER_TILE * NT + EXTRA
FRESH = (NK - AHEAD) // GB

VEC = {}
_at = 0
for _name, _n in (("ln_g00", KC), ("ln_g01", KC), ("ln_g10", KC), ("ln_g11", KC),
                  ("ln_b00", KC), ("ln_b01", KC), ("ln_b10", KC), ("ln_b11", KC),
                  ("b_pw1", 2 * KC), ("b_dw", KC), ("cln_g", KC), ("cln_b", KC), ("b_pw2", KC),
                  ("q_norm", QC), ("kv_norm", CC), ("out_norm", 1), ("lb", 3 * H), ("w_dw", CW * KC)):
    VEC[_name] = _at
    _at += _n
NVEC = _at


def bc(ap, axis, n):
    a = ap.unsqueeze(axis)
    shape = list(a.shape)
    shape[axis] = n
    return a.broadcast_to(shape)


def halves(ap):
    return ap.rearrange("p (a t) -> p a t", a=2)


def wait(eng, sem, value):
    eng.wait_ge(sem, value)
    if not isinstance(value, int):
        eng.nop(nofuse=True)


class Chain:

    def __init__(self, eng, sem):
        self.eng, self.sem, self.n = eng, sem, 0

    def __call__(self, ins, base=0):
        self.n += 1
        ins.then_inc(self.sem, 1)
        wait(self.eng, self.sem, base + self.n)


class Stage:

    def __init__(self, nc, name):
        self.nc, self.name, self.ctx, self.sems = nc, name, ExitStack(), []

    def __enter__(self):
        self.ctx.__enter__()
        return self

    def __exit__(self, *a):
        if self.sems and a[0] is None:
            self.nc.clear_and_free_semaphores(self.sems)
            self.nc.all_engine_barrier()
        return self.ctx.__exit__(*a)

    def sb(self, name, shape, dt=F32):
        return self.ctx.enter_context(self.nc.sbuf_tensor(f"{self.name}_{name}", shape, dt))

    def sem(self, name):
        self.sems.append(self.nc.alloc_semaphore(name=f"{self.name}_{name}"))
        return self.sems[-1]

    def block(self):
        return self.nc.Block()


def load_ahead(sp, loads, fetched):
    for dst, src in loads:
        sp.dma_start(dst, src).then_inc(fetched, 16)
    sp.wait_ge(fetched, 16 * len(loads))


def slabs(k, w):
    return [(k.ring[:, b], w[b]) for b in range(2)]


def load_constants(nc, a, k):
    with Stage(nc, "load") as s:
        landed = s.sem("landed")
        zeroed = s.sem("zeroed")
        filled = s.sem("filled")
        with s.block() as block:
            @block.sync
            def _(sp):
                sp.dma_start(k.x[:], a["x_t"]).then_inc(landed, 16)
                sp.dma_start(k.ring[:, 0], a["w_mix"][0]).then_inc(landed, 16)
                sp.dma_start(k.vec[:], a["vecs"]).then_inc(landed, 16)
                sp.dma_start(k.ring[:, 1], a["w_mix"][1]).then_inc(landed, 16)
                sp.wait_ge(landed, 64)

            @block.vector
            def _(v):
                v.memset(k.mean_d[:], 1.0 / D)
                v.memset(k.ones[:], 1.0)

            @block.gpsimd
            def _(g):
                g.memset(k.ident[:], 0.0).then_inc(zeroed, 1)
                g.wait_ge(zeroed, 1)
                g.affine_select(out=k.ident[:], in_=k.ident[:], compare_op=ALU.not_equal, fill=1.0, base=0,
                                pattern=[[-1, P]], channel_multiplier=1).then_inc(filled, 1)
                g.iota(k.iota[:], pattern=[[1, P]], base=0, channel_multiplier=0,
                       allow_small_or_imprecise_dtypes=True).then_inc(filled, 1)
                g.wait_ge(filled, 2)


def linear(nc, k, name, w, rhs, out, m, kc, residual=False, bias=None):
    with Stage(nc, name) as s:
        slab = k.ring
        slab_h = s.sb("slab_h", [P, 2, kc, P], F32R)
        slab_l = s.sb("slab_l", [P, 2, kc, P], F32R)
        rhs_h = s.sb("rhs_h", [P, kc, T], F32R)
        rhs_l = s.sb("rhs_l", [P, kc, T], F32R)
        landed = [s.sem(f"landed{b}") for b in range(2)]
        rhs_high = s.sem("rhs_high")
        rhs_split = s.sem("rhs_split")
        slab_high = s.sem("slab_high")
        slab_split = s.sem("slab_split")
        summed = s.sem("summed")
        psum_free = s.sem("psum_free")
        scaled = s.sem("scaled")
        with s.block() as block:
            @block.sync
            def _(sp):
                for b in range(2):
                    sp.sem_inc(landed[b], 16)
                with sp.Fori(0, m // 2 - 1) as i:
                    for b in range(2):
                        wait(sp, slab_split, 2 * i + b + 1)
                        sp.dma_start(slab[:, b], w[bass.ds(2 * i + 2 + b, 1)].rearrange("o p k m -> (o p) k m")
                                     ).then_inc(landed[b], 16)

            @block.tensor
            def _(pe):
                with pe.Fori(0, m // 2) as i:
                    for b in range(2):
                        pe.wait_ge(slab_split, 2 * i + b + 1)
                        pe.wait_ge(psum_free, 2 * i + b + 1)
                        for h in range(2):
                            o = k.ps[:, 2 * b + h, 0:TH]
                            t = slice(h * TH, (h + 1) * TH)
                            for c in range(kc):
                                if b == 0 and h == 0:
                                    pe.wait_ge(rhs_split, c + 1)
                                pe.matmul(o, slab_l[:, b, c], rhs_h[:, c, t], start=(c == 0), stop=False)
                                pe.matmul(o, slab_h[:, b, c], rhs_l[:, c, t], start=False, stop=False)
                                mm = pe.matmul(o, slab_h[:, b, c], rhs_h[:, c, t], start=False, stop=(c == kc - 1))
                        mm.then_inc(summed, 1)

            @block.scalar
            def _(act):
                def high(i, b):
                    act.wait_ge(landed[b], 16 * i + 16)
                    act.activation(slab_h[:, b], slab[:, b], ACT.Copy).then_inc(slab_high, 1)

                high(0, 0)
                for c in range(kc):
                    act.activation(rhs_h[:, c], rhs[:, c], ACT.Copy).then_inc(rhs_high, 1)
                if residual:
                    act.activation(out[:], k.x[:], ACT.Copy, scale=ALPHA).then_inc(scaled, 1)
                high(0, 1)
                with act.Fori(1, m // 2) as i:
                    for b in range(2):
                        act.wait_ge(summed, 2 * i + b - 1)
                        high(i, b)

            @block.vector
            def _(v):
                def low(i, b):
                    v.wait_ge(slab_high, 2 * i + b + 1)
                    v.tensor_tensor(slab_l[:, b], slab[:, b], slab_h[:, b].bitcast(F32), ALU.subtract
                                    ).then_inc(slab_split, 1)

                def collect(i, b):
                    o = halves(out[:, bass.ds(2 * i + b, 1), :].rearrange("p o t -> p (o t)"))
                    banks = k.ps[:, 2 * b:2 * b + 2, 0:TH]
                    v.wait_ge(summed, 2 * i + b + 1)
                    if bias is not None:
                        at = VEC[bias] + 2 * i + b
                        ins = v.scalar_tensor_tensor(o, banks, k.vec[:, bass.ds(at, 1)], o, ALU.add, ALU.add)
                    elif residual:
                        ins = v.tensor_tensor(o, banks, o, ALU.add)
                    else:
                        ins = v.tensor_copy(o, banks)
                    ins.then_inc(psum_free, 1)

                v.sem_inc(psum_free, 2)
                low(0, 0)
                for c in range(kc):
                    v.wait_ge(rhs_high, c + 1)
                    v.tensor_tensor(rhs_l[:, c], rhs[:, c], rhs_h[:, c].bitcast(F32), ALU.subtract).then_inc(rhs_split, 1)
                low(0, 1)
                if residual:
                    v.wait_ge(scaled, 1)
                with v.Fori(0, m // 2 - 1) as i:
                    for b in range(2):
                        collect(i, b)
                        low(i + 1, b)
                for b in range(2):
                    collect(m // 2 - 1, b)


def inverse_root(chain, var, root, tmp):
    v = chain.eng
    chain(v.reciprocal(root, root))
    chain(v.scalar_tensor_tensor(tmp, root, -0.5, root, ALU.mult, ALU.mult))
    chain(v.tensor_tensor(tmp, tmp, var, ALU.mult))
    chain(v.scalar_tensor_tensor(root, tmp, 1.5, root, ALU.add, ALU.mult))


def layer_norm(nc, k, name, r, g, b, out, func, ahead=()):
    with Stage(nc, name) as s:
        sq = s.sb("sq", [P, KC, T])
        var = s.sb("var", [P, T])
        rstd = s.sb("rstd", [P, T])
        newton = s.sb("newton", [P, T])
        mean_ready = s.sem("mean_ready")
        centred = s.sem("centred")
        squared = s.sem("squared")
        var_ready = s.sem("var_ready")
        var_copied = s.sem("var_copied")
        rooted = s.sem("rooted")
        link = s.sem("link")
        normed = s.sem("normed")
        fetched = s.sem("fetched")
        part = [slice(h * TH, (h + 1) * TH) for h in range(2)]
        with s.block() as block:
            if ahead:
                @block.sync
                def _(sp):
                    load_ahead(sp, ahead, fetched)

            @block.tensor
            def _(pe):
                for h in range(2):
                    for c in range(KC):
                        mm = pe.matmul(k.ps[:, h, 0:TH], k.mean_d[:], r[:, c, part[h]], start=(c == 0), stop=(c == KC - 1))
                    mm.then_inc(mean_ready, 1)
                for h in range(2):
                    for c in range(KC):
                        if c % 2 == 0:
                            pe.wait_ge(squared, KC // 2 * h + c // 2 + 1)
                        mm = pe.matmul(k.ps[:, 2 + h, 0:TH], k.mean_d[:], sq[:, c, part[h]],
                                       start=(c == 0), stop=(c == KC - 1))
                    mm.then_inc(var_ready, 1)

            @block.vector
            def _(v):
                chain = Chain(v, link)

                def centre(h):
                    v.wait_ge(mean_ready, h + 1)
                    for c in range(0, KC, 2):
                        rh = r[:, c:c + 2, part[h]]
                        v.tensor_tensor(rh, rh, bc(k.ps[:, h, 0:TH], 1, 2), ALU.subtract).then_inc(centred, 1)

                centre(0)
                centre(1)
                for h in range(2):
                    v.wait_ge(var_ready, h + 1)
                    v.tensor_scalar(var[:, part[h]], k.ps[:, 2 + h, 0:TH], LN_EPS, None, ALU.add).then_inc(var_copied, 1)
                    v.wait_ge(rooted, h + 1)
                    inverse_root(chain, var[:, part[h]], rstd[:, part[h]], newton[:, part[h]])
                    for c in range(0, KC, 2):
                        rh = r[:, c:c + 2, part[h]]
                        v.tensor_tensor(rh, rh, bc(rstd[:, part[h]], 1, 2), ALU.mult).then_inc(normed, 1)

            @block.scalar
            def _(act):
                def root(h):
                    act.wait_ge(var_copied, h + 1)
                    act.activation(rstd[:, part[h]], var[:, part[h]], ACT.Sqrt).then_inc(rooted, 1)

                def affine(h, c):
                    act.activation(out[:, c, part[h]], r[:, c, part[h]], func, bias=k.col(b, c), scale=k.col(g, c))

                for h in range(2):
                    for c in range(0, KC, 2):
                        act.wait_ge(centred, KC // 2 * h + c // 2 + 1)
                        act.activation(sq[:, c:c + 2, part[h]], r[:, c:c + 2, part[h]], ACT.Square).then_inc(squared, 1)
                root(0)
                root(1)
                for h in range(2):
                    for c in range(KC):
                        act.wait_ge(normed, KC // 2 * h + c // 2 + 1)
                        affine(h, c)


class Kept:

    def __init__(self, nc, ctx):
        def sb(name, shape, dt=F32):
            return ctx.enter_context(nc.sbuf_tensor(name, shape, dt))

        self.x = sb("x", [P, KC, T])
        self.vec = sb("vec", [P, NVEC])
        self.mean_d = sb("mean_d", [P, P])
        self.ones = sb("ones", [P, P])
        self.ident = sb("ident", [P, P])
        self.iota = sb("iota", [P, P])
        self.ring = sb("ring", [P, 2, KC, P])
        self.ps = ctx.enter_context(nc.psum_tensor("ps", [P, 8, 512], F32))

    def col(self, name, j=0):
        at = VEC[name] + j
        return self.vec[:, at:at + 1]


def turn_values(nc, k, proj, vt, vs):
    with Stage(nc, "values") as s:
        turned = s.sem("turned")
        with s.block() as block:
            @block.tensor
            def _(pe):
                for t in range(NCH + 1):
                    n = CL if t < NCH else TS
                    for h in range(H):
                        mm = pe.transpose(k.ps[0:n, t, h * P:(h + 1) * P], proj[:, MIX - H + h, t * CL:t * CL + n], k.ident[:])
                    mm.then_inc(turned, 1)

            @block.vector
            def _(v):
                for t in range(0, NCH, 2):
                    v.wait_ge(turned, t + 2)
                    v.tensor_copy(vt[:, t:t + 2, :], k.ps[:, t:t + 2, :])
                v.wait_ge(turned, NCH + 1)
                v.tensor_copy(vs[:], k.ps[0:TS, NCH, :])


def recurrence(nc, k, a, proj, vt, vs, cat):
    with Stage(nc, "rec") as s:
        f = s.sb("f", [P, H, T])
        kk = s.sb("k", [P, H, T])
        pre = s.sb("pre", [P, H, TP])
        suf = s.sb("suf", [P, H, TP])
        kd = s.sb("kd", [P, 2, H, TP])
        qd = s.sb("qd", [P, 2, H, TP])
        attn = s.sb("attn", [P, H, NCH, CL])
        masks = s.sb("masks", [P, LEVELS, CL], U32)
        lb = s.sb("lb", [P, 6, H])
        kt = s.sb("kt", [P, H, NCH, P])
        state = s.sb("state", [P, H, P])
        q = proj[:, 0:H]
        gate = proj[:, 2 * H:3 * H]
        landed = s.sem("landed")
        link = s.sem("link")
        lb_e = s.sem("lb_e")
        lb_m = s.sem("lb_m")
        sig = s.sem("sig")
        q_copied = s.sem("q_copied")
        cleared = s.sem("cleared")
        decayed = s.sem("decayed")
        level_ready = s.sem("level_ready")
        level_read = s.sem("level_read")
        turned = s.sem("turned")
        kt_ready = s.sem("kt_ready")
        chunk_ready = s.sem("chunk_ready")
        chunk_read = s.sem("chunk_read")
        stored = s.sem("stored")
        with s.block() as block:
            @block.sync
            def _(sp):
                sp.dma_start(masks[:], a["masks"]).then_inc(landed, 16)
                sp.wait_ge(chunk_read, NCH)
                sp.dma_start(a["new_hgrn_p"], state[:]).then_inc(stored, 16)
                sp.wait_ge(stored, 16)

            @block.scalar
            def _(act):
                act.wait_ge(lb_m, 1)
                act.activation(lb[:, 0:3], lb[:, 0:3], ACT.Exp).then_inc(lb_e, 1)
                act.activation(f[:], proj[:, H:2 * H], ACT.Sigmoid).then_inc(sig, 1)
                act.activation(kk[:], proj[:, H:2 * H], ACT.Sigmoid, scale=-1.0).then_inc(sig, 1)
                act.activation(qd[:, 0], q[:, :, 0:TP], ACT.Copy).then_inc(q_copied, 1)
                act.activation(gate, gate, ACT.Silu)

            @block.gpsimd
            def _(pool):
                pool.memset(suf[:], 1.0).then_inc(cleared, 1)
                pool.memset(attn[:], 0.0).then_inc(cleared, 1)

            @block.vector
            def _(v):
                chain = Chain(v, link)
                logit = k.vec[:, VEC["lb"]:VEC["lb"] + 3 * H].rearrange("p (l h) -> p l h", l=3)
                chain(v.tensor_tensor(lb[:, 3], logit[:, 0], logit[:, 1], ALU.max))
                chain(v.tensor_tensor(lb[:, 3], lb[:, 3], logit[:, 2], ALU.max))
                v.tensor_tensor(lb[:, 0:3], logit, bc(lb[:, 3], 1, 3), ALU.subtract).then_inc(lb_m, 1)
                v.wait_ge(lb_e, 1)
                chain(v.tensor_tensor(lb[:, 3], lb[:, 0], lb[:, 1], ALU.add))
                chain(v.tensor_tensor(lb[:, 3], lb[:, 3], lb[:, 2], ALU.add))
                chain(v.reciprocal(lb[:, 3], lb[:, 3]))
                chain(v.tensor_tensor(lb[:, 4], lb[:, 0], lb[:, 3], ALU.mult))
                chain(v.tensor_scalar(lb[:, 5], lb[:, 4], -1.0, 1.0, ALU.mult, ALU.add))
                v.wait_ge(sig, 1)
                for h in range(H):
                    v.tensor_scalar(f[:, h], f[:, h], lb[:, 5, h:h + 1], lb[:, 4, h:h + 1], ALU.mult, ALU.add)
                v.wait_ge(sig, 2)
                for h in range(H):
                    ins = v.tensor_scalar(kk[:, h], kk[:, h], lb[:, 5, h:h + 1], None, ALU.mult)
                chain(ins)
                v.tensor_copy(kd[:, 0], kk[:, :, 0:TP]).then_inc(decayed, 1)
                chain(v.tensor_copy(pre[:], f[:, :, 0:TP]))
                v.wait_ge(cleared, 2)
                v.wait_ge(landed, 16)

                def take(level):
                    v.wait_ge(level_ready, level + 1)
                    into = attn[:].rearrange("s h c t -> s (h c) t")
                    mask = bc(masks[:, level], 1, H * NCH)
                    new = k.ps[:, 4 * (level % 2):4 * (level % 2) + 4, :].rearrange("s h (c t) -> s (h c) t", t=CL)
                    if level:
                        m = 1 << (level - 1)
                        into, mask, new = (z.rearrange("s g (n b) -> s g n b", b=2 * m)[:, :, :, m:2 * m]
                                           for z in (into, mask, new))
                    v.copy_predicated(into, mask, new).then_inc(level_read, 1)

                for level in range(1, LEVELS + 1):
                    m = 1 << (level - 1)
                    if level > 1:
                        hf = m // 2
                        v.wait_ge(decayed, level)
                        p2 = pre[:].rearrange("p h (n m) -> p (h n) m", m=m)
                        s2 = suf[:].rearrange("p h (n m) -> p (h n) m", m=m)
                        chain(v.tensor_tensor(s2[:, :, 0:hf], s2[:, :, 0:hf], bc(p2[:, :, m - 1], 2, hf), ALU.mult))
                        chain(v.tensor_tensor(p2[:, :, hf:m], p2[:, :, hf:m], bc(p2[:, :, hf - 1], 2, hf), ALU.mult))
                    if level >= 2:
                        v.wait_ge(level_ready, level - 1)
                    ks = qs = slice(0, 2 * m if level < LEVELS else m)
                    if 1 < level < LEVELS:
                        ks, qs = slice(0, m), slice(m, 2 * m)
                    block_of = 2 * m if level < LEVELS else m
                    kdv, kkv, sv, qdv, qv, pv = (z.rearrange("p h (n b) -> p h n b", b=block_of) for z in (
                        kd[:, level % 2], kk[:, :, 0:TP], suf[:], qd[:, level % 2], q[:, :, 0:TP], pre[:]))
                    v.tensor_tensor(kdv[:, :, :, ks], kkv[:, :, :, ks], sv[:, :, :, ks], ALU.mult)
                    v.tensor_tensor(qdv[:, :, :, qs], qv[:, :, :, qs], pv[:, :, :, qs], ALU.mult).then_inc(decayed, 1)
                    take(level - 1)
                v.wait_ge(turned, 1)
                v.tensor_copy(kt[:].rearrange("s h c d -> s (h c d)"), k.ps[:, 0:4, :].rearrange("s b d -> s (b d)")
                              ).then_inc(kt_ready, 1)
                for c in range(NCH):
                    v.wait_ge(chunk_ready, c + 1)
                    bank = 4 + 2 * (c % 2)
                    v.tensor_copy(cat[:, 0:H, c * CL:(c + 1) * CL], k.ps[:, bank, :].rearrange("p (h t) -> p h t", h=H))
                    new = k.ps[:, bank + 1, :].rearrange("p (h d) -> p h d", h=H)
                    if c == 0:
                        v.tensor_copy(state[:], new).then_inc(chunk_read, 1)
                    else:
                        last = pre[:].rearrange("p h (c t) -> p h c t", t=CL)[:, :, c, CL - 1]
                        chain(v.tensor_tensor(state[:], state[:], bc(last, 2, P), ALU.mult))
                        v.tensor_tensor(state[:], state[:], new, ALU.add).then_inc(chunk_read, 1)
                    v.wait_ge(chunk_read, c + 1)

            @block.tensor
            def _(pe):
                for level in range(LEVELS):
                    pe.wait_ge(decayed, level + 1)
                    pe.wait_ge(q_copied, 1)
                    if level >= 2:
                        pe.wait_ge(level_read, level - 1)
                    for h in range(H):
                        for c in range(NCH):
                            t = slice(c * CL, (c + 1) * CL)
                            mm = pe.matmul(k.ps[:, 4 * (level % 2) + h, t], kd[:, level % 2, h, t], qd[:, level % 2, h, t],
                                           start=True, stop=True)
                    mm.then_inc(level_ready, 1)
                pe.wait_ge(decayed, LEVELS + 1)
                pe.wait_ge(level_read, LEVELS)
                for h in range(H):
                    for c in range(NCH):
                        t = slice(c * CL, (c + 1) * CL)
                        mm = pe.transpose(k.ps[:, h, t], kd[:, 0, h, t], k.ident[:])
                mm.then_inc(turned, 1)
                pe.wait_ge(kt_ready, 1)
                for c in range(NCH):
                    bank = 4 + 2 * (c % 2)
                    if c:
                        pe.wait_ge(chunk_read, c)
                    for h in range(H):
                        o = k.ps[:, bank, h * CL:(h + 1) * CL]
                        pe.matmul(o, vt[:, c, h * P:(h + 1) * P], attn[:, h, c], start=True, stop=(c == 0))
                        if c:
                            pe.matmul(o, state[:, h], qd[:, 0, h, c * CL:(c + 1) * CL], start=False, stop=True)
                        mm = pe.matmul(k.ps[:, bank + 1, h * P:(h + 1) * P], kt[:, h, c], vt[:, c, h * P:(h + 1) * P],
                                       start=True, stop=True)
                    mm.then_inc(chunk_ready, 1)

        old = s.sb("old", [P, 2, H, P])
        new = s.sb("new", [P, 2, H, P])
        kv = s.sb("kv", [P, H, P])
        old_landed = [s.sem(f"old_landed{b}") for b in range(2)]
        new_stored = [s.sem(f"new_stored{b}") for b in range(2)]
        v_spread = s.sem("v_spread")
        step = s.sem("step")
        new_ready = s.sem("new_ready")
        read_out = s.sem("read_out")
        with s.block() as block:
            @block.sync
            def _(sp):
                for b in range(2):
                    sp.dma_start(old[:, b], a["state_hgrn"][b]).then_inc(old_landed[b], 16)
                for n in range(TS):
                    sp.wait_ge(new_ready, n + 1)
                    sp.dma_start(a["new_hgrn_s"][n], new[:, n % 2]).then_inc(new_stored[n % 2], 16)
                    if n + 2 < TS:
                        sp.dma_start(old[:, n % 2], a["state_hgrn"][n + 2]).then_inc(old_landed[n % 2], 16)
                for b in range(2):
                    sp.wait_ge(new_stored[b], 16 * TS // 2)

            @block.tensor
            def _(pe):
                def spread(n):
                    pe.matmul(k.ps[:, n % 2, :], k.ident[0:TS, n:n + 1].broadcast_to([TS, P]), vs[:],
                              start=True, stop=True).then_inc(v_spread, 1)

                spread(0)
                spread(1)
                for n in range(TS):
                    pe.wait_ge(new_ready, n + 1)
                    if n + 2 < TS:
                        spread(n + 2)
                    for h in range(H):
                        mm = pe.matmul(k.ps[:, 2, n * H + h:n * H + h + 1], new[:, n % 2, h],
                                       q[:, h, TP + n:TP + n + 1], start=True, stop=True)
                    mm.then_inc(read_out, 1)

            @block.vector
            def _(v):
                chain = Chain(v, step)
                for n in range(TS):
                    v.wait_ge(v_spread, n + 1)
                    v.wait_ge(old_landed[n % 2], n // 2 * 16 + 16)
                    if n >= 2:
                        v.wait_ge(new_stored[n % 2], (n // 2) * 16)
                        v.wait_ge(read_out, n - 1)
                    chain(v.tensor_tensor(kv[:], k.ps[:, n % 2, :].rearrange("p (h d) -> p h d", h=H),
                                          bc(kk[:, :, TP + n], 2, P), ALU.mult))
                    chain(v.tensor_tensor(new[:, n % 2], old[:, n % 2], bc(f[:, :, TP + n], 2, P), ALU.mult))
                    v.tensor_tensor(new[:, n % 2], new[:, n % 2], kv[:], ALU.add).then_inc(new_ready, 1)
                    v.wait_ge(new_ready, n + 1)
                v.wait_ge(read_out, TS)
                v.tensor_copy(cat[:, 0:H, TP:T], k.ps[:, 2, 0:TS * H].rearrange("p (n h) -> p h n", h=H))


def norms(nc, k, proj, cat, ckv, ahead):
    GP = 16
    CQ = 3 * H
    norm_of = list(range(H)) + [H] * QC + [H + 1] * CC
    sizes = [P] * H + [QL, KVL]
    with Stage(nc, "norms") as s:
        sq = s.sb("sq", [P, len(norm_of), T])
        mean = s.sb("mean", [P, len(sizes), P])
        var = s.sb("var", [P, T])
        rstd = s.sb("rstd", [P, T])
        newton = s.sb("newton", [P, T])
        masked = s.sem("masked")
        squared = s.sem("squared")
        summed = s.sem("summed")
        copied = s.sem("copied")
        rooted = s.sem("rooted")
        link = s.sem("link")
        inverse = s.sem("inverse")
        spread = s.sem("spread")
        used = s.sem("used")
        fetched = s.sem("fetched")
        with s.block() as block:
            @block.sync
            def _(sp):
                load_ahead(sp, ahead, fetched)

            @block.scalar
            def _(act):
                act.activation(sq[:, 0:H], cat[:, 0:H], ACT.Square).then_inc(squared, 1)
                act.activation(sq[:, H:], proj[:, CQ:CQ + QC + CC], ACT.Square).then_inc(squared, 1)
                act.wait_ge(copied, 1)
                act.activation(rstd[:], var[:], ACT.Sqrt).then_inc(rooted, 1)

            @block.tensor
            def _(pe):
                pe.wait_ge(masked, 1)
                pe.wait_ge(squared, 1)
                for h in range(2):
                    for j, n in enumerate(norm_of):
                        if h == 0 and j == H:
                            pe.wait_ge(squared, 2)
                        mm = pe.matmul(k.ps[:, h, 0:TH], mean[:, n], sq[:, j, h * TH:(h + 1) * TH],
                                       start=(j == 0), stop=(j == len(norm_of) - 1))
                mm.then_inc(summed, 1)
                pe.wait_ge(inverse, 1)
                for n in range(len(sizes)):
                    if n >= 4:
                        pe.wait_ge(used, n - 3)
                    for h in range(2):
                        mm = pe.matmul(k.ps[:, 2 * (n % 4) + h, 0:TH], k.ident[:, GP * n:GP * n + 1].broadcast_to([P, P]),
                                       rstd[:, h * TH:(h + 1) * TH], start=True, stop=True)
                    mm.then_inc(spread, 1)

            @block.vector
            def _(v):
                chain = Chain(v, link)
                chain(v.memset(mean[:], 0.0))
                for n, size in enumerate(sizes):
                    ins = v.memset(mean[:, n, GP * n:GP * (n + 1)], 1.0 / size)
                ins.then_inc(masked, 1)
                v.wait_ge(summed, 1)
                v.tensor_scalar(halves(var[:]), k.ps[:, 0:2, 0:TH], RMS_EPS, None, ALU.add).then_inc(copied, 1)
                v.wait_ge(rooted, 1)
                inverse_root(chain, var[:], rstd[:], newton[:])
                v.sem_inc(inverse, 1)
                for n in range(len(sizes)):
                    v.wait_ge(spread, n + 1)
                    root = k.ps[:, 2 * (n % 4):2 * (n % 4) + 2, 0:TH]
                    if n < H:
                        pairs = [(cat[:, n], cat[:, n], "out_norm", 0)]
                    elif n == H:
                        pairs = [(proj[:, CQ + c], proj[:, CQ + c], "q_norm", c) for c in range(QC)]
                    else:
                        pairs = [(ckv[:, c], proj[:, CQ + QC + c], "kv_norm", c) for c in range(CC)]
                    for o, x, g, c in pairs:
                        ins = v.scalar_tensor_tensor(halves(o), halves(x), k.col(g, c), root, ALU.mult, ALU.mult)
                    ins.then_inc(used, 1)
                for h in range(H):
                    v.wait_ge(used, h + 1)
                    v.tensor_tensor(cat[:, h], cat[:, h], proj[:, 2 * H + h], ALU.mult)


def latent_queries(nc, k, a, proj, wuq, wuk, qabs, qpe, kpe, ckv):
    with Stage(nc, "lq") as s:
        cq = proj[:, 3 * H:3 * H + QC]
        qn = s.sb("qn", [P, H, T])
        cos = s.sb("cos", [ROPE, T])
        sin = s.sb("sin", [ROPE, T])
        swapped = s.sb("swapped", [ROPE, T])
        rot = s.sb("rot", [ROPE, T])
        tables = s.sem("tables")
        ready = s.sem("ready")
        free = s.sem("free")
        link = s.sem("link")
        abs_ready = s.sem("abs_ready")
        abs_free = s.sem("abs_free")
        k_ready = s.sem("k_ready")
        stored = s.sem("stored")
        with s.block() as block:
            @block.sync
            def _(sp):
                sp.dma_start(cos[:], a["cos"]).then_inc(tables, 16)
                sp.dma_start(sin[:], a["sin"]).then_inc(tables, 16)
                sp.dma_start(swapped[:], proj[ROPE:P, 3 * H + QC + CC, :]).then_inc(tables, 16)
                sp.dma_start(a["new_lat"], ckv[:]).then_inc(stored, 16)
                sp.wait_ge(k_ready, 1)
                sp.dma_start(a["new_kpe"], kpe[:]).then_inc(stored, 16)
                sp.wait_ge(stored, 32)

            @block.tensor
            def _(pe):
                n = 0
                for h in range(H):
                    if n >= 2:
                        pe.wait_ge(free, n - 1)
                    for b in range(2):
                        for c in range(QC):
                            mm = pe.matmul(k.ps[:, 2 * (n % 2) + b, 0:TH], wuq[:, c, h * P:(h + 1) * P],
                                           cq[:, c, b * TH:(b + 1) * TH], start=(c == 0), stop=(c == QC - 1))
                    mm.then_inc(ready, 1)
                    n += 1
                for h in range(H):
                    for sw in range(2):
                        pe.wait_ge(free, n - 1)
                        at = H * P + sw * H * ROPE + h * ROPE
                        for b in range(2):
                            for c in range(QC):
                                mm = pe.matmul(k.ps[0:ROPE, 2 * (n % 2) + b, 0:TH], wuq[:, c, at:at + ROPE],
                                               cq[:, c, b * TH:(b + 1) * TH], start=(c == 0), stop=(c == QC - 1))
                        mm.then_inc(ready, 1)
                        n += 1
                pe.wait_ge(free, H)
                for h in range(H):
                    for c in range(CC):
                        m = CC * h + c
                        if m >= 2:
                            pe.wait_ge(abs_free, m - 1)
                        for b in range(2):
                            mm = pe.matmul(k.ps[:, 4 + 2 * (m % 2) + b, 0:TH], wuk[:, h, c * P:(c + 1) * P],
                                           qn[:, h, b * TH:(b + 1) * TH], start=True, stop=True)
                        mm.then_inc(abs_ready, 1)

            @block.scalar
            def _(act):
                for m in range(H * CC):
                    act.wait_ge(abs_ready, m + 1)
                    act.copy(halves(qabs[:, m // CC, m % CC]), k.ps[:, 4 + 2 * (m % 2):6 + 2 * (m % 2), 0:TH]
                             ).then_inc(abs_free, 1)

            @block.vector
            def _(v):
                chain = Chain(v, link)
                v.wait_ge(tables, 48)
                kr = proj[0:ROPE, 3 * H + QC + CC]
                v.tensor_tensor(kpe[:], kr, cos[:], ALU.mult)
                chain(v.tensor_tensor(rot[:], swapped[:], sin[:], ALU.mult))
                v.tensor_tensor(kpe[:], kpe[:], rot[:], ALU.add).then_inc(k_ready, 1)
                for h in range(H):
                    v.wait_ge(ready, h + 1)
                    v.tensor_copy(halves(qn[:, h]), k.ps[:, 2 * (h % 2):2 * (h % 2) + 2, 0:TH]).then_inc(free, 1)
                for h in range(H):
                    v.wait_ge(ready, H + 2 * h + 1)
                    v.tensor_tensor(halves(qpe[:, h]), k.ps[0:ROPE, 0:2, 0:TH], halves(cos[:]), ALU.mult).then_inc(free, 1)
                    v.wait_ge(ready, H + 2 * h + 2)
                    v.tensor_tensor(halves(rot[:]), k.ps[0:ROPE, 2:4, 0:TH], halves(sin[:]), ALU.mult).then_inc(free, 1)
                    v.wait_ge(free, H + 2 * h + 2)
                    chain(v.tensor_tensor(qpe[:, h], qpe[:, h], rot[:], ALU.add))


def attention(nc, k, a, qabs, qpe, kpe, ckv, proj):
    olat = proj[:, 0:H * CC].rearrange("p (h c) t -> p h c t", h=H)
    sc = proj[:, 2 * H:3 * H, 0:512]
    prob = proj[:, 3 * H:4 * H, 0:512]
    ctok = proj[:, 5 * H:5 * H + 2].rearrange("p c t -> p (c t)")[:, 0:NCH * KVL].rearrange("p (n f) -> p n f", n=NCH)
    pt = proj[:, 4 * H:5 * H, 0:512]
    NS = TS * H
    WT = KVL + PAGE
    with Stage(nc, "pa") as s:
        mask = s.sb("mask", [P, 512])
        mx = s.sb("mx", [P, H])
        total = s.sb("total", [P, H])
        pages = s.sb("pages", [1, TS * NPG], I32)
        ct = s.sb("ct", [P, 2, NPG, WT + KVL])
        qa = s.sb("qa", [P, CC, TS, H])
        qp = s.sb("qp", [ROPE, TS, H])
        prod = s.sb("prod", [P, CC + 1, TS, H])
        snew = s.sb("snew", [P, TS, H])
        smx = s.sb("smx", [P, 2, H])
        mrow = s.sb("mrow", [2 * H, 1])
        mdiag = s.sb("mdiag", [2 * H, 2 * H])
        sprob = s.sb("sprob", [P, 2, NPG, H])
        pnew = s.sb("pnew", [P, 2, H])
        part = s.sb("part", [P, 2, H])
        rec = s.sb("rec", [P, 2, H])
        add = s.sb("add", [P, CC, 2, H])
        rows = s.sb("rows", [H, 2 * KVL])
        zeroed = s.sem("zeroed")
        masked = s.sem("masked")
        c_turned = s.sem("c_turned")
        c_ready = s.sem("c_ready")
        s_ready = s.sem("s_ready")
        s_read = s.sem("s_read")
        mx_ready = s.sem("mx_ready")
        exped = s.sem("exped")
        p_ready = s.sem("p_ready")
        p_turned = s.sem("p_turned")
        pt_ready = s.sem("pt_ready")
        o_ready = s.sem("o_ready")
        o_read = s.sem("o_read")
        link = s.sem("link")
        page_list = s.sem("page_list")
        pages_landed = [s.sem(f"pages_landed{b}") for b in range(2)]
        q_ready = s.sem("q_ready")
        prod_ready = s.sem("prod_ready")
        new_ready = s.sem("new_ready")
        new_read = s.sem("new_read")
        scored = s.sem("scored")
        smx_ready = s.sem("smx_ready")
        mx_turned = s.sem("mx_turned")
        diag_ready = s.sem("diag_ready")
        spread = s.sem("spread")
        shifted = s.sem("shifted")
        sexped = s.sem("sexped")
        part_ready = s.sem("part_ready")
        sum_ready = s.sem("sum_ready")
        weighed = s.sem("weighed")
        rows_ready = s.sem("rows_ready")
        rows_turned = s.sem("rows_turned")
        pair_done = s.sem("pair_done")
        UNR = 4

        def fetch(eng, n, first):
            b = n % 2
            if n >= 2:
                eng.wait_ge(weighed, n - 1)
            with eng.Fori(first // UNR, (first + NPG // 2) // UNR) as p:
                page = [eng.value_load(pages[0:1, bass.ds(UNR * p + (NPG * n + j), 1)], min_val=0, max_val=POOL_PAGES - 1)
                        for j in range(UNR)]
                for j in range(UNR):
                    eng.dma_start(ct[:, b, bass.ds(UNR * p + j, 1)].rearrange("k o f -> k (o f)"),
                                  a["cache"][bass.ds(page[j], 1)].rearrange("o k f -> (o k) f")
                                  ).then_inc(pages_landed[b], 16)

        with s.block() as block:
            @block.gpsimd
            def _(pool):
                pool.memset(mask[:], 0.0).then_inc(zeroed, 1)
                pool.wait_ge(zeroed, 1)
                pool.affine_select(out=mask[:, 384:512], in_=mask[:, 384:512], compare_op=ALU.is_ge, fill=NEG, base=0,
                                   pattern=[[-1, P]], channel_multiplier=1).then_inc(masked, 1)

            @block.sync
            def _(sp):
                sp.dma_start(pages[:], a["page_table"]).then_inc(page_list, 16)
                sp.wait_ge(page_list, 16)
                for n in range(TS):
                    fetch(sp, n, 0)

            @block.tensor
            def _(pe):
                def prompt_scores(qb):
                    w = (qb + 1) * P
                    qs = slice(qb * P, w)
                    if qb:
                        pe.wait_ge(o_read, qb)
                    for h in range(H):
                        o = k.ps[:, h, 0:w]
                        for c in range(CC):
                            pe.matmul(o, qabs[:, h, c, qs], ckv[:, c, 0:w], start=(c == 0), stop=False)
                        mm = pe.matmul(o, qpe[:, h, qs], kpe[:, 0:w], start=False, stop=True)
                    mm.then_inc(s_ready, 1)

                def pair(qb):
                    for b in range(2):
                        n = 2 * qb + b
                        pe.wait_ge(pages_landed[b], 16 * NPG * (qb + 1))
                        for p in range(NPG):
                            at = (b * NPG + p) * H
                            o = k.ps[:, 4, at:at + H]
                            for c in range(CC):
                                pe.matmul(o, ct[:, b, p, c * PAGE:(c + 1) * PAGE], qa[:, c, n, :], start=(c == 0), stop=False)
                            mm = pe.matmul(o, ct[0:ROPE, b, p, KVL:WT], qp[:, n, :], start=False, stop=True)
                    mm.then_inc(scored, 1)
                    pe.wait_ge(smx_ready, qb + 1)
                    pe.transpose(k.ps[0:2 * H, 5, 0:P], smx[:].rearrange("p n h -> p (n h)"), k.ident[:]).then_inc(mx_turned, 1)
                    pe.wait_ge(diag_ready, qb + 1)
                    pe.matmul(k.ps[:, 5, P:P + 2 * H], k.ones[0:2 * H, :], mdiag[:], start=True, stop=True).then_inc(spread, 1)
                    pe.wait_ge(sexped, 2 * qb + 2)
                    for b in range(2):
                        for p in range(NPG):
                            mm = pe.matmul(k.ps[0:H, 6, b * KVL:(b + 1) * KVL], sprob[:, b, p, :], ct[:, b, p, WT:WT + KVL],
                                           start=(p == 0), stop=(p == NPG - 1))
                        mm.then_inc(weighed, 1)
                    pe.wait_ge(part_ready, qb + 1)
                    pe.matmul(k.ps[:, 7, 0:2 * H], k.ones[:], part[:].rearrange("p n h -> p (n h)"), start=True, stop=True
                              ).then_inc(sum_ready, 1)
                    pe.wait_ge(rows_ready, qb + 1)
                    for b in range(2):
                        for c in range(CC):
                            at = 2 * P + (c * 2 + b) * H
                            mm = pe.transpose(k.ps[:, 5, at:at + H], rows[:, b * KVL + c * P:b * KVL + (c + 1) * P],
                                              k.ident[0:H, 0:H])
                    mm.then_inc(rows_turned, 1)

                for c in range(CC):
                    for t in range(NCH):
                        mm = pe.transpose(k.ps[:, 4 + c, t * P:(t + 1) * P], ckv[:, c, t * P:(t + 1) * P], k.ident[:])
                mm.then_inc(c_turned, 1)
                prompt_scores(0)
                pe.wait_ge(prod_ready, 1)
                for c in range(CC):
                    pe.matmul(k.ps[:, 6, 0:NS], k.ones[:], prod[:, c].rearrange("p n h -> p (n h)"),
                              start=(c == 0), stop=False)
                pe.matmul(k.ps[:, 6, 0:NS], k.ones[0:ROPE, :], prod[0:ROPE, CC].rearrange("p n h -> p (n h)"),
                          start=False, stop=True).then_inc(new_ready, 1)
                for qb in range(NCH):
                    pe.wait_ge(p_ready, qb + 1)
                    pe.wait_ge(c_ready, 1)
                    pe.wait_ge(new_read, 1)
                    if qb:
                        pe.wait_ge(pair_done, qb)
                    for h in range(H):
                        for kb in range(qb + 1):
                            mm = pe.transpose(k.ps[:, 4 + h, kb * P:(kb + 1) * P], prob[:, h, kb * P:(kb + 1) * P], k.ident[:])
                    mm.then_inc(p_turned, 1)
                    pe.wait_ge(pt_ready, qb + 1)
                    for h in range(H):
                        for c in range(CC):
                            for kb in range(qb + 1):
                                mm = pe.matmul(k.ps[:, h, c * P:(c + 1) * P], ctok[:, kb, c * P:(c + 1) * P],
                                               pt[:, h, kb * P:(kb + 1) * P], start=(kb == 0), stop=(kb == qb))
                    mm.then_inc(o_ready, 1)
                    if qb < NCH - 1:
                        prompt_scores(qb + 1)
                    pair(qb)

            @block.vector
            def _(v):
                chain = Chain(v, link)

                def prompt_max(qb):
                    w = (qb + 1) * P
                    v.wait_ge(s_ready, qb + 1)
                    v.tensor_tensor(sc[:, :, 0:w], k.ps[:, 0:H, 0:w], bc(mask[:, 512 - w:512], 1, H), ALU.add
                                    ).then_inc(s_read, 1)
                    v.wait_ge(s_read, qb + 1)
                    chain(v.tensor_reduce(mx[:], sc[:, :, 0:w], AX.X, ALU.max))
                    v.tensor_scalar(mx[:], mx[:], -SCALE, None, ALU.mult).then_inc(mx_ready, 1)

                def prompt_probs(qb):
                    w = (qb + 1) * P
                    v.wait_ge(exped, qb + 1)
                    chain(v.reciprocal(total[:], total[:]))
                    v.tensor_tensor(prob[:, :, 0:w], prob[:, :, 0:w], bc(total[:], 2, w), ALU.mult).then_inc(p_ready, 1)

                def pair(qb):
                    sscore = k.ps[:, 4, 0:2 * NPG * H].rearrange("p (n g h) -> p n g h", n=2, g=NPG)
                    new = snew[:, 2 * qb:2 * qb + 2]
                    v.wait_ge(scored, qb + 1)
                    v.tensor_reduce(smx[:], sscore.rearrange("p n g h -> p n h g"), AX.X, ALU.max).then_inc(smx_ready, 1)
                    v.wait_ge(mx_turned, qb + 1)
                    chain(v.tensor_reduce(mrow[:], k.ps[0:2 * H, 5, 0:P], AX.X, ALU.max))
                    v.tensor_scalar(mdiag[:], k.ident[0:2 * H, 0:2 * H], mrow[:], None, ALU.mult).then_inc(diag_ready, 1)
                    v.wait_ge(spread, qb + 1)
                    chain(v.tensor_tensor(smx[:], new, k.ps[:, 5, P:P + 2 * H].rearrange("p (n h) -> p n h", n=2), ALU.max))
                    v.tensor_tensor(sprob[:], sscore, bc(smx[:], 2, NPG), ALU.subtract)
                    v.tensor_tensor(pnew[:], new, smx[:], ALU.subtract).then_inc(shifted, 1)
                    if qb < NCH - 1:
                        prompt_probs(qb + 1)
                    v.wait_ge(sexped, 2 * qb + 2)
                    v.tensor_reduce(part[:], sprob[:].rearrange("p n g h -> p n h g"), AX.X, ALU.add).then_inc(part_ready, 1)
                    for c in range(CC):
                        ins = v.tensor_tensor(add[:, c], pnew[:], bc(ckv[:, c, TP + 2 * qb:TP + 2 * qb + 2], 2, H), ALU.mult)
                    chain(ins)
                    v.wait_ge(weighed, 2 * qb + 2)
                    v.tensor_copy(rows[:], k.ps[0:H, 6, :]).then_inc(rows_ready, 1)
                    v.wait_ge(sum_ready, qb + 1)
                    chain(v.tensor_tensor(rec[:], pnew[:], k.ps[:, 7, 0:2 * H].rearrange("p (n h) -> p n h", n=2), ALU.add))
                    chain(v.reciprocal(rec[:], rec[:]))
                    v.wait_ge(rows_turned, qb + 1)
                    chain(v.tensor_tensor(add[:], add[:], k.ps[:, 5, 2 * P:2 * P + 2 * CC * H]
                                          .rearrange("p (c n h) -> p c n h", c=CC, h=H), ALU.add))
                    v.tensor_tensor(olat.rearrange("p h c t -> p c t h")[:, :, TP + 2 * qb:TP + 2 * qb + 2, :], add[:],
                                    bc(rec[:], 1, CC), ALU.mult).then_inc(pair_done, 1)

                v.wait_ge(c_turned, 1)
                v.tensor_copy(ctok.rearrange("t n (c f) -> t c n f", c=CC),
                              k.ps[:, 4:6, :].rearrange("t c (n f) -> t c n f", n=NCH)).then_inc(c_ready, 1)
                v.tensor_copy(qa[:].rearrange("p c n h -> p c h n"),
                              qabs[:].rearrange("p h c t -> p c h t")[:, :, :, TP:T])
                v.tensor_copy(qp[:].rearrange("p n h -> p h n"), qpe[:, :, TP:T]).then_inc(q_ready, 1)
                v.wait_ge(q_ready, 1)
                for c in range(CC):
                    v.tensor_tensor(prod[:, c], qa[:, c], bc(ckv[:, c, TP:T], 2, H), ALU.mult)
                v.tensor_tensor(prod[0:ROPE, CC], qp[:], bc(kpe[:, TP:T], 2, H), ALU.mult).then_inc(prod_ready, 1)
                v.wait_ge(masked, 1)
                prompt_max(0)
                v.wait_ge(new_ready, 1)
                v.tensor_copy(snew[:].rearrange("p n h -> p (n h)"), k.ps[:, 6, 0:NS]).then_inc(new_read, 1)
                prompt_probs(0)
                for qb in range(NCH):
                    w = (qb + 1) * P
                    v.wait_ge(p_turned, qb + 1)
                    v.tensor_copy(pt[:, :, 0:w], k.ps[:, 4:4 + H, 0:w]).then_inc(pt_ready, 1)
                    v.wait_ge(o_ready, qb + 1)
                    v.tensor_copy(olat[:, :, :, qb * P:(qb + 1) * P],
                                  k.ps[:, 0:H, 0:CC * P].rearrange("p h (c q) -> p h c q", c=CC)).then_inc(o_read, 1)
                    if qb < NCH - 1:
                        prompt_max(qb + 1)
                    pair(qb)

            @block.scalar
            def _(act):
                def prompt_exp(qb):
                    w = (qb + 1) * P
                    act.wait_ge(mx_ready, qb + 1)
                    if qb:
                        act.wait_ge(p_turned, qb)
                    for h in range(H):
                        ins = act.activation(prob[:, h, 0:w], sc[:, h, 0:w], ACT.Exp, bias=mx[:, h:h + 1], scale=SCALE,
                                             accum_out=total[:, h:h + 1])
                    ins.then_inc(exped, 1)

                act.wait_ge(page_list, 16)
                for b in range(2):
                    fetch(act, b, NPG // 2)
                prompt_exp(0)
                for qb in range(NCH):
                    if qb < NCH - 1:
                        prompt_exp(qb + 1)
                    act.wait_ge(shifted, qb + 1)
                    act.activation(sprob[:], sprob[:], ACT.Exp, scale=SCALE).then_inc(sexped, 1)
                    act.activation(pnew[:], pnew[:], ACT.Exp, scale=SCALE).then_inc(sexped, 1)
                    if qb < NCH - 1:
                        for b in range(2):
                            fetch(act, 2 * qb + 2 + b, NPG // 2)


def latent_values(nc, k, a, olat, cat):
    with Stage(nc, "lv") as s:
        w = s.sb("w", [P, H, CC, P])
        landed = s.sem("landed")
        fetched = s.sem("fetched")
        ready = s.sem("ready")
        with s.block() as block:
            @block.sync
            def _(sp):
                sp.dma_start(w[:], a["w_uv"]).then_inc(landed, 16)
                load_ahead(sp, slabs(k, a["w_mix_out"]), fetched)

            @block.tensor
            def _(pe):
                pe.wait_ge(landed, 16)
                for h in range(H):
                    for b in range(2):
                        for c in range(CC):
                            mm = pe.matmul(k.ps[:, 2 * h + b, 0:TH], w[:, h, c], olat[:, h, c, b * TH:(b + 1) * TH],
                                           start=(c == 0), stop=(c == CC - 1))
                    mm.then_inc(ready, 1)

            @block.vector
            def _(v):
                for h in range(H):
                    v.wait_ge(ready, h + 1)
                    v.tensor_copy(halves(cat[:, H + h]), k.ps[:, 2 * h:2 * h + 2, 0:TH])


def mixer(nc, k, a, proj, r):
    with Stage(nc, "mixer") as s:
        cat = s.sb("cat", [P, 2 * H, T])
        linear(nc, k, "mix_in", a["w_mix"], k.x, proj, MIX, KC)
        with Stage(nc, "hg") as t:
            vt = t.sb("vt", [P, NCH, H * P])
            vs = t.sb("vs", [TS, H * P])
            turn_values(nc, k, proj, vt, vs)
            recurrence(nc, k, a, proj, vt, vs, cat)
        with Stage(nc, "mla") as t:
            ckv = t.sb("ckv", [P, CC, T])
            kpe = t.sb("kpe", [ROPE, T])
            qabs = t.sb("qabs", [P, H, CC, T])
            qpe = t.sb("qpe", [ROPE, H, T])
            with Stage(nc, "uq") as u:
                wuq = u.sb("wuq", [P, QC, 2 * H * P])
                wuk = u.sb("wuk", [P, H, KVL])
                norms(nc, k, proj, cat, ckv, [(wuq[:], a["w_uq"]), (wuk[:], a["w_uk"])])
                latent_queries(nc, k, a, proj, wuq, wuk, qabs, qpe, kpe, ckv)
            olat = proj[:, 0:H * CC].rearrange("p (h c) t -> p h c t", h=H)
            attention(nc, k, a, qabs, qpe, kpe, ckv, proj)
            latent_values(nc, k, a, olat, cat)
        linear(nc, k, "mix_out", a["w_mix_out"], cat, r, KC, KC, residual=True)


class Split:

    def __init__(self, s):
        self.xh = s.sb("xh", [P, KC, T], F32R)
        self.xl = s.sb("xl", [P, KC, T], F32R)
        self.u = s.sb("u", [P, 2, KC, P])
        self.uh = s.sb("uh", [P, 2, KC, P], F32R)
        self.ul = s.sb("ul", [P, 2, KC, P], F32R)

    def product(self, pe, k, bank, b):
        for h in range(2):
            o = k.ps[:, bank + h, 0:TH]
            t = slice(h * TH, (h + 1) * TH)
            for c in range(KC):
                pe.matmul(o, self.ul[:, b, c], self.xh[:, c, t], start=(c == 0), stop=False)
                pe.matmul(o, self.uh[:, b, c], self.xl[:, c, t], start=False, stop=False)
                mm = pe.matmul(o, self.uh[:, b, c], self.xh[:, c, t], start=False, stop=(c == KC - 1))
        return mm


def peer_retrieve(nc, k, a, layer, sp_x, values, ranks):
    with Stage(nc, f"retrieve{layer}") as s:
        w = a["peer_wq"][layer]
        slab = k.ring
        slab_h = s.sb("slab_h", [P, 2, KC, P], F32R)
        slab_l = s.sb("slab_l", [P, 2, KC, P], F32R)
        q = s.sb("q", [P, 2, T])
        keys = s.sb("keys", [P, HP, NK])
        rest = s.sb("rest", [TT, NT, NK])
        top = s.sb("top", [TT, NT, TOPK])
        topi = s.sb("topi", [TT, NT, TOPK], U32)
        landed = [s.sem(f"landed{b}") for b in range(2)]
        keys_landed = s.sem("keys_landed")
        fetched = s.sem("fetched")
        slab_high = s.sem("slab_high")
        slab_split = s.sem("slab_split")
        summed = s.sem("summed")
        x_high = s.sem("x_high")
        q_copied = s.sem("q_copied")
        score_free = s.sem("score_free")
        score_ready = s.sem("score_ready")
        link = s.sem("link")
        x_split = s.sem("x_split")
        score = [k.ps[0:TT, 4 + 2 * b:6 + 2 * b, :].rearrange("t a n -> t (a n)")[:, 0:NT * NK]
                 .rearrange("t (n m) -> t n m", m=NK) for b in range(2)]
        with s.block() as block:
            @block.sync
            def _(sp):
                for b in range(2):
                    sp.sem_inc(landed[b], 16)
                sp.dma_start(keys[:], a["peer_keys"][layer]).then_inc(keys_landed, 16)
                load_ahead(sp, [(sp_x.u[:, b], a["peer_u"][layer * NK + b]) for b in range(2)], fetched)
                with sp.Fori(0, HP // 2 - 1) as i:
                    for b in range(2):
                        wait(sp, slab_split, 2 * i + b + 1)
                        sp.dma_start(slab[:, b], w[bass.ds(2 * i + 2 + b, 1)].rearrange("o p k m -> (o p) k m")
                                     ).then_inc(landed[b], 16)

            @block.tensor
            def _(pe):
                def project(i, b):
                    pe.wait_ge(slab_split, 2 * i + b + 1)
                    pe.wait_ge(q_copied, 2 * i + b + 1)
                    for h in range(2):
                        o = k.ps[:, 2 * b + h, 0:TH]
                        t = slice(h * TH, (h + 1) * TH)
                        for c in range(KC):
                            if isinstance(i, int) and i == 0 and b == 0 and h == 0:
                                pe.wait_ge(x_split, c + 1)
                            pe.matmul(o, slab_l[:, b, c], sp_x.xh[:, c, t], start=(c == 0), stop=False)
                            pe.matmul(o, slab_h[:, b, c], sp_x.xl[:, c, t], start=False, stop=False)
                            mm = pe.matmul(o, slab_h[:, b, c], sp_x.xh[:, c, t], start=False, stop=(c == KC - 1))
                    mm.then_inc(summed, 1)

                def scores(i, b):
                    n = 2 * i + b
                    pe.wait_ge(q_copied, n + 3)
                    pe.wait_ge(score_free, n + 1)
                    for t in range(NT):
                        mm = pe.matmul(score[b][:, t], q[:, b, t * TT:(t + 1) * TT],
                                       keys[:, bass.ds(n, 1) if not isinstance(n, int) else slice(n, n + 1), :]
                                       .rearrange("p o n -> p (o n)"), start=True, stop=True)
                    mm.then_inc(score_ready, 1)

                pe.wait_ge(keys_landed, 16)
                project(0, 0)
                with pe.Fori(0, HP // 2 - 1) as i:
                    project(i, 1)
                    scores(i, 0)
                    project(i + 1, 0)
                    scores(i, 1)
                project(HP // 2 - 1, 1)
                scores(HP // 2 - 1, 0)
                scores(HP // 2 - 1, 1)

            @block.scalar
            def _(act):
                act.sem_inc(q_copied, 2)
                act.sem_inc(score_ready, 2)

                def high(i, b):
                    act.wait_ge(landed[b], 16 * i + 16)
                    act.activation(slab_h[:, b], slab[:, b], ACT.Copy).then_inc(slab_high, 1)

                high(0, 0)
                for c in range(KC):
                    act.activation(sp_x.xh[:, c], k.x[:, c], ACT.Copy).then_inc(x_high, 1)
                high(0, 1)

                def turn(i, last=False):
                    for b in range(2):
                        act.wait_ge(summed, 2 * i + b + 1)
                        if not last:
                            high(i + 1, b)
                        act.wait_ge(score_ready, 2 * i + b + 1)
                        act.activation(halves(q[:, b]), k.ps[:, 2 * b:2 * b + 2, 0:TH], ACT.Copy).then_inc(q_copied, 1)

                with act.Fori(0, HP // 2 - 1) as i:
                    turn(i)
                turn(HP // 2 - 1, True)

            @block.vector
            def _(v):
                v.sem_inc(score_free, 2)

                def low(i, b):
                    v.wait_ge(slab_high, 2 * i + b + 1)
                    v.tensor_tensor(slab_l[:, b], slab[:, b], slab_h[:, b].bitcast(F32), ALU.subtract
                                    ).then_inc(slab_split, 1)

                low(0, 0)
                for c in range(KC):
                    v.wait_ge(x_high, c + 1)
                    v.tensor_tensor(sp_x.xl[:, c], k.x[:, c], sp_x.xh[:, c].bitcast(F32), ALU.subtract).then_inc(x_split, 1)
                low(0, 1)

                def search(i, splits=2):
                    chain = Chain(v, link)
                    base = 8 * i
                    for b in range(2):
                        sc = score[b]
                        wait(v, score_ready, 2 * i + b + 3)
                        for t in range(NT):
                            ins = v.max(top[:, t, 0:8], sc[:, t])
                        chain(ins, base)
                        for t in range(NT):
                            v.max_index(topi[:, t, 0:8], top[:, t, 0:8], sc[:, t])
                            ins = v.match_replace(rest[:, t], top[:, t, 0:8], sc[:, t], NEG)
                            if t == NT - 1:
                                ins.then_inc(score_free, 1)
                        wait(v, score_free, 2 * i + b + 3)
                        for t in range(NT):
                            ins = v.max(top[:, t, 8:16], rest[:, t])
                        chain(ins, base)
                        for t in range(NT):
                            ins = v.max_index(topi[:, t, 8:16], top[:, t, 8:16], rest[:, t])
                        n = bass.ds(2 * i + b, 1)
                        v.tensor_copy(values[:, :, n, :].rearrange("t n o r -> t n (o r)"), top[:])
                        if b < splits:
                            low(i + 1 + b, 1 - b)
                        chain(ins, base)
                        chain(v.tensor_copy(ranks[:, :, n, :].rearrange("t n o r -> t n (o r)"), topi[:]), base)
                    assert chain.n == 8

                low(1, 0)
                with v.Fori(0, HP // 2 - 2) as i:
                    search(i)
                search(HP // 2 - 2, 1)
                search(HP // 2 - 1, 0)


def peer_gates(nc, k, a, layer, sp_x, values, ranks):
    with Stage(nc, f"gates{layer}") as s:
        cand = s.sb("cand", [TT, PH, NCAND])
        rest = s.sb("rest", [TT, PH, NCAND])
        best = s.sb("best", [TT, PH, TOPK])
        expd = s.sb("expd", [TT, PH, TOPK])
        pos = s.sb("pos", [TT, PH, TOPK], U32)
        part = s.sb("part", [TT, PH, TOPK], U32)
        shift = s.sb("shift", [TT, 2, PH, TOPK], U32)
        is_b = s.sb("is_b", [TT, PH, TOPK])
        ra = s.sb("ra", [TT, PH, TOPK])
        rb = s.sb("rb", [TT, PH, TOPK])
        pick = s.sb("pick", [TT, 2, PH * TOPK, TOPK])
        ijg = s.sb("ijg", [TT, 3, PH * TOPK])
        total = s.sb("total", [TT, PH])
        cols = s.sb("cols", [P, 3, TT])
        onej = s.sb("onej", [P, 2, 4, NK])
        onei = s.sb("onei", [P, 2, 4, NK])
        g = s.sb("g", [P, NK, TT])
        hid = s.sb("hid", [P, 2, T])
        link = s.sem("link")
        centred = s.sem("centred")
        exped = s.sem("exped")
        ijg_ready = s.sem("ijg_ready")
        turned = s.sem("turned")
        one_ready = s.sem("one_ready")
        g_ready = s.sem("g_ready")
        g_free = s.sem("g_free")
        g_stored = s.sem("g_stored")
        u_landed = [s.sem(f"u_landed{b}") for b in range(2)]
        u_high = s.sem("u_high")
        u_split = s.sem("u_split")
        h_ready = s.sem("h_ready")
        gelu_ready = s.sem("gelu_ready")
        hid_stored = [s.sem(f"hid_stored{b}") for b in range(2)]
        turn = k.ps[:, 2, 0:3 * TT].rearrange("p (c t) -> p c t", c=3)
        iota16 = k.iota[0:TT, 0:TOPK]
        banks = TT // 4
        rounds = (PER_TILE - SELECT) // 2
        assert banks == 4 * rounds + 2
        with s.block() as block:
            @block.vector
            def _(v):
                def split(s, b):
                    v.wait_ge(u_high, s + 1)
                    v.tensor_tensor(sp_x.ul[:, b % 2], sp_x.u[:, b % 2], sp_x.uh[:, b % 2].bitcast(F32), ALU.subtract
                                    ).then_inc(u_split, 1)

                def one_hot(t, at, b):
                    v.wait_ge(g_ready, banks * t + at + b + 1)
                    for n in range(4):
                        tok = bass.ds(4 * at + 4 * b + n, 1)
                        v.tensor_scalar(onej[:, b % 2, n], k.iota[:], cols[:, 1, tok], None, ALU.is_equal)
                        ins = v.tensor_scalar(onei[:, b % 2, n], k.iota[:], cols[:, 0, tok], cols[:, 2, tok],
                                              ALU.is_equal, ALU.mult)
                    ins.then_inc(one_ready, 1)

                split(0, 0)
                split(1, 1)
                with v.Fori(0, NT) as t:
                    chain = Chain(v, link)
                    base = 15 * t
                    ahead = PER_TILE * t + 2
                    tile = bass.ds(t, 1)
                    val = values[:, tile].rearrange("t o (h p) r -> t (o h) p r", p=2)
                    rank = ranks[:, tile].rearrange("t o (h p) r -> t (o h) p r", p=2)
                    v.tensor_tensor(cand[:, :, 0:CANDA * 16].rearrange("t h (x y) -> t h x y", y=16),
                                    bc(val[:, :, 0, 0:CANDA], 3, 16), bc(val[:, :, 1, :], 2, CANDA), ALU.add)
                    chain(v.tensor_tensor(cand[:, :, CANDA * 16:NCAND].rearrange("t h (x y) -> t h x y", y=4),
                                          bc(val[:, :, 0, CANDA:16], 3, 4), bc(val[:, :, 1, 0:4], 2, CANDB), ALU.add), base)
                    for h in range(PH):
                        ins = v.max(best[:, h, 0:8], cand[:, h])
                    chain(ins, base)
                    for h in range(PH):
                        v.max_index(pos[:, h, 0:8], best[:, h, 0:8], cand[:, h])
                        ins = v.match_replace(rest[:, h], best[:, h, 0:8], cand[:, h], NEG)
                    split(ahead, 0)
                    chain(ins, base)
                    for h in range(PH):
                        ins = v.max(best[:, h, 8:16], rest[:, h])
                    chain(ins, base)
                    for h in range(PH):
                        ins = v.max_index(pos[:, h, 8:16], best[:, h, 8:16], rest[:, h])
                    split(ahead + 1, 1)
                    chain(ins, base)
                    v.tensor_tensor(expd[:], best[:], bc(best[:, :, 0], 2, TOPK), ALU.subtract).then_inc(centred, 1)
                    v.tensor_single_scalar(shift[:, 0], pos[:], 4, ALU.logical_shift_right)
                    v.tensor_single_scalar(shift[:, 1], pos[:], 2, ALU.logical_shift_right)
                    v.tensor_single_scalar(is_b[:], pos[:], float(CANDA * 16), ALU.is_ge)
                    chain(v.tensor_single_scalar(part[:], pos[:], 3, ALU.bitwise_and), base)
                    v.tensor_tensor(ra[:], shift[:, 1], shift[:, 0], ALU.subtract)
                    chain(v.tensor_single_scalar(pos[:], pos[:], 15, ALU.bitwise_and), base)
                    v.tensor_scalar(ra[:], ra[:], -12.0, None, ALU.add)
                    chain(v.tensor_tensor(rb[:], part[:], pos[:], ALU.subtract), base)
                    split(ahead + 2, 2)
                    v.tensor_tensor(ra[:], ra[:], is_b[:], ALU.mult)
                    chain(v.tensor_tensor(rb[:], rb[:], is_b[:], ALU.mult), base)
                    v.tensor_tensor(ra[:], ra[:], shift[:, 0], ALU.add)
                    chain(v.tensor_tensor(rb[:], rb[:], pos[:], ALU.add), base)
                    for p, r in enumerate((ra, rb)):
                        ins = v.tensor_tensor(pick[:, p], bc(r[:].rearrange("t h r -> t (h r)"), 2, TOPK),
                                              bc(iota16, 1, PH * TOPK), ALU.is_equal)
                    chain(ins, base)
                    split(ahead + 3, 3)
                    for p in range(2):
                        ins = v.tensor_tensor(pick[:, p].rearrange("t (h r) x -> t h r x", h=PH),
                                              pick[:, p].rearrange("t (h r) x -> t h r x", h=PH),
                                              bc(rank[:, :, p, :], 2, TOPK), ALU.mult)
                    split(ahead + 4, 4)
                    chain(ins, base)
                    for p in range(2):
                        v.tensor_reduce(ijg[:, p], pick[:, p], AX.X, ALU.add)
                    v.wait_ge(exped, t + 1)
                    chain(v.tensor_reduce(total[:], expd[:], AX.X, ALU.add), base)
                    split(ahead + 5, 5)
                    chain(v.reciprocal(total[:], total[:]), base)
                    v.tensor_tensor(ijg[:, 2].rearrange("t (h r) -> t h r", h=PH), expd[:], bc(total[:], 2, TOPK),
                                    ALU.mult).then_inc(ijg_ready, 1)
                    v.wait_ge(turned, t + 1)
                    v.wait_ge(g_ready, banks * t + 2)
                    chain(v.tensor_copy(cols[:], turn), base)
                    assert chain.n == 15
                    split(ahead + 6, 6)
                    with v.Fori(0, rounds) as u:
                        for b in range(0, 4, 2):
                            one_hot(t, 4 * u, b)
                            one_hot(t, 4 * u, b + 1)
                            split(ahead + 2 * u + 7 + b // 2, 7 + b // 2)
                    one_hot(t, 4 * rounds, 0)
                    one_hot(t, 4 * rounds, 1)
                    split(ahead + PER_TILE - 1, PER_TILE - 1)
                for b in range(EXTRA):
                    split(PER_TILE * NT + 2 + b, b)

            @block.tensor
            def _(pe):
                def hidden(s, b):
                    pe.wait_ge(u_split, s + 1)
                    pe.wait_ge(gelu_ready, s + 1)
                    sp_x.product(pe, k, 4 + 2 * (b % 2), b % 2).then_inc(h_ready, 1)

                def gates(t, at, b):
                    n = banks * t + at + b
                    pe.wait_ge(one_ready, n + 1)
                    pe.wait_ge(g_free, n + 1)
                    for m in range(4):
                        mm = pe.matmul(k.ps[:, b % 2, m * NK:(m + 1) * NK], onej[:, b % 2, m], onei[:, b % 2, m],
                                       start=True, stop=True)
                    mm.then_inc(g_ready, 1)

                pe.sem_inc(g_ready, 2)
                with pe.Fori(0, NT) as t:
                    first = PER_TILE * t
                    for b in range(SELECT - 1):
                        hidden(first + b, b)
                    pe.wait_ge(ijg_ready, t + 1)
                    for c in range(3):
                        mm = pe.transpose(turn[:, c], ijg[:, c], k.ident[0:TT, 0:TT])
                    mm.then_inc(turned, 1)
                    hidden(first + SELECT - 1, SELECT - 1)
                    with pe.Fori(0, rounds) as u:
                        for b in range(0, 4, 2):
                            gates(t, 4 * u, b)
                            gates(t, 4 * u, b + 1)
                            hidden(first + SELECT + 2 * u + b // 2, SELECT + b // 2)
                    gates(t, 4 * rounds, 0)
                    gates(t, 4 * rounds, 1)
                for b in range(EXTRA):
                    hidden(PER_TILE * NT + b, b)

            @block.scalar
            def _(act):
                def split(s, b, first=False):
                    act.wait_ge(u_landed[b % 2], 8 * (s - b % 2) + 16)
                    if not first:
                        act.wait_ge(h_ready, s - 1)
                    act.activation(sp_x.uh[:, b % 2], sp_x.u[:, b % 2], ACT.Copy).then_inc(u_high, 1)

                def step(s, b):
                    split(s + 2, b)
                    act.wait_ge(h_ready, s + 1)
                    act.wait_ge(hid_stored[b % 2], 8 * (s - b % 2) + 16)
                    act.activation(halves(hid[:, b % 2]), k.ps[:, 4 + 2 * (b % 2):6 + 2 * (b % 2), 0:TH], ACT.Gelu
                                   ).then_inc(gelu_ready, 1)

                def copy_gates(t, at, b):
                    act.wait_ge(g_ready, banks * t + at + b + 3)
                    act.activation(g[:, :, bass.ds(4 * at + 4 * b, 4)],
                                   k.ps[:, b % 2].rearrange("j (t i) -> j i t", t=4), ACT.Copy).then_inc(g_free, 1)

                act.sem_inc(g_free, 2)
                act.sem_inc(gelu_ready, 2)
                act.sem_inc(hid_stored[0], 16)
                act.sem_inc(hid_stored[1], 16)
                split(0, 0, True)
                split(1, 1, True)
                with act.Fori(0, NT) as t:
                    first = PER_TILE * t
                    for b in range(SELECT - 1):
                        step(first + b, b)
                        if b == 3:
                            act.wait_ge(centred, t + 1)
                            act.activation(expd[:], expd[:], ACT.Exp).then_inc(exped, 1)
                    with act.Fori(0, rounds) as u:
                        for b in range(0, 4, 2):
                            step(first + SELECT - 1 + 2 * u + b // 2, SELECT - 1 + b // 2)
                            if b == 0:
                                act.wait_ge(g_stored, 16 * SELECT * t + 16)
                            copy_gates(t, 4 * u, b)
                            copy_gates(t, 4 * u, b + 1)
                    step(first + PER_TILE - 1, PER_TILE - 1)
                    copy_gates(t, 4 * rounds, 0)
                    copy_gates(t, 4 * rounds, 1)
                for b in range(EXTRA):
                    step(PER_TILE * NT + b, b)

            @block.sync
            def _(sp):
                def load_u(n, b):
                    sp.dma_start(sp_x.u[:, b % 2], a["peer_u"][bass.ds(layer * NK + n, 1)]
                                 .rearrange("o p k e -> (o p) k e")).then_inc(u_landed[b % 2], 16)

                def step(s, b):
                    wait(sp, u_split, s + 3)
                    load_u(s + 4, b)
                    wait(sp, gelu_ready, s + 3)
                    sp.dma_start(a["hidden"][bass.ds(s, 1)].rearrange("o p t -> (o p) t"), hid[:, b % 2]
                                 ).then_inc(hid_stored[b % 2], 16)

                def store_gates(t, c):
                    n = NG // SELECT
                    sp.dma_start(a["gates"][n * c:n * c + n, bass.ds(t, 1)].rearrange("g o j i t -> (o j) g (i t)"),
                                 g[:, n * GB * c:n * GB * (c + 1)].rearrange("j (g i) t -> j g (i t)", i=GB)
                                 ).then_inc(g_stored, 16)

                sp.sem_inc(g_stored, 16)
                for b in range(2):
                    sp.sem_inc(u_landed[b], 16)
                for b in range(2):
                    sp.wait_ge(u_split, b + 1)
                    load_u(b + 2, b)
                for b in range(SELECT):
                    step(b, b)
                with sp.Fori(0, NT - 1) as t:
                    with sp.Fori(0, rounds) as u:
                        for b in range(2):
                            step(PER_TILE * t + SELECT + 2 * u + b, b)
                    wait(sp, g_free, banks * t + banks + 2)
                    for b in range(SELECT):
                        store_gates(t, b)
                        step(PER_TILE * t + PER_TILE + b, b)
                with sp.Fori(0, rounds) as u:
                    for b in range(2):
                        step(PER_TILE * (NT - 1) + SELECT + 2 * u + b, b)
                sp.wait_ge(g_free, banks * NT + 2)
                for b in range(SELECT):
                    store_gates(NT - 1, b)
                    step(PER_TILE * NT + b, b)
                sp.wait_ge(g_stored, 16 * SELECT * NT + 16)
                for b in range(2):
                    sp.wait_ge(hid_stored[b], 8 * AHEAD + 16)
                    sp.wait_ge(u_landed[b], 8 * AHEAD + 32)


def peer_experts(nc, k, a, layer, sp_x, r):
    with Stage(nc, f"experts{layer}") as s:
        w = s.sb("v", [P, 2, D])
        wh = s.sb("vh", [P, GB, D], F32R)
        wl = s.sb("vl", [P, GB, D], F32R)
        g = s.sb("g", [P, 2, NT, GB, TT])
        act_out = s.sb("act", [P, 2, T])
        gated = s.sb("gated", [P, T])
        gh = s.sb("gh", [P, 2, GB, T], F32R)
        gl = s.sb("gl", [P, 2, GB, T], F32R)
        u, uh, ul = sp_x.u, sp_x.uh, sp_x.ul
        places = [[z[:].rearrange("p c t -> p (c t)")[:, 0:GB * D].rearrange("p (b d) -> p b d", b=GB)
                   for z in (sp_x.xh, sp_x.xl)], [wh[:], wl[:]]]
        u_landed = [s.sem(f"u_landed{b}") for b in range(2)]
        g_landed = [s.sem(f"g_landed{b}") for b in range(2)]
        v_landed = [s.sem(f"v_landed{b}") for b in range(2)]
        hid_landed = [s.sem(f"hid_landed{b}") for b in range(2)]
        started = s.sem("started")
        u_high = s.sem("u_high")
        u_split = s.sem("u_split")
        v_high = s.sem("v_high")
        v_split = s.sem("v_split")
        h_ready = s.sem("h_ready")
        gelu_ready = s.sem("gelu_ready")
        gated_ready = s.sem("gated_ready")
        a_high = s.sem("a_high")
        a_ready = s.sem("a_ready")
        y_ready = s.sem("y_ready")
        y_free = s.sem("y_free")
        with s.block() as block:
            @block.sync
            def _(sp):
                def load_u(n, b):
                    sp.dma_start(u[:, b % 2], a["peer_u"][bass.ds(layer * NK + AHEAD + n, 1)]
                                 .rearrange("o p k e -> (o p) k e")).then_inc(u_landed[b % 2], 16)

                def load_g(grp, par):
                    at = grp + AHEAD // GB if isinstance(grp, int) and grp < FRESH else grp - FRESH
                    sp.dma_start(g[:, par], a["gates"][bass.ds(at, 1)].rearrange("o n j i t -> (o j) n (i t)")
                                 ).then_inc(g_landed[par], 16)

                def load_v(n, b, at):
                    sp.dma_start(w[:, b % 2], a["peer_v"][bass.ds(layer * NK + at, 1)].rearrange("o e d -> (o e) d")
                                 ).then_inc(v_landed[b % 2], 16)

                def load_hid(at, b):
                    sp.dma_start(act_out[:, b % 2], a["hidden"][bass.ds(at, 1)].rearrange("o p t -> (o p) t")
                                 ).then_inc(hid_landed[b % 2], 16)

                def next_v(n, b):
                    wait(sp, v_split, n + 1)
                    load_v(n + 2, b, n + 2 - GB * FRESH if not isinstance(n, int) or n + 2 >= GB * FRESH else n + 2 + AHEAD)

                load_g(0, 0)
                for b in range(2):
                    load_v(b, b, AHEAD + b)
                load_g(1, 1)
                for grp in range(FRESH):
                    for b in range(GB):
                        n = GB * grp + b
                        if grp > 0:
                            next_v(n - GB, b)
                        if n + 4 < GB * FRESH:
                            sp.wait_ge(u_split, n + 3)
                            load_u(n + 4, b)
                    sp.wait_ge(gated_ready, GB * (grp + 1))
                    load_g(grp + 2, grp % 2)
                    if grp == FRESH - 1:
                        load_hid(0, 0)
                        load_hid(1, 1)
                for b in range(GB):
                    next_v(GB * (FRESH - 1) + b, b)

                def stored(grp, par, last=False):
                    for b in range(GB):
                        n = GB * grp + b
                        if not (last and b >= 2):
                            next_v(n, b)
                            wait(sp, gated_ready, n + 1)
                            load_hid(n + 2 - GB * FRESH, b)
                    if not last:
                        load_g(grp + 2, par)

                stored(FRESH, FRESH % 2)
                with sp.Fori(FRESH // 2, NG // 2 - 2) as i:
                    stored(2 * i + 2, 0)
                    stored(2 * i + 3, 1)
                for grp in (NG - 2, NG - 1):
                    for b in range(GB):
                        n = GB * grp + b
                        if n + 2 < NK:
                            next_v(n, b)
                            sp.wait_ge(gated_ready, n + 1)
                            load_hid(n + 2 - GB * FRESH, b)

            @block.tensor
            def _(pe):
                def hidden(grp):
                    for b in range(GB):
                        n = GB * grp + b
                        pe.wait_ge(u_split, n + 1)
                        pe.wait_ge(gelu_ready, n + 1)
                        sp_x.product(pe, k, 2 * (b % 2), b % 2).then_inc(h_ready, 1)

                def output(grp, par, place):
                    vh, vl = places[place]
                    pe.wait_ge(v_split, GB * grp + GB)
                    pe.wait_ge(a_ready, GB * grp + GB)
                    for c in range(KC):
                        pe.wait_ge(y_free, KC * grp + c + 1)
                        for h in range(2):
                            o = k.ps[:, 4 + 2 * (c % 2) + h, 0:TH]
                            t = slice(h * TH, (h + 1) * TH)
                            f = slice(c * P, (c + 1) * P)
                            for b in range(GB):
                                pe.matmul(o, vl[:, b, f], gh[:, par, b, t], start=(b == 0), stop=False)
                                pe.matmul(o, vh[:, b, f], gl[:, par, b, t], start=False, stop=False)
                                mm = pe.matmul(o, vh[:, b, f], gh[:, par, b, t], start=False, stop=(b == GB - 1))
                        mm.then_inc(y_ready, 1)

                hidden(0)
                with pe.Fori(0, FRESH // 2) as i:
                    hidden(2 * i + 1)
                    output(2 * i, 0, 1)
                    hidden(2 * i + 2)
                    output(2 * i + 1, 1, 1)
                output(FRESH - 1, 0, 0)
                output(FRESH, 1, 1)
                with pe.Fori(FRESH // 2, NG // 2 - 1) as i:
                    output(2 * i + 2, 0, 0)
                    output(2 * i + 3, 1, 1)

            @block.scalar
            def _(act):
                def split_u(n, b):
                    if not isinstance(n, int) or n >= GB:
                        act.wait_ge(u_landed[b % 2], 8 * (n - b % 2) - 16)
                    act.wait_ge(h_ready, n - 1)
                    act.activation(uh[:, b % 2], u[:, b % 2], ACT.Copy).then_inc(u_high, 1)

                def split_v(n, b, place):
                    act.wait_ge(v_landed[b % 2], 8 * (n - b % 2) + 16)
                    act.activation(places[place][0][:, b], w[:, b % 2], ACT.Copy).then_inc(v_high, 1)

                def gelu(n, b):
                    act.wait_ge(h_ready, n + 1)
                    if not isinstance(n, int) or n > 1:
                        act.wait_ge(gated_ready, n - 1)
                    act.activation(halves(act_out[:, b % 2]), k.ps[:, 2 * (b % 2):2 * (b % 2) + 2, 0:TH], ACT.Gelu
                                   ).then_inc(gelu_ready, 1)

                def group(grp):
                    for b in range(GB):
                        n = GB * grp + b
                        last = isinstance(grp, int) and grp == FRESH - 1 and b >= GB - 2
                        if b == 0 and not (isinstance(grp, int) and grp == 1):
                            act.wait_ge(y_ready, KC * (grp - 1))
                        split_v(n - GB, b, 1)
                        if not last:
                            split_u(n + 2, b)
                        gelu(n, b)

                def later(grp, place):
                    act.wait_ge(y_ready, KC * (grp - 1))
                    for b in range(GB):
                        split_v(GB * grp + b, b, place)

                act.sem_inc(gelu_ready, 2)
                act.sem_inc(u_high, 2)
                for b in range(GB):
                    split_u(b + 2, b)
                    gelu(b, b)
                group(1)
                with act.Fori(1, FRESH // 2) as i:
                    group(2 * i)
                    group(2 * i + 1)
                group(FRESH - 1)
                for b in range(GB):
                    split_v(GB * (FRESH - 1) + b, b, 0)
                later(FRESH, 1)
                with act.Fori(FRESH // 2, NG // 2 - 1) as i:
                    later(2 * i + 2, 0)
                    later(2 * i + 3, 1)

            @block.vector
            def _(v):
                def split_u(n, b):
                    v.wait_ge(u_high, n + 1)
                    v.tensor_tensor(ul[:, b % 2], u[:, b % 2], uh[:, b % 2].bitcast(F32), ALU.subtract
                                    ).then_inc(u_split, 1)

                def split_v(n, b, place):
                    v.wait_ge(v_high, n + 1)
                    vh, vl = places[place]
                    v.tensor_tensor(vl[:, b], w[:, b % 2], vh[:, b].bitcast(F32), ALU.subtract).then_inc(v_split, 1)

                def gate(n, b, par):
                    if not isinstance(n, int) or n > 0:
                        v.wait_ge(a_ready, n)
                    v.tensor_tensor(gated[:].rearrange("p (n t) -> p n t", n=NT),
                                    act_out[:, b % 2].rearrange("p (n t) -> p n t", n=NT), g[:, par, :, b], ALU.mult
                                    ).then_inc(gated_ready, 1)
                    v.wait_ge(gated_ready, n + 1)
                    v.tensor_copy(gh[:, par, b], gated[:]).then_inc(a_high, 1)
                    v.wait_ge(a_high, n + 1)
                    v.tensor_tensor(gl[:, par, b], gated[:], gh[:, par, b].bitcast(F32), ALU.subtract
                                    ).then_inc(a_ready, 1)

                def collect(grp, chunks):
                    for c in chunks:
                        v.wait_ge(y_ready, KC * grp + c + 1)
                        rc = halves(r[:, c])
                        v.tensor_tensor(rc, rc, k.ps[:, 4 + 2 * (c % 2):6 + 2 * (c % 2), 0:TH], ALU.add
                                        ).then_inc(y_free, 1)

                def group(grp, par):
                    v.wait_ge(g_landed[par], 8 * (grp - par) + 16)
                    for b in range(GB):
                        n = GB * grp + b
                        last = isinstance(grp, int) and grp == FRESH - 1 and b >= GB - 2
                        if not isinstance(grp, int) or grp > 0:
                            split_v(n - GB, b, 1)
                        if not last:
                            split_u(n + 2, b)
                        v.wait_ge(gelu_ready, n + 3)
                        gate(n, b, par)

                def later(grp, par, place):
                    v.wait_ge(g_landed[par], 8 * (grp - par) + 16)
                    for b in range(GB):
                        n = GB * grp + b
                        split_v(n, b, place)
                        v.wait_ge(hid_landed[b % 2], 8 * (n - GB * FRESH - b % 2) + 16)
                        gate(n, b, par)
                        collect(grp - 1, (2 * b, 2 * b + 1))

                v.sem_inc(y_free, 2)
                v.sem_inc(u_split, 2)
                v.tensor_scalar(r[:], k.x[:], ALPHA, None, ALU.mult).then_inc(started, 1)
                v.wait_ge(started, 1)
                group(0, 0)
                group(1, 1)
                collect(0, range(KC))
                with v.Fori(1, FRESH // 2) as i:
                    group(2 * i, 0)
                    collect(2 * i - 1, range(KC))
                    group(2 * i + 1, 1)
                    collect(2 * i, range(KC))
                group(FRESH - 1, 0)
                for b in range(GB):
                    split_v(GB * (FRESH - 1) + b, b, 0)
                    collect(FRESH - 2, (2 * b, 2 * b + 1))
                later(FRESH, 1, 1)
                with v.Fori(FRESH // 2, NG // 2 - 1) as i:
                    later(2 * i + 2, 0, 0)
                    later(2 * i + 3, 1, 1)
                collect(NG - 1, range(KC))


def peer_layer(nc, k, a, layer):
    with Stage(nc, f"peer{layer}") as s:
        sp_x = Split(s)
        with Stage(nc, f"ranks{layer}") as t:
            values = t.sb("values", [TT, NT, HP, TOPK])
            ranks = t.sb("ranks", [TT, NT, HP, TOPK])
            peer_retrieve(nc, k, a, layer, sp_x, values, ranks)
            peer_gates(nc, k, a, layer, sp_x, values, ranks)
        with Stage(nc, f"peer_out{layer}") as t:
            r = t.sb("r", [P, KC, T])
            peer_experts(nc, k, a, layer, sp_x, r)
            layer_norm(nc, k, f"ln{layer}1", r, f"ln_g{layer}1", f"ln_b{layer}1", k.x, ACT.Identity,
                       slabs(k, a["w_pw1"]) if layer == 0 else ())


def conv_module(nc, k, a, h, r):
    LEFT = CW - 1
    ON_PE = 4
    with Stage(nc, "conv") as s:
        y = s.sb("y", [P, KC, T])
        with Stage(nc, "convin") as t:
            linear(nc, k, "pw1", a["w_pw1"], k.x, h, 2 * KC, KC)
            ext = t.sb("ext", [P, KC, LEFT + TP])
            exts = t.sb("exts", [P, KC, TS, CW])
            old = t.sb("old", [P, KC, TS, LEFT])
            tails = t.sb("tails", [P, KC, TS, LEFT])
            prod = t.sb("prod", [P, KC, TS, CW])
            diag = t.sb("diag", [P, 2, ON_PE, P])
            landed = t.sem("landed")
            sig = t.sem("sig")
            glu = t.sem("glu")
            done = t.sem("done")
            tails_ready = t.sem("tails_ready")
            link = t.sem("link")
            stored = t.sem("stored")
            diag_ready = t.sem("diag_ready")
            diag_used = t.sem("diag_used")
            with t.block() as block:
                @block.sync
                def _(sp):
                    sp.dma_start(old[:], a["state_conv"]).then_inc(landed, 16)
                    sp.wait_ge(tails_ready, 1)
                    sp.dma_start(a["new_conv_s"], tails[:]).then_inc(stored, 16)
                    sp.dma_start(a["new_conv_p"], ext[:, :, TP:TP + LEFT]).then_inc(stored, 16)
                    sp.wait_ge(stored, 32)

                @block.tensor
                def _(pe):
                    def tap(j, b, last=False):
                        for c in range(ON_PE):
                            pe.wait_ge(diag_ready, ON_PE * j + c + 1)
                            first = isinstance(j, int) and j == 0
                            if first:
                                pe.wait_ge(glu, c + 1)
                            pe.matmul(k.ps[:, c, :], diag[:, b, c], ext[:, c, bass.ds(j, TP)], start=first, stop=last
                                      ).then_inc(diag_used, 1)

                    tap(0, 0)
                    with pe.Fori(0, CW // 2 - 1) as i:
                        tap(2 * i + 1, 1)
                        tap(2 * i + 2, 0)
                    tap(CW - 2, 1)
                    tap(CW - 1, 0, True)

                @block.scalar
                def _(act):
                    def diagonals(j, b):
                        for c in range(ON_PE):
                            if not isinstance(j, int) or j > 1:
                                act.wait_ge(diag_used, ON_PE * (j - 2) + c + 1)
                            act.activation(diag[:, b, c], k.ident[:], ACT.Copy,
                                           scale=k.vec[:, bass.ds(j + (VEC["w_dw"] + c * CW), 1)]).then_inc(diag_ready, 1)

                    for c in range(KC):
                        act.activation(h[:, KC + c], h[:, KC + c], ACT.Sigmoid, bias=k.col("b_pw1", KC + c)).then_inc(sig, 1)
                        if c == ON_PE - 1:
                            diagonals(0, 0)
                            diagonals(1, 1)
                    with act.Fori(1, CW // 2) as i:
                        diagonals(2 * i, 0)
                        diagonals(2 * i + 1, 1)
                    diagonals(CW - 1, 0)
                    act.wait_ge(diag_used, ON_PE * CW)
                    for c in range(ON_PE):
                        act.activation(y[:, c, 0:TP], k.ps[:, c, :], ACT.Identity, bias=k.col("b_dw", c))

                @block.vector
                def _(v):
                    chain = Chain(v, link)
                    mine = range(ON_PE, KC)
                    v.memset(ext[:, :, 0:LEFT], 0.0)
                    for c in range(KC):
                        v.wait_ge(sig, c + 1)
                        b = k.col("b_pw1", c)
                        v.scalar_tensor_tensor(exts[:, c, :, LEFT], h[:, c, TP:T], b, h[:, KC + c, TP:T], ALU.add, ALU.mult)
                        v.scalar_tensor_tensor(ext[:, c, LEFT:LEFT + TP], h[:, c, 0:TP], b, h[:, KC + c, 0:TP], ALU.add, ALU.mult
                                               ).then_inc(glu, 1)
                    v.wait_ge(landed, 16)
                    chain(v.tensor_copy(exts[:, :, :, 0:LEFT], old[:]))
                    v.wait_ge(glu, KC)
                    v.tensor_copy(tails[:], exts[:, :, :, 1:CW]).then_inc(tails_ready, 1)
                    for c in range(KC):
                        w = k.vec[:, VEC["w_dw"] + c * CW:VEC["w_dw"] + (c + 1) * CW]
                        ins = v.tensor_tensor(prod[:, c], exts[:, c], bc(w, 1, TS), ALU.mult)
                    chain(ins)
                    chain(v.tensor_reduce(y[:, :, TP:T], prod[:], AX.X, ALU.add))
                    v.tensor_tensor(y[:, :, TP:T], y[:, :, TP:T], bc(k.vec[:, VEC["b_dw"]:VEC["b_dw"] + KC], 2, TS), ALU.add)
                    for c in mine:
                        v.tensor_scalar(y[:, c, 0:TP], ext[:, c, 0:TP], k.col("w_dw", c * CW), k.col("b_dw", c), ALU.mult, ALU.add
                                        ).then_inc(done, 1)
                    with v.Fori(1, CW) as j:
                        for c in mine:
                            o = y[:, c, 0:TP]
                            v.wait_ge(done, (KC - ON_PE) * (j - 1) + c - ON_PE + 1)
                            v.scalar_tensor_tensor(o, ext[:, c, bass.ds(j, TP)],
                                                   k.vec[:, bass.ds(j + (VEC["w_dw"] + c * CW), 1)], o, ALU.mult, ALU.add
                                                   ).then_inc(done, 1)
        act_in = s.sb("act", [P, KC, T])
        layer_norm(nc, k, "cln", y, "cln_g", "cln_b", act_in, ACT.Silu, slabs(k, a["w_pw2"]))
        linear(nc, k, "pw2", a["w_pw2"], act_in, r, KC, KC, residual=True, bias="b_pw2")


def build(nc, a):
    with ExitStack() as ctx:
        k = Kept(nc, ctx)
        load_constants(nc, a, k)
        for layer, mix in enumerate((mixer, conv_module)):
            with Stage(nc, f"layer{layer}") as s:
                wide = s.sb("wide", [P, MIX, T])
                r = wide[:, 0:KC]
                mix(nc, k, a, wide, r)
                layer_norm(nc, k, f"ln{layer}0", r, f"ln_g{layer}0", f"ln_b{layer}0", k.x, ACT.Identity,
                           slabs(k, a["peer_wq"][layer]))
            peer_layer(nc, k, a, layer)
        with Stage(nc, "store") as s:
            stored = s.sem("stored")
            with s.block() as block:
                @block.sync
                def _(sp):
                    sp.dma_start(a["y"], k.x[:]).then_inc(stored, 16)
                    sp.wait_ge(stored, 16)


_OUTS = {"y": (P, KC, T), "new_lat": (P, CC, T), "new_kpe": (ROPE, T), "new_hgrn_p": (P, H, P),
         "new_hgrn_s": (TS, P, H, P), "new_conv_p": (P, KC, CW - 1), "new_conv_s": (P, KC, TS, CW - 1)}
_SCRATCH = {"gates": (NG, NT, NK, GB, TT), "hidden": (AHEAD, P, T)}


def _slabs(w):
    i, o = w.shape
    return w.reshape(i // P, P, o // P, P).transpose(2, 1, 0, 3)


def _rows(w):
    return w.reshape(w.shape[0] // P, P, -1).transpose(1, 0, 2)


def _layout(i):
    swap = np.r_[ROPE // 2:ROPE, 0:ROPE // 2]
    x = np.concatenate([i["x_prompt"].reshape(TP, D), i["x_sample"].reshape(TS, D)])
    w_in = i["mix_w_in"][0]
    kr = w_in[:, 2048 + QL + KVL:]
    w_mix = np.concatenate([w_in[:, 0:1024], w_in[:, 1536:2048], w_in[:, 2048:2048 + QL + KVL], kr, kr[:, swap],
                            w_in[:, 1024:1536]], axis=1)
    uq = i["mla_w_uq"][0].reshape(QL, H, P + ROPE)
    w_uq = np.concatenate([uq[:, :, :P].reshape(QL, -1), uq[:, :, P:].reshape(QL, -1), uq[:, :, P:][:, :, swap].reshape(QL, -1)], axis=1)
    ukv = i["mla_w_ukv"][0]
    half = ROPE // 2
    inv = np.float32(10000.0) ** (-np.arange(half, dtype=np.float32) / np.float32(half))
    pos = np.r_[0:TP, [PAST] * TS].astype(np.float32)
    ang = (pos[:, None] * inv[None, :]).astype(np.float32).astype(np.float64)
    cos, sin = np.cos(ang).T.astype(np.float32), np.sin(ang).T.astype(np.float32)
    s_, t_ = np.arange(P)[:, None], np.arange(P)[None, :]
    masks = [s_ == t_] + [(s_ // (2 * m) == t_ // (2 * m)) & (s_ % (2 * m) < m) & (t_ % (2 * m) >= m)
                          for m in (1 << n for n in range(LEVELS - 1))]

    lat_t = i["cache_mla_latent"][0].reshape(POOL_PAGES, PAGE, CC, P).transpose(0, 3, 2, 1).reshape(POOL_PAGES, P, KVL)
    rope_t = np.pad(i["cache_mla_krope"][0].transpose(0, 2, 1), ((0, 0), (0, P - ROPE), (0, 0)))

    def cols(w):
        return w.reshape(-1, P).T

    vec = [cols(i["ln_g"][l, j]) for l in range(2) for j in range(2)] + [cols(i["ln_b"][l, j]) for l in range(2) for j in range(2)]
    vec += [cols(i["conv_b_pw1"][0]), cols(i["conv_b_dw"][0]), cols(i["conv_ln_g"][0]), cols(i["conv_ln_b"][0]),
            cols(i["conv_b_pw2"][0]), cols(i["mla_q_norm"][0]), cols(i["mla_kv_norm"][0]), cols(i["hg_out_norm"][0]),
            cols(i["hg_lb_logits"]), i["conv_w_dw"][0].reshape(CW, KC, P).transpose(2, 1, 0).reshape(P, -1)]
    return {
        "x_t": _rows(x.T),
        "vecs": np.concatenate(vec, axis=1),
        "masks": np.stack(masks, axis=1).astype(np.uint32),
        "cos": np.concatenate([cos, cos]),
        "sin": np.concatenate([-sin, sin]),
        "w_mix": _slabs(w_mix),
        "w_uq": _rows(w_uq),
        "w_uk": ukv[:, :, :P].transpose(2, 1, 0),
        "w_uv": ukv[:, :, P:].reshape(CC, P, H, P).transpose(1, 2, 0, 3),
        "w_mix_out": _slabs(i["mix_w_out"][0]),
        "page_table": i["page_table"].reshape(1, -1),
        "cache": np.concatenate([lat_t, rope_t, i["cache_mla_latent"][0]], axis=2),
        "state_hgrn": i["state_hgrn"][0].transpose(0, 2, 1, 3),
        "state_conv": i["state_conv"][0].reshape(TS, CW - 1, KC, P).transpose(3, 2, 0, 1),
        "w_pw1": _slabs(i["conv_w_pw1"][0]),
        "w_pw2": _slabs(i["conv_w_pw2"][0]),
        "peer_wq": np.stack([_slabs(w) for w in i["peer_w_q"]]),
        "peer_keys": i["peer_sub_keys"].transpose(0, 4, 2, 1, 3).reshape(2, P, HP, NK),
        "peer_u": i["peer_u"].reshape(2 * NK, P, KC, P).transpose(0, 3, 2, 1),
        "peer_v": i["peer_v"].reshape(2 * NK, P, D),
    }


def kernel(**inputs):
    import concourse.bacc as bacc
    from concourse.bass_utils import run_bass_kernel_spmd

    nc = bacc.Bacc("TRN2", target_bir_lowering=False, num_devices=1)
    arrays = {n: np.ascontiguousarray(z) for n, z in _layout({n: np.asarray(z) for n, z in inputs.items()}).items()}
    a = {n: nc.dram_tensor(n, z.shape, mybir.dt.from_np(z.dtype), kind="ExternalInput").ap() for n, z in arrays.items()}
    for n, shape in _OUTS.items():
        a[n] = nc.dram_tensor(n, shape, F32, kind="ExternalOutput").ap()
    for n, shape in _SCRATCH.items():
        a[n] = nc.dram_tensor(n, shape, F32).ap()
    build(nc, a)
    o = run_bass_kernel_spmd(nc, [arrays], core_ids=[0]).results[0]
    tok = [o[n].transpose(2, 1, 0).reshape(T, -1) for n in ("y", "new_lat")] + [o["new_kpe"].T]
    prompt = [z[:TP] for z in tok]
    sample = [z[TP:].reshape(TS, 1, -1) for z in tok]
    out = (prompt[0][None], sample[0], prompt[1][None, None], prompt[2][None, None],
           o["new_hgrn_p"].transpose(1, 0, 2)[None, None],
           o["new_conv_p"].transpose(2, 1, 0).reshape(1, 1, CW - 1, D),
           sample[1][None], sample[2][None], o["new_hgrn_s"].transpose(0, 2, 1, 3)[None],
           o["new_conv_s"].transpose(2, 3, 1, 0).reshape(1, TS, CW - 1, D))
    return tuple(np.ascontiguousarray(z) for z in out)
```
